# Optimizing a Trainium2 kernel written in Bass

```python
import math
import jax, jax.numpy as jnp
from jax import lax
import numpy as np

D_MODEL = 1024
BATCH = 1
SEQ = 256
DEPTH = 2

GRID_W = 64
CTX_LEN = 256
WIN_H = 8
WIN_W = 16
HD_A = 64
H_A = D_MODEL // 2 // HD_A
H_B = 4
DV_B = D_MODEL // 2 // H_B
DK_B = DV_B // 2
MLSTM_CHUNK = 64
HD_C = 128
H_C = D_MODEL // HD_C
KV_C = max(H_C // 4, 1)
Q_BLOCK = 128
ROPE_THETA = 10000.0
N_EXPERTS = 16
N_GROUPS = 4
EXP_PER_GROUP = N_EXPERTS // N_GROUPS
TOP_K = 2
D_FF_EXPERT = D_MODEL // 2
N_EVEN = (DEPTH + 1) // 2
N_ODD = DEPTH // 2
D_MIX = H_A * HD_A + H_B * DV_B
SIZES_EVEN = (H_A * HD_A, H_A * HD_A, H_A * HD_A,
              H_B * DK_B, H_B * DK_B, H_B * DV_B, H_B * DV_B, 4 * H_B)
D_IN_EVEN = sum(SIZES_EVEN)
SIZES_ODD = (H_C * HD_C, KV_C * HD_C, KV_C * HD_C)
D_IN_ODD = sum(SIZES_ODD)
EPS = 1e-6
NEG_BIG = -1e30


def rms_norm(x, g):
    xf = x.astype(jnp.float32)
    y = xf * lax.rsqrt(jnp.mean(xf * xf, axis=-1, keepdims=True) + EPS)
    return (y * g.astype(jnp.float32)).astype(x.dtype)

def modulate(x, g, shift, scale):
    return rms_norm(x, g) * (1 + scale) + shift

def split_cols(p, sizes):
    points = [int(s) for s in np.cumsum(sizes)[:-1]]
    return jnp.split(p, points, axis=-1)

def rope_2d_tables(n_tokens, head_dim):
    n_freq = head_dim // 4
    inv_freq = ROPE_THETA ** (-jnp.arange(n_freq, dtype=jnp.float32) / n_freq)
    t = jnp.arange(n_tokens)
    rows = (t // GRID_W).astype(jnp.float32)
    cols = (t % GRID_W).astype(jnp.float32)
    ang = jnp.concatenate([rows[:, None] * inv_freq, cols[:, None] * inv_freq], axis=-1)
    return jnp.cos(ang), jnp.sin(ang)

def apply_rope(x, cos, sin):
    xr = x.astype(jnp.float32).reshape(*x.shape[:-1], -1, 2)
    x0, x1 = xr[..., 0], xr[..., 1]
    c = cos[:, None, :]
    s = sin[:, None, :]
    out = jnp.stack([x0 * c - x1 * s, x0 * s + x1 * c], axis=-1).reshape(x.shape)
    return out.astype(x.dtype)

def block_attention(q, k, v):
    B, S, H, d = q.shape
    kv = k.shape[2]
    G = H // kv
    qb = q.reshape(B, S // Q_BLOCK, Q_BLOCK, kv, G, d).transpose(1, 0, 2, 3, 4, 5)

    def one_block(qi):
        s = jnp.einsum('bqkgd,btkd->bkgqt', qi, k).astype(jnp.float32)
        p = jax.nn.softmax(s, axis=-1).astype(v.dtype)
        return jnp.einsum('bkgqt,btkd->bqkgd', p, v)

    o = lax.map(one_block, qb)
    return o.transpose(1, 0, 2, 3, 4, 5).reshape(B, S, H * d)

def neighbourhood_attention(q, k, v, kc, vc, rpb):
    B, S, H, d = q.shape
    rows = S // GRID_W
    kh = min(WIN_H, rows)
    n_loc = kh * WIN_W
    qg = q.reshape(B, rows, GRID_W, H, d)
    kg = k.reshape(B, rows, GRID_W, H, d)
    vg = v.reshape(B, rows, GRID_W, H, d)
    qcol = np.arange(GRID_W)
    col_start = np.clip(qcol - WIN_W // 2, 0, GRID_W - WIN_W)
    col_idx = col_start[:, None] + np.arange(WIN_W)[None, :]
    dcol = col_idx - qcol[:, None] + (WIN_W - 1)

    def row_block(r):
        r0 = jnp.clip(r - kh // 2, 0, rows - kh)
        q_r = lax.dynamic_index_in_dim(qg, r, axis=1, keepdims=False)
        k_r = lax.dynamic_slice_in_dim(kg, r0, kh, axis=1)
        v_r = lax.dynamic_slice_in_dim(vg, r0, kh, axis=1)
        k_win = k_r[:, :, col_idx]
        v_win = v_r[:, :, col_idx]
        s_loc = jnp.einsum('bqhd,biqjhd->bhqij', q_r, k_win)
        drow = r0 + jnp.arange(kh) - r + (WIN_H - 1)
        bias = rpb[:, drow][:, :, dcol].transpose(0, 2, 1, 3)
        s_loc = s_loc + bias[None].astype(s_loc.dtype)
        s_ctx = jnp.einsum('bqhd,blhd->bhql', q_r, kc)
        s = jnp.concatenate([s_loc.reshape(B, H, GRID_W, n_loc), s_ctx], axis=-1)
        p = jax.nn.softmax(s.astype(jnp.float32), axis=-1).astype(v.dtype)
        p_loc = p[..., :n_loc].reshape(B, H, GRID_W, kh, WIN_W)
        o = jnp.einsum('bhqij,biqjhd->bqhd', p_loc, v_win) + jnp.einsum('bhql,blhd->bqhd', p[..., n_loc:], vc)
        return o

    o = lax.map(row_block, jnp.arange(rows))
    return o.transpose(1, 0, 2, 3, 4).reshape(B, S, H * d)

def mlstm_chunkwise(q, k, v, ig, lf):
    B, H, T, dk = q.shape
    dv = v.shape[-1]
    n_ch = T // MLSTM_CHUNK

    def to_chunks(a):
        return jnp.moveaxis(a.reshape(B, H, n_ch, MLSTM_CHUNK, *a.shape[3:]), 2, 0)

    causal = jnp.tril(jnp.ones((MLSTM_CHUNK, MLSTM_CHUNK), dtype=bool))

    def step(carry, inp):
        C, n, m = carry
        qj, kj, vj, ij, fj = inp
        b = jnp.cumsum(fj, axis=-1)
        a = b + m[..., None]
        Dm = jnp.where(causal, b[..., :, None] - b[..., None, :] + ij[..., None, :], NEG_BIG)
        m_row = jnp.maximum(a, Dm.max(axis=-1))
        w_intra = jnp.exp(Dm - m_row[..., None])
        w_inter = jnp.exp(a - m_row)
        qk = jnp.einsum('bhid,bhjd->bhij', qj, kj) * w_intra
        num = w_inter[..., None] * jnp.einsum('bhvd,bhid->bhiv', C, qj) + jnp.einsum('bhij,bhjv->bhiv', qk, vj)
        den = w_inter * jnp.einsum('bhd,bhid->bhi', n, qj) + qk.sum(axis=-1)
        h = num / jnp.maximum(jnp.abs(den), jnp.exp(-m_row))[..., None]
        bL = b[..., -1]
        g = bL[..., None] - b + ij
        m_new = jnp.maximum(bL + m, g.max(axis=-1))
        w_old = jnp.exp(bL + m - m_new)
        w_tok = jnp.exp(g - m_new[..., None])
        C_new = w_old[..., None, None] * C + jnp.einsum('bhj,bhjv,bhjd->bhvd', w_tok, vj, kj)
        n_new = w_old[..., None] * n + jnp.einsum('bhj,bhjd->bhd', w_tok, kj)
        return (C_new, n_new, m_new), h

    init = (jnp.zeros((B, H, dv, dk), jnp.float32), jnp.zeros((B, H, dk), jnp.float32),
            jnp.full((B, H), NEG_BIG, jnp.float32))
    _, hs = lax.scan(step, init, (to_chunks(q), to_chunks(k), to_chunks(v), to_chunks(ig), to_chunks(lf)))
    return jnp.moveaxis(hs, 0, 2).reshape(B, H, T, dv)

def even_mixer(h_lat, h_ctx, w_in, w_out, na_qg, na_kg, rpb, gate_b, ml_norm_g, need_ctx_out):
    B, S, _ = h_lat.shape
    L = h_ctx.shape[1]
    aq, ak, av, mq, mk, mv, mo, mg = split_cols(h_lat @ w_in, SIZES_EVEN)
    caq, cak, cav, cmq, cmk, cmv, cmo, cmg = split_cols(h_ctx @ w_in, SIZES_EVEN)

    def heads_a(t):
        return t.reshape(B, -1, H_A, HD_A)
    q_a = rms_norm(heads_a(aq), na_qg) * HD_A ** -0.5
    k_a = rms_norm(heads_a(ak), na_kg)
    ck_a = rms_norm(heads_a(cak), na_kg)
    cv_a = heads_a(cav)
    o_a = neighbourhood_attention(q_a, k_a, heads_a(av), ck_a, cv_a, rpb)

    def heads_b(t, dh):
        return jnp.moveaxis(t.reshape(B, -1, H_B, dh), 2, 1).astype(jnp.float32)
    q_m = jnp.concatenate([heads_b(cmq, DK_B), heads_b(mq, DK_B)], axis=2) * DK_B ** -0.5
    k_m = jnp.concatenate([heads_b(cmk, DK_B), heads_b(mk, DK_B)], axis=2)
    v_m = jnp.concatenate([heads_b(cmv, DV_B), heads_b(mv, DV_B)], axis=2)
    gates = jnp.concatenate([cmg, mg], axis=1).astype(jnp.float32) + gate_b.astype(jnp.float32)
    i_f, f_f, i_b, f_b = gates.reshape(B, L + S, 4, H_B).transpose(2, 0, 3, 1)

    def flip(t):
        return jnp.concatenate([t[:, :, :L][:, :, ::-1], t[:, :, L:][:, :, ::-1]], axis=2)

    h_f = mlstm_chunkwise(q_m, k_m, v_m, i_f, jax.nn.log_sigmoid(f_f))
    h_bw = flip(mlstm_chunkwise(flip(q_m), flip(k_m), flip(v_m), flip(i_b), flip(jax.nn.log_sigmoid(f_b))))
    h_m = jnp.moveaxis(h_f + h_bw, 1, 2)
    h_m = rms_norm(h_m, ml_norm_g.reshape(H_B, DV_B)).reshape(B, L + S, H_B * DV_B).astype(h_lat.dtype)
    h_m = h_m * jax.nn.sigmoid(jnp.concatenate([cmo, mo], axis=1))

    out_lat = jnp.concatenate([o_a, h_m[:, L:]], axis=-1) @ w_out
    if not need_ctx_out:
        return out_lat, None
    cq_a = rms_norm(heads_a(caq), na_qg) * HD_A ** -0.5
    co_a = block_attention(cq_a, ck_a, cv_a)
    out_ctx = jnp.concatenate([co_a, h_m[:, :L]], axis=-1) @ w_out
    return out_lat, out_ctx

def odd_mixer(h_lat, h_ctx, w_in, w_out, qg, kg, cos, sin, need_ctx_out):
    B, S, _ = h_lat.shape
    L = h_ctx.shape[1]
    q, k, v = split_cols(h_lat @ w_in, SIZES_ODD)
    q = apply_rope(rms_norm(q.reshape(B, S, H_C, HD_C), qg), cos, sin) * HD_C ** -0.5
    k = apply_rope(rms_norm(k.reshape(B, S, KV_C, HD_C), kg), cos, sin)
    v = v.reshape(B, S, KV_C, HD_C)
    if need_ctx_out:
        cq, ck, cv = split_cols(h_ctx @ w_in, SIZES_ODD)
    else:
        ck, cv = split_cols(h_ctx @ w_in[:, H_C * HD_C:], SIZES_ODD[1:])
    ck = rms_norm(ck.reshape(B, L, KV_C, HD_C), kg)
    cv = cv.reshape(B, L, KV_C, HD_C)
    k_all = jnp.concatenate([ck, k], axis=1)
    v_all = jnp.concatenate([cv, v], axis=1)
    out_lat = block_attention(q, k_all, v_all) @ w_out
    if not need_ctx_out:
        return out_lat, None
    cq = rms_norm(cq.reshape(B, L, H_C, HD_C), qg) * HD_C ** -0.5
    out_ctx = block_attention(cq, ck, cv) @ w_out
    return out_lat, out_ctx

def moe(h, router_w, router_b, w1, w3, w2):
    N = h.shape[0]
    scores = jax.nn.sigmoid((h @ router_w).astype(jnp.float32))
    sel = (scores + router_b.astype(jnp.float32)).reshape(N, N_GROUPS, EXP_PER_GROUP)
    group_score = lax.top_k(sel, TOP_K)[0].sum(axis=-1)
    g_idx = jnp.argmax(group_score, axis=-1)
    sel_in = jnp.take_along_axis(sel, g_idx[:, None, None], axis=1)[:, 0]
    _, local = lax.top_k(sel_in, TOP_K)
    e_idx = g_idx[:, None] * EXP_PER_GROUP + local
    w = jnp.take_along_axis(scores, e_idx, axis=-1)
    w = w / w.sum(axis=-1, keepdims=True)
    comb = (jax.nn.one_hot(e_idx, N_EXPERTS, dtype=jnp.float32) * w[..., None]).sum(axis=1).astype(h.dtype)
    y = jnp.zeros_like(h)
    for e in range(N_EXPERTS):
        y = y + comb[:, e:e + 1] * ((jax.nn.silu(h @ w1[e]) * (h @ w3[e])) @ w2[e])
    return y

def first_inputs(seed: int = 0) -> dict:
    key = jax.random.key(seed)
    ks = jax.random.split(key, 32)
    D = D_MODEL

    def nrm(k, shape, scale):
        return jax.random.normal(k, shape, jnp.float32) * scale

    i_b = nrm(ks[13], (N_EVEN, 2, H_B), 0.1)
    f_b = 3.0 + 3.0 * jax.random.uniform(ks[14], (N_EVEN, 2, H_B), jnp.float32)
    mlstm_gate_b = jnp.stack([i_b[:, 0], f_b[:, 0], i_b[:, 1], f_b[:, 1]], axis=1).reshape(N_EVEN, 4 * H_B)
    return {
        "x": nrm(ks[0], (BATCH, SEQ, D), 1.0),
        "c": nrm(ks[1], (BATCH, D), 1.0),
        "ctx": nrm(ks[2], (BATCH, CTX_LEN, D), 1.0),
        "c_ctx": nrm(ks[3], (D,), 1.0),
        "ada_w": nrm(ks[4], (DEPTH, D, 6 * D), 0.5 * D ** -0.5),
        "ada_b": nrm(ks[5], (DEPTH, 6 * D), 0.02),
        "norm_mix_g": 1.0 + nrm(ks[6], (DEPTH, D), 0.05),
        "norm_ffn_g": 1.0 + nrm(ks[7], (DEPTH, D), 0.05),
        "even_w_in": nrm(ks[8], (N_EVEN, D, D_IN_EVEN), D ** -0.5),
        "even_w_out": nrm(ks[9], (N_EVEN, D_MIX, D), D_MIX ** -0.5),
        "na_q_norm_g": 1.0 + nrm(ks[10], (N_EVEN, HD_A), 0.05),
        "na_k_norm_g": 1.0 + nrm(ks[11], (N_EVEN, HD_A), 0.05),
        "na_rpb": nrm(ks[12], (N_EVEN, H_A, 2 * WIN_H - 1, 2 * WIN_W - 1), 0.02),
        "mlstm_gate_b": mlstm_gate_b,
        "mlstm_norm_g": 1.0 + nrm(ks[15], (N_EVEN, H_B * DV_B), 0.05),
        "odd_w_in": nrm(ks[16], (N_ODD, D, D_IN_ODD), D ** -0.5),
        "odd_w_out": nrm(ks[17], (N_ODD, H_C * HD_C, D), (H_C * HD_C) ** -0.5),
        "gqa_q_norm_g": 1.0 + nrm(ks[18], (N_ODD, HD_C), 0.05),
        "gqa_k_norm_g": 1.0 + nrm(ks[19], (N_ODD, HD_C), 0.05),
        "router_w": nrm(ks[20], (D, N_EXPERTS), D ** -0.5),
        "router_b": nrm(ks[21], (N_EXPERTS,), 0.01),
        "exp_w1": nrm(ks[22], (DEPTH, N_EXPERTS, D, D_FF_EXPERT), D ** -0.5),
        "exp_w3": nrm(ks[23], (DEPTH, N_EXPERTS, D, D_FF_EXPERT), D ** -0.5),
        "exp_w2": nrm(ks[24], (DEPTH, N_EXPERTS, D_FF_EXPERT, D), D_FF_EXPERT ** -0.5),
    }

def first_block(x, c, ctx, c_ctx, ada_w, ada_b, norm_mix_g, norm_ffn_g, even_w_in, even_w_out,
              na_q_norm_g, na_k_norm_g, na_rpb, mlstm_gate_b, mlstm_norm_g, odd_w_in, odd_w_out,
              gqa_q_norm_g, gqa_k_norm_g, router_w, router_b, exp_w1, exp_w3, exp_w2):
    B, S, D = x.shape
    L = ctx.shape[1]
    cos, sin = rope_2d_tables(S, HD_C)
    silu_c = jax.nn.silu(c)
    silu_cc = jax.nn.silu(c_ctx)
    x_lat, x_ctx = x, ctx
    for l in range(DEPTH):
        last = l == DEPTH - 1
        mod_lat = (silu_c @ ada_w[l] + ada_b[l])[:, None, :]
        mod_ctx = (silu_cc @ ada_w[l] + ada_b[l])[None, None, :]
        sh1, sc1, g1, sh2, sc2, g2 = jnp.split(mod_lat, 6, axis=-1)
        csh1, csc1, cg1, csh2, csc2, cg2 = jnp.split(mod_ctx, 6, axis=-1)

        h_lat = modulate(x_lat, norm_mix_g[l], sh1, sc1)
        h_ctx = modulate(x_ctx, norm_mix_g[l], csh1, csc1)
        if l % 2 == 0:
            i = l // 2
            o_lat, o_ctx = even_mixer(h_lat, h_ctx, even_w_in[i], even_w_out[i], na_q_norm_g[i], na_k_norm_g[i],
                                      na_rpb[i], mlstm_gate_b[i], mlstm_norm_g[i], not last)
        else:
            i = l // 2
            o_lat, o_ctx = odd_mixer(h_lat, h_ctx, odd_w_in[i], odd_w_out[i], gqa_q_norm_g[i], gqa_k_norm_g[i],
                                     cos, sin, not last)
        x_lat = x_lat + g1 * o_lat

        h_lat = modulate(x_lat, norm_ffn_g[l], sh2, sc2).reshape(B * S, D)
        if last:
            y_lat = moe(h_lat, router_w, router_b, exp_w1[l], exp_w3[l], exp_w2[l])
        else:
            x_ctx = x_ctx + cg1 * o_ctx
            h_ctx = modulate(x_ctx, norm_ffn_g[l], csh2, csc2).reshape(B * L, D)
            y = moe(jnp.concatenate([h_lat, h_ctx], axis=0), router_w, router_b, exp_w1[l], exp_w3[l], exp_w2[l])
            y_lat = y[:B * S]
            x_ctx = x_ctx + cg2 * y[B * S:].reshape(B, L, D)
        x_lat = x_lat + g2 * y_lat.reshape(B, S, D)
    return x_lat


N_HEADS = 8
HEAD_DIM = 128
N_KV_HEADS = 2
ROPE_FRACTION_DIV = 4
ROPE_THETA_2 = 500000.0
IDX_HEADS = 8
IDX_DIM = 64
TOPK_MAX = 256
CONF_WIDTH = D_MODEL
CONF_KERNEL = 31
SC_WIDTH = D_MODEL
SC_KERNEL = 3
FFN_DIM = 2816
FFN_KERNEL = 3
N_BRANCH = 3
NORM_EPS = 1e-6

Q_COLS = N_HEADS * HEAD_DIM
KV_COLS = N_KV_HEADS * HEAD_DIM
IQ_COLS = IDX_HEADS * IDX_DIM
IK_COLS = IDX_DIM
IW_COLS = IDX_HEADS
A_COLS = 2 * CONF_WIDTH
C_COLS = 3 * SC_WIDTH
G_COLS = N_BRANCH * D_MODEL
_IN_SIZES = (Q_COLS, KV_COLS, KV_COLS, IQ_COLS, IK_COLS, IW_COLS, A_COLS, C_COLS, G_COLS)
N_IN = sum(_IN_SIZES)
IN_SPLITS = tuple(sum(_IN_SIZES[:i + 1]) for i in range(len(_IN_SIZES) - 1))


def rms_norm_2(x, g):
    xf = x.astype(jnp.float32)
    r = lax.rsqrt(jnp.mean(xf * xf, axis=-1, keepdims=True) + NORM_EPS)
    return (xf * r * g.astype(jnp.float32)).astype(x.dtype)

def layer_norm(x, g, b):
    xf = x.astype(jnp.float32)
    mu = jnp.mean(xf, axis=-1, keepdims=True)
    xc = xf - mu
    r = lax.rsqrt(jnp.mean(xc * xc, axis=-1, keepdims=True) + NORM_EPS)
    return (xc * r * g.astype(jnp.float32) + b.astype(jnp.float32)).astype(x.dtype)

def causal_dwconv(x, w):
    K, C = w.shape
    return lax.conv_general_dilated(
        x, w[:, None, :].astype(x.dtype), window_strides=(1,), padding=[(K - 1, 0)],
        dimension_numbers=("NWC", "WIO", "NWC"), feature_group_count=C)

def rope_tables(seq_len, rot_dim):
    pos = jnp.arange(seq_len, dtype=jnp.float32)
    inv_freq = jnp.power(ROPE_THETA_2, -jnp.arange(0, rot_dim, 2, dtype=jnp.float32) / rot_dim)
    ang = pos[:, None] * inv_freq[None, :]
    return jnp.cos(ang), jnp.sin(ang)

def partial_rope(x, cos, sin):
    half = cos.shape[-1]
    xf = x.astype(jnp.float32)
    x1, x2, xp = xf[..., :half], xf[..., half:2 * half], xf[..., 2 * half:]
    c = cos[None, :, None, :]
    s = sin[None, :, None, :]
    out = jnp.concatenate([x1 * c - x2 * s, x2 * c + x1 * s, xp], axis=-1)
    return out.astype(x.dtype)

def dsa_attention(q, k, v, iq, ik, iw):
    B, S, H, dh = q.shape
    G = k.shape[2]
    rep = H // G
    k_sel = min(TOPK_MAX, S // 4)
    n_blocks = S // Q_BLOCK
    key_pos = jnp.arange(S)
    scale = HEAD_DIM ** -0.5
    gather = jax.vmap(lambda arr, idx: arr[idx])

    def block(i):
        t0 = i * Q_BLOCK
        qb = lax.dynamic_slice_in_dim(q, t0, Q_BLOCK, axis=1)
        iqb = lax.dynamic_slice_in_dim(iq, t0, Q_BLOCK, axis=1)
        iwb = lax.dynamic_slice_in_dim(iw, t0, Q_BLOCK, axis=1)
        q_pos = t0 + jnp.arange(Q_BLOCK)
        rel = jax.nn.relu(jnp.einsum('bthd,bsd->bths', iqb, ik).astype(jnp.float32))
        score = jnp.einsum('bths,bth->bts', rel, iwb.astype(jnp.float32))
        causal = key_pos[None, :] <= q_pos[:, None]
        score = jnp.where(causal[None], score, -jnp.inf)
        _, idx = lax.top_k(score, k_sel)
        valid = idx <= q_pos[None, :, None]
        flat = idx.reshape(B, Q_BLOCK * k_sel)
        kg = gather(k, flat).reshape(B, Q_BLOCK, k_sel, G, dh)
        vg = gather(v, flat).reshape(B, Q_BLOCK, k_sel, G, dh)
        qg = qb.reshape(B, Q_BLOCK, G, rep, dh)
        logits = jnp.einsum('btgrd,btkgd->btgrk', qg, kg).astype(jnp.float32) * scale
        logits = jnp.where(valid[:, :, None, None, :], logits, -jnp.inf)
        p = jax.nn.softmax(logits, axis=-1).astype(v.dtype)
        o = jnp.einsum('btgrk,btkgd->btgrd', p, vg)
        return o.reshape(B, Q_BLOCK, H * dh)

    out = lax.map(block, jnp.arange(n_blocks))
    return out.transpose(1, 0, 2, 3).reshape(B, S, H * dh)

def hybrid_layer(x, rope_attn, rope_idx, norm1_g, w_in, q_norm_g, k_norm_g, w_attn_out,
                 conf_conv_w, conf_conv_b, conf_ln_g, conf_ln_b, w_conf_out,
                 sc_conv_w, w_sc_out, w_o, norm2_g, w_up, ffn_conv_w, ffn_conv_b, w_down):
    B, S, _ = x.shape
    h = rms_norm_2(x, norm1_g)
    proj = h @ w_in
    q, k, v, iq, ik, iw, a_in, c_in, g_in = jnp.split(proj, IN_SPLITS, axis=-1)

    q = partial_rope(rms_norm_2(q.reshape(B, S, N_HEADS, HEAD_DIM), q_norm_g), *rope_attn)
    k = partial_rope(rms_norm_2(k.reshape(B, S, N_KV_HEADS, HEAD_DIM), k_norm_g), *rope_attn)
    v = v.reshape(B, S, N_KV_HEADS, HEAD_DIM)
    iq = partial_rope(iq.reshape(B, S, IDX_HEADS, IDX_DIM), *rope_idx)
    ik = partial_rope(ik[:, :, None, :], *rope_idx)[:, :, 0, :]
    iw = iw * (IDX_HEADS ** -0.5 * IDX_DIM ** -0.5)
    y_attn = dsa_attention(q, k, v, iq, ik, iw) @ w_attn_out

    a_val, a_gate = jnp.split(a_in, 2, axis=-1)
    a = causal_dwconv(a_val * jax.nn.sigmoid(a_gate), conf_conv_w) + conf_conv_b
    y_conf = jax.nn.silu(layer_norm(a, conf_ln_g, conf_ln_b)) @ w_conf_out

    c_b, c_c, c_x = jnp.split(c_in, 3, axis=-1)
    y_sc = (c_b * causal_dwconv(c_c * c_x, sc_conv_w)) @ w_sc_out

    gates = jax.nn.sigmoid(g_in.reshape(B, S, N_BRANCH, D_MODEL).astype(jnp.float32)).astype(x.dtype)
    merged = gates[:, :, 0] * y_conf + gates[:, :, 1] * y_attn + gates[:, :, 2] * y_sc
    x = x + merged @ w_o

    u = causal_dwconv(rms_norm_2(x, norm2_g) @ w_up, ffn_conv_w) + ffn_conv_b
    u_gate, u_val = jnp.split(u, 2, axis=-1)
    return x + (jax.nn.silu(u_gate) * u_val) @ w_down

def second_inputs(seed: int = 0) -> dict:
    key = jax.random.key(seed)
    ks = jax.random.split(key, 20)
    f32 = jnp.float32

    def nrm(k, shape, scale):
        return jax.random.normal(k, shape, f32) * scale

    L = DEPTH
    return {
        "x": nrm(ks[0], (BATCH, SEQ, D_MODEL), 1.0),
        "norm1_g": 1.0 + nrm(ks[1], (L, D_MODEL), 0.05),
        "w_in": nrm(ks[2], (L, D_MODEL, N_IN), D_MODEL ** -0.5),
        "q_norm_g": 1.0 + nrm(ks[3], (L, HEAD_DIM), 0.05),
        "k_norm_g": 1.0 + nrm(ks[4], (L, HEAD_DIM), 0.05),
        "w_attn_out": nrm(ks[5], (L, Q_COLS, D_MODEL), Q_COLS ** -0.5),
        "conf_conv_w": nrm(ks[6], (L, CONF_KERNEL, CONF_WIDTH), CONF_KERNEL ** -0.5),
        "conf_conv_b": nrm(ks[7], (L, CONF_WIDTH), 0.01),
        "conf_ln_g": 1.0 + nrm(ks[8], (L, CONF_WIDTH), 0.05),
        "conf_ln_b": nrm(ks[9], (L, CONF_WIDTH), 0.01),
        "w_conf_out": nrm(ks[10], (L, CONF_WIDTH, D_MODEL), CONF_WIDTH ** -0.5),
        "sc_conv_w": nrm(ks[11], (L, SC_KERNEL, SC_WIDTH), SC_KERNEL ** -0.5),
        "w_sc_out": nrm(ks[12], (L, SC_WIDTH, D_MODEL), SC_WIDTH ** -0.5),
        "w_o": nrm(ks[13], (L, D_MODEL, D_MODEL), D_MODEL ** -0.5),
        "norm2_g": 1.0 + nrm(ks[14], (L, D_MODEL), 0.05),
        "w_up": nrm(ks[15], (L, D_MODEL, 2 * FFN_DIM), D_MODEL ** -0.5),
        "ffn_conv_w": nrm(ks[16], (L, FFN_KERNEL, 2 * FFN_DIM), FFN_KERNEL ** -0.5),
        "ffn_conv_b": nrm(ks[17], (L, 2 * FFN_DIM), 0.01),
        "w_down": nrm(ks[18], (L, FFN_DIM, D_MODEL), FFN_DIM ** -0.5),
    }

def second_block(x, norm1_g, w_in, q_norm_g, k_norm_g, w_attn_out, conf_conv_w, conf_conv_b,
              conf_ln_g, conf_ln_b, w_conf_out, sc_conv_w, w_sc_out, w_o, norm2_g, w_up,
              ffn_conv_w, ffn_conv_b, w_down):
    S = x.shape[1]
    rope_attn = rope_tables(S, HEAD_DIM // ROPE_FRACTION_DIV)
    rope_idx = rope_tables(S, IDX_DIM // ROPE_FRACTION_DIV)
    for l in range(DEPTH):
        x = hybrid_layer(x, rope_attn, rope_idx, norm1_g[l], w_in[l], q_norm_g[l], k_norm_g[l],
                         w_attn_out[l], conf_conv_w[l], conf_conv_b[l], conf_ln_g[l], conf_ln_b[l],
                         w_conf_out[l], sc_conv_w[l], w_sc_out[l], w_o[l], norm2_g[l], w_up[l],
                         ffn_conv_w[l], ffn_conv_b[l], w_down[l])
    return x


def setup_inputs(seed=0):
    out = dict(first_inputs(seed))
    for name, value in second_inputs(seed + 1).items():
        if name != "x":
            out[name + "_2"] = value
    return out


def reference(
    x, c, ctx, c_ctx, ada_w, ada_b, norm_mix_g, norm_ffn_g, even_w_in, even_w_out, na_q_norm_g,
    na_k_norm_g, na_rpb, mlstm_gate_b, mlstm_norm_g, odd_w_in, odd_w_out, gqa_q_norm_g,
    gqa_k_norm_g, router_w, router_b, exp_w1, exp_w3, exp_w2, norm1_g_2, w_in_2, q_norm_g_2,
    k_norm_g_2, w_attn_out_2, conf_conv_w_2, conf_conv_b_2, conf_ln_g_2, conf_ln_b_2,
    w_conf_out_2, sc_conv_w_2, w_sc_out_2, w_o_2, norm2_g_2, w_up_2, ffn_conv_w_2, ffn_conv_b_2,
    w_down_2,
):
    x = first_block(
        x, c, ctx, c_ctx, ada_w, ada_b, norm_mix_g, norm_ffn_g, even_w_in, even_w_out,
        na_q_norm_g, na_k_norm_g, na_rpb, mlstm_gate_b, mlstm_norm_g, odd_w_in, odd_w_out,
        gqa_q_norm_g, gqa_k_norm_g, router_w, router_b, exp_w1, exp_w3, exp_w2,
    )
    return second_block(
        x, norm1_g_2, w_in_2, q_norm_g_2, k_norm_g_2, w_attn_out_2, conf_conv_w_2,
        conf_conv_b_2, conf_ln_g_2, conf_ln_b_2, w_conf_out_2, sc_conv_w_2, w_sc_out_2, w_o_2,
        norm2_g_2, w_up_2, ffn_conv_w_2, ffn_conv_b_2, w_down_2,
    )


_drawn_inputs = setup_inputs


def setup_inputs(seed=0):
    import zlib

    import numpy as np

    out = dict(_drawn_inputs(seed))
    spreads = {}
    factors = {'na_q_norm_g': 8.0,
     'na_k_norm_g': 7.615,
     'na_rpb': 8.0,
     'gqa_q_norm_g': 5.25,
     'gqa_k_norm_g': 5.199,
     'q_norm_g_2': 5.98,
     'k_norm_g_2': 5.862,
     'conf_conv_b_2': 4.98,
     'conf_ln_b_2': 8.0,
     'ffn_conv_b_2': 4.958}
    for name, (base, spread) in spreads.items():
        noise = np.random.default_rng([zlib.crc32(name.encode()), seed]).standard_normal(out[name].shape)
        drawn = base * np.exp(spread * noise) if base else spread * noise
        out[name] = __import__('jax').numpy.asarray(drawn.astype(out[name].dtype))
    for name, factor in factors.items():
        out[name] = (out[name] * factor).astype(out[name].dtype)
    return out
```

```python
from contextlib import ExitStack

import numpy as np
import concourse.bass as bass
from concourse import mybir

F32 = mybir.dt.float32
BF16 = mybir.dt.bfloat16
ALU = mybir.AluOpType
ACT = mybir.ActivationFunctionType
AX = mybir.AxisListType.X

P = 128
D = 1024
KT = D // P
RING = 3
COLS = 512
EPS = 1e-6
BIG = 1e30

S_LAT = 256
S_CTX = 256
LT = S_LAT // P
CT = S_CTX // P
GRID_W = 64
ROWS = S_LAT // GRID_W
H_A, HD_A = 8, 64
H_B, DK_B, DV_B = 4, 64, 128
D_IN_EVEN = 3 * H_A * HD_A + 2 * H_B * DK_B + 2 * H_B * DV_B + 4 * H_B
AQ, AK, AV = 0, 512, 1024
MQ, MK, MV, MO, MG = 1536, 1792, 2048, 2560, 3072
MQ0, MK0, MV0, MO0, MG0 = 0, MK - MQ, MV - MQ, MO - MQ, MG - MQ
H_C, KV_C, HD_C = 8, 2, 128
N_EXP, N_GROUPS, EPG = 16, 4, 4
D_FF = 512
FFN = 2816
FT = FFN // P
CONF_K, SC_K = 31, 3
IDX_H, IDX_D = 8, 64
TOPK = 64
N_IN2 = 10312
Q2, K2, V2, IQ2, IK2, IW2, A2, C2, G2 = 0, 1024, 1280, 1536, 2048, 2112, 2120, 4168, 7240
QKV2 = A2


class Signal:

    def __init__(self, sem):
        self.sem = sem
        self.n = 0


def build(nc, A, out, upto=None):
    ctx = ExitStack()
    serial = [0]

    def sb(stack, name, shape, dt=F32):
        serial[0] += 1
        return stack.enter_context(nc.sbuf_tensor(name, shape, dt))

    def signal(name):
        return Signal(ctx.enter_context(nc.semaphore(name)))

    bank = [ctx.enter_context(nc.psum_tensor(f"bank{i}", [P, COLS], F32)) for i in range(8)]

    ring = [sb(ctx, f"ring{i}", [P, KT * COLS]) for i in range(RING)]
    x = sb(ctx, "x", [P, 4, D])
    hT = sb(ctx, "hT", [P, KT, 512])
    ident = sb(ctx, "ident", [P, P])
    ones = sb(ctx, "ones", [P, P])
    eps_col = sb(ctx, "eps_col", [P, 1])
    stats = sb(ctx, "stats", [P, 3, 64])

    chunk_landed = [signal(f"chunk_landed{i}") for i in range(RING)]
    chunk_used = signal("chunk_used")
    stage_done = signal("stage_done")
    small_landed = signal("small_landed")
    out_landed = signal("out_landed")
    bank_full = signal("bank_full")
    bank_free_act = signal("bank_free_act")
    bank_free_dve = signal("bank_free_dve")
    act_out = signal("act_out")
    dve_out = signal("dve_out")
    scores_ready = signal("scores_ready")
    max_ready = signal("max_ready")
    probs_ready = signal("probs_ready")
    turned_ready = signal("turned_ready")
    probsT_ready = signal("probsT_ready")
    pv_ready = signal("pv_ready")
    head_stored = signal("head_stored")
    chunks = [0]

    block = ctx.enter_context(nc.Block())

    class Stage:

        def __init__(self):
            self.before = stage_done.n
            self.members = 0

        def _run(self, start, fn):
            before = self.before
            self.members += 1

            @start
            def _(eng):
                if before:
                    eng.wait_ge(stage_done.sem, before)
                fn(eng)
                eng.drain()
                eng.sem_inc(stage_done.sem, 1)

        def tensor(self, fn):
            self._run(block.tensor, fn)

        def vector(self, fn):
            self._run(block.vector, fn)

        def scalar(self, fn):
            self._run(block.scalar, fn)

        def gpsimd(self, fn):
            self._run(block.gpsimd, fn)

        def end(self):
            stage_done.n += self.members

    def chunk(n):
        return ring[n % RING]

    def stream(parts):
        n0 = chunks[0]

        @block.sync
        def _(sp):
            for j, pieces in enumerate(parts):
                n = n0 + j
                if n >= RING:
                    used, value = used_at[n - RING]
                    sp.wait_ge(used.sem, value)
                for off, src in pieces:
                    k, w = src.shape[1], src.shape[2]
                    dst = chunk(n)[:, :].rearrange("p (k n) -> p k n", k=KT)[:, 0:k, off:off + w]
                    if len(pieces) == 1:
                        dst = chunk(n)[:, 0:k * w].rearrange("p (k n) -> p k n", k=k)
                    sp.dma_start(dst, src).then_inc(chunk_landed[n % RING].sem, 16)
                    chunk_landed[n % RING].n += 16
                landed_at[n] = chunk_landed[n % RING].n
        chunks[0] += len(parts)
        return n0

    landed_at = {}
    used_at = {}

    def arrived(eng, n):
        eng.wait_ge(chunk_landed[n % RING].sem, landed_at[n])

    def rows(w):
        return w.rearrange("(t p) n -> p t n", p=P)

    _small = [0]

    def load_small(pairs):
        st = Stage()

        @st.scalar
        def _(act):
            for dst, src in pairs:
                act.dma_start(dst, src).then_inc(small_landed.sem, 16)
                small_landed.n += 16
            act.wait_ge(small_landed.sem, small_landed.n)
        st.end()

    st = Stage()

    @st.gpsimd
    def _(pool):
        pool.memset(ident[:, :], 0.0)
        pool.memset(ones[:, :], 1.0)
        pool.memset(eps_col[:, :], EPS)
        pool.drain()
        pool.affine_select(out=ident[:, :], in_=ident[:, :], compare_op=ALU.not_equal, fill=1.0,
                           base=0, pattern=[[-1, P]], channel_multiplier=1)
    st.end()

    load_small([(x[:, CT:CT + LT, :], A["x"][0].rearrange("(m p) d -> p m d", p=P)),
                (x[:, 0:CT, :], A["ctx"][0].rearrange("(m p) d -> p m d", p=P))])

    def normalise(tiles, xn):
        st = Stage()
        a0, d0 = act_out.n, dve_out.n

        @st.scalar
        def _(act):
            for i, m in enumerate(tiles):
                act.activation(xn[:, i, :], x[:, m, :], ACT.Square, accum_out=stats[:, 0, i:i + 1])
            act.drain()
            act.activation(stats[:, 1, 0:len(tiles)], stats[:, 0, 0:len(tiles)], ACT.Sqrt,
                           scale=1.0 / D, bias=eps_col[:, :]).then_inc(act_out.sem, 1)

        @st.vector
        def _(dve):
            dve.wait_ge(act_out.sem, a0 + 1)
            dve.reciprocal(stats[:, 2, 0:len(tiles)], stats[:, 1, 0:len(tiles)])
            dve.drain()
            for i, m in enumerate(tiles):
                dve.tensor_scalar(xn[:, i, :], x[:, m, :], stats[:, 2, i:i + 1], None, ALU.mult)
        act_out.n = a0 + 1
        st.end()

    def turn(src, dst, n_tok, n_feat, mods=None):
        st = Stage()
        f0, a0 = bank_full.n, bank_free_act.n

        @st.tensor
        def _(pe):
            for k in range(n_feat):
                if k >= 8:
                    pe.wait_ge(bank_free_act.sem, a0 + k - 7)
                for i in range(n_tok):
                    mm = pe.transpose(bank[k % 8][:, i * P:(i + 1) * P], src(i, k), ident[:, :])
                mm.then_inc(bank_full.sem, 1)

        @st.scalar
        def _(act):
            for k in range(n_feat):
                act.wait_ge(bank_full.sem, f0 + k + 1)
                if mods is None:
                    a = act.activation(dst(k), bank[k % 8][:, 0:n_tok * P], ACT.Copy)
                else:
                    for lo, hi, scale, shift in mods(k):
                        a = act.activation(dst(k)[:, lo:hi], bank[k % 8][:, lo:hi], ACT.Identity,
                                           scale=scale, bias=shift)
                a.then_inc(bank_free_act.sem, 1)
        bank_full.n += n_feat
        bank_free_act.n += n_feat
        st.end()

    def linear(lhs, tiles, parts, evac, on="vector", side=None, accumulate=None, w_rows=P):
        g = accumulate or 1
        nt = len(tiles)
        f0, n0 = bank_full.n, chunks[0]
        for c in range(len(parts)):
            if c % g == g - 1:
                used_at[n0 + c] = (bank_full, f0 + (c // g + 1) * nt)
            else:
                chunk_used.n += 1
                used_at[n0 + c] = (chunk_used, chunk_used.n)
        stream([pieces for _, _, pieces in parts])
        st = Stage()
        free = bank_free_act if on == "scalar" else bank_free_dve
        e0 = free.n

        @st.tensor
        def _(pe):
            for c, (k_tiles, w, _) in enumerate(parts):
                arrived(pe, n0 + c)
                wt = chunk(n0 + c)[:, 0:k_tiles * w].rearrange("p (k n) -> p k n", k=k_tiles)
                for i, m in enumerate(tiles):
                    use = (c // g) * nt + i
                    if c % g == 0 and use >= 8:
                        pe.wait_ge(free.sem, e0 + use - 7)
                    for k in range(k_tiles):
                        lt = lhs(c, m, k)
                        mm = pe.matmul(bank[use % 8][0:lt.shape[1], 0:w], lt, wt[:, k, :],
                                       start=(k == 0 and c % g == 0),
                                       stop=(k == k_tiles - 1 and c % g == g - 1))
                    if c % g == g - 1:
                        mm.then_inc(bank_full.sem, 1)
                if c % g != g - 1:
                    mm.then_inc(chunk_used.sem, 1)

        def reader(eng):
            for c in range(len(parts) // g):
                for i, m in enumerate(tiles):
                    use = c * nt + i
                    eng.wait_ge(bank_full.sem, f0 + use + 1)
                    evac(eng, c, i, bank[use % 8]).then_inc(free.sem, 1)
        if on == "scalar":
            st.scalar(reader)
            if side:
                st.vector(side)
        else:
            st.vector(reader)
            if side:
                st.scalar(side)
        bank_full.n += nt * (len(parts) // g)
        free.n += nt * (len(parts) // g)
        st.end()


    def head_norm(views, d, tmp):
        n = [v.shape[1] for v in views]
        at = [sum(n[:j]) for j in range(len(n))]
        total = sum(n)
        st = Stage()
        a0, d0 = act_out.n, dve_out.n

        @st.vector
        def _(dve):
            for j, v in enumerate(views):
                sq = tmp[:, j % 2, 0:n[j] * d].rearrange("p (n d) -> p n d", d=d)
                dve.tensor_tensor(sq, v, v, ALU.mult)
                dve.drain()
                red = dve.tensor_reduce(stats[:, 0, at[j]:at[j] + n[j]], sq, AX, ALU.add)
            red.then_inc(dve_out.sem, 1)
            dve.wait_ge(act_out.sem, a0 + 1)
            dve.reciprocal(stats[:, 2, 0:total], stats[:, 1, 0:total])
            dve.drain()
            for j, v in enumerate(views):
                r = stats[:, 2, at[j]:at[j] + n[j]].unsqueeze(2).to_broadcast([P, n[j], d])
                dve.tensor_tensor(v, v, r, ALU.mult)

        @st.scalar
        def _(act):
            act.wait_ge(dve_out.sem, d0 + 1)
            act.activation(stats[:, 1, 0:total], stats[:, 0, 0:total], ACT.Sqrt,
                           scale=1.0 / d, bias=eps_col[:, :]).then_inc(act_out.sem, 1)
        act_out.n += 1
        dve_out.n += 1
        st.end()

    def attend(units, probs, probsT, col):
        st = Stage()
        n = len(units)
        s0, m0, p0, t0 = scores_ready.n, max_ready.n, probs_ready.n, turned_ready.n
        pt0, v0, h0 = probsT_ready.n, pv_ready.n, head_stored.n
        S, T, O = bank[0:2], bank[2:4], bank[4:6]

        @st.tensor
        def _(pe):
            for s in range(n + 2):
                if s < n:
                    if s >= 2:
                        pe.wait_ge(probs_ready.sem, p0 + s - 1)
                    for lt, rhs, lo, start, stop in units[s][0]:
                        mm = pe.matmul(S[s % 2][:, lo:lo + rhs.shape[1]], lt, rhs,
                                       start=start, stop=stop)
                    mm.then_inc(scores_ready.sem, 1)
                if 1 <= s <= n:
                    u = s - 1
                    pe.wait_ge(probs_ready.sem, p0 + u + 1)
                    if u >= 2:
                        pe.wait_ge(probsT_ready.sem, pt0 + u - 1)
                    for j in range(units[u][1] // P):
                        mm = pe.transpose(T[u % 2][:, j * P:(j + 1) * P],
                                          probs[:, u % 2, j * P:(j + 1) * P], ident[:, :])
                    mm.then_inc(turned_ready.sem, 1)
                if s >= 2:
                    u = s - 2
                    pe.wait_ge(probsT_ready.sem, pt0 + u + 1)
                    if u >= 2:
                        pe.wait_ge(head_stored.sem, h0 + u - 1)
                    vs = units[u][2]
                    for j, v in enumerate(vs):
                        mm = pe.matmul(O[u % 2][:, 0:v.shape[1]], probsT[:, u % 2, j * P:(j + 1) * P],
                                       v, start=(j == 0), stop=(j == len(vs) - 1))
                    mm.then_inc(pv_ready.sem, 1)

        @st.vector
        def _(dve):
            for s in range(n + 1):
                if s < n:
                    dve.wait_ge(scores_ready.sem, s0 + s + 1)
                    dve.tensor_reduce(col[:, 1, s % 4:s % 4 + 1], S[s % 2][:, 0:units[s][1]], AX, ALU.max)
                    dve.drain()
                    dve.tensor_scalar(col[:, 0, s % 4:s % 4 + 1], col[:, 1, s % 4:s % 4 + 1], -1.0, None,
                                      ALU.mult).then_inc(max_ready.sem, 1)
                if s >= 1:
                    u = s - 1
                    dve.wait_ge(turned_ready.sem, t0 + u + 1)
                    dve.reciprocal(col[:, 3, u % 4:u % 4 + 1], col[:, 2, u % 4:u % 4 + 1])
                    if u >= 2:
                        dve.wait_ge(pv_ready.sem, v0 + u - 1)
                    dve.tensor_copy(probsT[:, u % 2, 0:units[u][1]],
                                    T[u % 2][:, 0:units[u][1]]).then_inc(probsT_ready.sem, 1)

        @st.scalar
        def _(act):
            for s in range(n + 2):
                if s < n:
                    act.wait_ge(max_ready.sem, m0 + s + 1)
                    if s >= 2:
                        act.wait_ge(turned_ready.sem, t0 + s - 1)
                    act.activation(probs[:, s % 2, 0:units[s][1]], S[s % 2][:, 0:units[s][1]], ACT.Exp,
                                   bias=col[:, 0, s % 4:s % 4 + 1],
                                   accum_out=col[:, 2, s % 4:s % 4 + 1]).then_inc(probs_ready.sem, 1)
                if s >= 2:
                    u = s - 2
                    act.wait_ge(probsT_ready.sem, pt0 + u + 1)
                    act.wait_ge(pv_ready.sem, v0 + u + 1)
                    dst = units[u][3]
                    act.activation(dst, O[u % 2][:, 0:dst.shape[1]], ACT.Copy,
                                   scale=col[:, 3, u % 4:u % 4 + 1]).then_inc(head_stored.sem, 1)
        for sig in (scores_ready, max_ready, probs_ready, turned_ready, probsT_ready, pv_ready, head_stored):
            sig.n += n
        st.end()

    def wait_value(sig):
        return sig.n

    silu_c = sb(ctx, "silu_c", [P, KT, 2])
    router_w = sb(ctx, "router_w_sb", [P, KT, N_EXP])
    router_b = sb(ctx, "router_b_sb", [P, N_EXP])
    load_small([(silu_c[:, :, :], A["cond"]),
                (router_w[:, :, :], rows(A["router_w"])),
                (router_b[:, :], A["router_b"].unsqueeze(0).to_broadcast([P, N_EXP]))])
    st = Stage()

    @st.scalar
    def _(act):
        act.activation(silu_c[:, :, :], silu_c[:, :, :], ACT.Silu)
    st.end()

    def ada(l, modc, gateb, gcols):
        with ExitStack() as mem:
            mod = sb(mem, f"mod{l}", [2, 6 * D])
            load_small([(mod[s:s + 1, :], A["ada_b"][l:l + 1, :]) for s in range(2)]
                       + [(gcols[:, 0, :], A["norm_mix_cols"][l]), (gcols[:, 1, :], A["norm_ffn_cols"][l])])
            w = A["ada_w"][l].rearrange("(t p) n -> p t n", p=P)

            def evac(eng, c, i, b):
                cols = slice(c * COLS, (c + 1) * COLS)
                return eng.tensor_tensor(mod[:, cols], b[0:2, :], mod[:, cols], ALU.add)
            linear(lambda c, m, k: silu_c[:, k, :], [0],
                   [(KT, COLS, [(0, w[:, :, c * COLS:(c + 1) * COLS])]) for c in range(6 * D // COLS)], evac)
            st = Stage()
            f0, a0 = bank_full.n, bank_free_act.n

            @st.tensor
            def _(pe):
                for v, part in enumerate((0, 1, 3, 4)):
                    for k in range(KT):
                        j = v * KT + k
                        mm = pe.transpose(bank[0][:, 2 * j:2 * j + 2],
                                          mod[:, part * D + k * P:part * D + (k + 1) * P], ident[0:2, 0:2])
                mm.then_inc(bank_full.sem, 1)
                for g, part in enumerate((2, 5)):
                    for s in range(2):
                        for half in range(2):
                            j = 1 + (g * 2 + s) * 2 + half
                            if j == 8:
                                pe.wait_ge(bank_free_act.sem, a0 + 1)
                            mm = pe.matmul(bank[j % 8][:, :], ident[0:2, s:s + 1].to_broadcast([2, P]),
                                           mod[:, part * D + half * COLS:part * D + (half + 1) * COLS],
                                           start=True, stop=True)
                            mm.then_inc(bank_full.sem, 1)

            @st.scalar
            def _(act):
                act.wait_ge(bank_full.sem, f0 + 1)
                act.activation(modc[:, :, :], bank[0][:, 0:64], ACT.Copy).then_inc(bank_free_act.sem, 1)
                for j in range(1, 9):
                    act.wait_ge(bank_full.sem, f0 + 1 + j)
                    g, s, half = (j - 1) // 4, (j - 1) // 2 % 2, (j - 1) % 2
                    act.activation(gateb[:, g, s, half * COLS:(half + 1) * COLS], bank[j % 8][:, :], ACT.Copy)

            @st.vector
            def _(dve):
                dve.wait_ge(bank_free_act.sem, a0 + 1)
                for v in range(2):
                    sc = modc[:, (2 * v + 1) * KT:(2 * v + 2) * KT, :]
                    dve.scalar_tensor_tensor(sc, sc, 1.0, gcols[:, v, :].unsqueeze(2).to_broadcast([P, KT, 2]),
                                             ALU.add, ALU.mult)
            bank_full.n += 9
            bank_free_act.n += 1
            st.end()

    def modulated(modc, v, tiles):
        n_ctx = sum(m < CT for m in tiles)

        def mods(k):
            sh, sc = modc[:, 2 * v * KT + k, :], modc[:, (2 * v + 1) * KT + k, :]
            out = []
            if n_ctx:
                out.append((0, n_ctx * P, sc[:, 1:2], sh[:, 1:2]))
            out.append((n_ctx * P, len(tiles) * P, sc[:, 0:1], sh[:, 0:1]))
            return out
        with ExitStack() as mem:
            xn = sb(mem, f"xn{serial[0]}", [P, len(tiles), D])
            normalise(tiles, xn)
            turn(lambda i, k: xn[:, i, k * P:(k + 1) * P], lambda k: hT[:, k, 0:len(tiles) * P],
                 len(tiles), KT, mods)

    def project_out(o, w, tiles, gateb, g):
        turn(lambda i, k: o[:, i, k * P:(k + 1) * P], lambda k: hT[:, k, 0:len(tiles) * P], len(tiles), KT)
        with ExitStack() as mem:
            tmp = sb(mem, f"po{serial[0]}", [P, 2, COLS])

            def evac(eng, c, i, b):
                m, cols = tiles[i], slice(c * COLS, (c + 1) * COLS)
                t = tmp[:, i % 2, :]
                eng.drain()
                if gateb is None:
                    return eng.tensor_tensor(x[:, m, cols], b[:, :], x[:, m, cols], ALU.add)
                eng.tensor_tensor(t, b[:, :], gateb[:, g, int(m < CT), cols], ALU.mult)
                eng.drain()
                return eng.tensor_tensor(x[:, m, cols], t, x[:, m, cols], ALU.add)
            linear(lambda c, m, k: hT[:, k, tiles.index(m) * P:(tiles.index(m) + 1) * P], tiles,
                   [(KT, COLS, [(0, rows(w)[:, :, c * COLS:(c + 1) * COLS])]) for c in range(D // COLS)], evac)

    moe_up = signal("moe_up")
    moe_silu = signal("moe_silu")
    moe_hidden = signal("moe_hidden")
    moe_down = signal("moe_down")
    moe_added = signal("moe_added")

    def moe(l, tiles, gateb):
        nt = len(tiles)
        N = nt * P
        n_y = nt * (D // COLS)
        with ExitStack() as mem:
            comb = sb(mem, f"comb{l}", [P, N_EXP, nt])
            with ExitStack() as mem2:
                route(l, mem2, comb, nt)
            y = sb(mem, f"y{l}", [P, nt, D])
            hid = sb(mem, f"hid{l}", [P, 4, N])
            sg = sb(mem, f"sg{l}", [P, 4, N])
            cc = sb(mem, f"cc{l}", [P, nt])
            w1, w3, w2 = A["exp_w1"][l], A["exp_w3"][l], A["exp_w2"][l]
            n0 = chunks[0]
            slot = [(n0 + j) % RING for j in range(3)]
            land0 = [chunk_landed[s].n for s in slot]
            cu0, u0, si0, h0, d0, y0 = (chunk_used.n, moe_up.n, moe_silu.n, moe_hidden.n, moe_down.n,
                                        moe_added.n)

            def load(sp, j, e):
                w = (w1, w3, w2)[j][bass.ds(e, 1)].rearrange("a (t p) n -> p (a t) n", p=P)
                k = w.shape[1]
                sp.dma_start(ring[slot[j]][:, :].rearrange("p (k n) -> p k n", k=k), w)\
                    .then_inc(chunk_landed[slot[j]].sem, 16)

            @block.sync
            def _(sp):
                for j in range(3):
                    if n0 + j >= RING:
                        used, value = used_at[n0 + j - RING]
                        sp.wait_ge(used.sem, value)
                    load(sp, j, 0)
                with sp.Fori(1, N_EXP) as e:
                    sp.wait_ge(chunk_used.sem, e + cu0)
                    load(sp, 0, e)
                    sp.wait_ge(moe_up.sem, e * 4 + u0)
                    load(sp, 1, e)
                    sp.wait_ge(moe_down.sem, e * n_y + d0)
                    load(sp, 2, e)

            st = Stage()

            @st.tensor
            def _(pe):
                up1 = ring[slot[0]][:, :].rearrange("p (k n) -> p k n", k=KT)
                up3 = ring[slot[1]][:, :].rearrange("p (k n) -> p k n", k=KT)
                down = ring[slot[2]][:, :].rearrange("p (k n) -> p k n", k=4)
                with pe.Fori(0, N_EXP) as e:
                    pe.wait_ge(chunk_landed[slot[0]].sem, e * 16 + (land0[0] + 16))
                    for f in range(4):
                        if f >= 2:
                            pe.wait_ge(moe_hidden.sem, e * 4 + (h0 + f - 1))
                        fs = slice(f * P, (f + 1) * P)
                        for k in range(KT):
                            mm = pe.matmul(bank[2 * f % 4][:, 0:N], up1[:, k, fs], hT[:, k, 0:N],
                                           start=(k == 0), stop=(k == KT - 1))
                        if f == 3:
                            mm.then_inc(chunk_used.sem, 1)
                        if f == 0:
                            pe.wait_ge(chunk_landed[slot[1]].sem, e * 16 + (land0[1] + 16))
                        for k in range(KT):
                            mm = pe.matmul(bank[2 * f % 4 + 1][:, 0:N], up3[:, k, fs], hT[:, k, 0:N],
                                           start=(k == 0), stop=(k == KT - 1))
                        mm.then_inc(moe_up.sem, 1)
                    pe.wait_ge(chunk_landed[slot[2]].sem, e * 16 + (land0[2] + 16))
                    pe.wait_ge(moe_hidden.sem, e * 4 + (h0 + 4))
                    for i in range(n_y):
                        m, half = i // 2, i % 2
                        pe.wait_ge(moe_added.sem, e * n_y + (y0 + i + 1))
                        for k in range(4):
                            mm = pe.matmul(bank[4 + i % 4][:, :], hid[:, k, m * P:(m + 1) * P],
                                           down[:, k, half * COLS:(half + 1) * COLS],
                                           start=(k == 0), stop=(k == 3))
                        mm.then_inc(moe_down.sem, 1)

            @st.scalar
            def _(act):
                with act.Fori(0, N_EXP) as e:
                    for f in range(4):
                        act.wait_ge(moe_up.sem, e * 4 + (u0 + f + 1))
                        act.activation(sg[:, f, :], bank[2 * f % 4][:, 0:N], ACT.Silu)\
                            .then_inc(moe_silu.sem, 1)

            @st.vector
            def _(dve):
                for q in range(4):
                    w = nt * D // 4
                    dve.memset(y[:, :, :].rearrange("p m d -> p (m d)")[:, q * w:(q + 1) * w], 0.0)\
                        .then_inc(moe_added.sem, 1)
                with dve.Fori(0, N_EXP) as e:
                    dve.drain()
                    dve.tensor_copy(cc[:, :], comb[:, bass.ds(e, 1), :].rearrange("p a m -> p (a m)"))
                    for f in range(4):
                        dve.wait_ge(moe_silu.sem, e * 4 + (si0 + f + 1))
                        dve.tensor_tensor(hid[:, f, :], sg[:, f, :], bank[2 * f % 4 + 1][:, 0:N], ALU.mult)\
                            .then_inc(moe_hidden.sem, 1)
                    dve.drain()
                    for i in range(n_y):
                        m, cols = i // 2, slice(i % 2 * COLS, (i % 2 + 1) * COLS)
                        dve.wait_ge(moe_down.sem, e * n_y + (d0 + i + 1))
                        dve.scalar_tensor_tensor(y[:, m, cols], bank[4 + i % 4][:, :], cc[:, m:m + 1],
                                                 y[:, m, cols], ALU.mult, ALU.add)\
                            .then_inc(moe_added.sem, 1)
                dve.drain()
                for i, m in enumerate(tiles):
                    dve.tensor_tensor(y[:, i, :], y[:, i, :], gateb[:, 1, int(m < CT), :], ALU.mult)
                dve.drain()
                for i, m in enumerate(tiles):
                    dve.tensor_tensor(x[:, m, :], y[:, i, :], x[:, m, :], ALU.add)
            st.end()
            chunks[0] += 3 * N_EXP
            chunk_used.n += N_EXP
            moe_up.n += 4 * N_EXP
            moe_silu.n += 4 * N_EXP
            moe_hidden.n += 4 * N_EXP
            moe_down.n += n_y * N_EXP
            moe_added.n += n_y * N_EXP + 4
            for j, used in enumerate((chunk_used, moe_up, moe_down)):
                chunk_landed[slot[j]].n += 16 * N_EXP
                used_at[chunks[0] - 3 + j] = (used, used.n)

    def route(l, mem, comb, nt):
        f0, a0 = bank_full.n, act_out.n
        sc = sb(mem, f"r_sc{l}", [P, nt, N_EXP])
        sel = sb(mem, f"r_sel{l}", [P, nt, N_EXP])
        pair = sb(mem, f"r_pair{l}", [P, nt * N_GROUPS, 6])
        gs = sb(mem, f"r_gs{l}", [P, nt * N_GROUPS])
        best = sb(mem, f"r_best{l}", [P, nt])
        hot = sb(mem, f"r_hot{l}", [P, nt, N_EXP])
        hot2 = sb(mem, f"r_hot2{l}", [P, nt, N_EXP])
        prio = sb(mem, f"r_prio{l}", [P, N_EXP])
        st = Stage()

        @st.gpsimd
        def _(pool):
            pool.iota(prio[:, :], pattern=[[-1, N_EXP]], base=N_EXP, channel_multiplier=0,
                      allow_small_or_imprecise_dtypes=True)

        @st.tensor
        def _(pe):
            for m in range(nt):
                for k in range(KT):
                    mm = pe.matmul(bank[m][:, 0:N_EXP], hT[:, k, m * P:(m + 1) * P], router_w[:, k, :],
                                   start=(k == 0), stop=(k == KT - 1))
            mm.then_inc(bank_full.sem, 1)

        @st.scalar
        def _(act):
            act.wait_ge(bank_full.sem, f0 + 1)
            for m in range(nt):
                act.activation(sc[:, m, :], bank[m][:, 0:N_EXP], ACT.Sigmoid)
        bank_full.n += 1
        st.end()
        st = Stage()

        @st.vector
        def _(dve):
            def bc(a, n):
                return a.unsqueeze(2).to_broadcast([P, a.shape[1], n])

            def first_hot(dst, values, top, n, groups):
                dve.tensor_tensor(dst, values, bc(top, n), ALU.is_equal)
                dve.drain()
                dve.tensor_tensor(dst, dst, prio[:, N_EXP - n:].unsqueeze(1).to_broadcast([P, groups, n]), ALU.mult)
                dve.drain()
                dve.tensor_reduce(top, dst, AX, ALU.max)
                dve.drain()
                dve.tensor_tensor(dst, dst, bc(top, n), ALU.is_equal)
                dve.drain()

            dve.tensor_tensor(sel[:, :, :], sc[:, :, :], router_b[:, :].unsqueeze(1).to_broadcast([P, nt, N_EXP]),
                              ALU.add)
            dve.drain()
            s4 = sel[:, :, :].rearrange("p m (g e) -> p (m g) e", e=EPG)
            for j, (a, b) in enumerate([(0, 1), (0, 2), (0, 3), (1, 2), (1, 3), (2, 3)]):
                dve.tensor_tensor(pair[:, :, j], s4[:, :, a], s4[:, :, b], ALU.add)
            dve.drain()
            dve.tensor_reduce(gs[:, :], pair[:, :, :], AX, ALU.max)
            dve.drain()
            g3 = gs[:, :].rearrange("p (m g) -> p m g", g=N_GROUPS)
            dve.tensor_reduce(best[:, :], g3, AX, ALU.max)
            dve.drain()
            hg = pair[:, :, 0].rearrange("p (m g) -> p m g", g=N_GROUPS)
            first_hot(hg, g3, best[:, :], N_GROUPS, nt)
            dve.tensor_scalar(gs[:, :], pair[:, :, 0], -1.0, BIG, ALU.add, ALU.mult)
            dve.drain()
            dve.tensor_tensor(s4, s4, bc(gs[:, :], EPG), ALU.add)
            dve.drain()
            dve.tensor_reduce(best[:, :], sel[:, :, :], AX, ALU.max)
            dve.drain()
            first_hot(hot[:, :, :], sel[:, :, :], best[:, :], N_EXP, nt)
            dve.scalar_tensor_tensor(sel[:, :, :], hot[:, :, :], -2 * BIG, sel[:, :, :], ALU.mult, ALU.add)
            dve.drain()
            dve.tensor_reduce(best[:, :], sel[:, :, :], AX, ALU.max)
            dve.drain()
            first_hot(hot2[:, :, :], sel[:, :, :], best[:, :], N_EXP, nt)
            dve.tensor_tensor(hot[:, :, :], hot[:, :, :], hot2[:, :, :], ALU.add)
            dve.drain()
            dve.tensor_tensor(sc[:, :, :], sc[:, :, :], hot[:, :, :], ALU.mult)
            dve.drain()
            dve.tensor_reduce(best[:, :], sc[:, :, :], AX, ALU.add)
            dve.drain()
            dve.reciprocal(gs[:, 0:nt], best[:, :])
            dve.drain()
            dve.tensor_tensor(comb[:, :, :].rearrange("p e m -> p m e"), sc[:, :, :], bc(gs[:, 0:nt], N_EXP),
                              ALU.mult)
        st.end()

    def even_mixer(gateb):
        with ExitStack() as mem:
            omix = sb(mem, "omix", [P, 4, D])
            proj_m = sb(mem, "proj_m", [P, 4, D_IN_EVEN - MQ])
            with ExitStack() as m2:
                proj_a = sb(m2, "proj_a", [P, 4, MQ])
                w = rows(A["even_w_in"][0])
                for dst, lo, hi in ((proj_m, MQ, D_IN_EVEN), (proj_a, 0, MQ)):
                    starts = list(range(lo, hi, COLS))
                    widths = [min(COLS, hi - c) for c in starts]

                    def evac(eng, c, i, b, dst=dst, widths=widths):
                        return eng.activation(dst[:, i, c * COLS:c * COLS + widths[c]], b[:, 0:widths[c]], ACT.Copy)
                    linear(lambda c, m, k: hT[:, k, m * P:(m + 1) * P], range(4),
                           [(KT, n, [(0, w[:, :, c:c + n])]) for c, n in zip(starts, widths)], evac, on="scalar")
                neighbourhood(m2, proj_a, omix)
            with ExitStack() as m2:
                mlstm(m2, proj_m, omix)
            project_out(omix, A["even_w_out"][0], list(range(4)), gateb, 0)

    def neighbourhood(mem, proj, omix):
        with ExitStack() as early:
            tmp = sb(early, "na_tmp", [P, 2, 1024])
            head_norm([proj[:, m, 0:1024].rearrange("p (n d) -> p n d", d=HD_A) for m in range(4)], HD_A, tmp)
        qT = sb(mem, "na_qT", [P, 4, 512])
        kT = sb(mem, "na_kT", [P, 4, 512])
        gain = sb(mem, "na_gain", [P, 2])
        flip = sb(mem, "na_flip", [P, P])
        window = sb(mem, "na_window", [P, GRID_W])
        bias = sb(mem, "na_bias", [P, LT, H_A, S_LAT])
        probs = sb(mem, "na_probs", [P, 2, 512])
        probsT = sb(mem, "na_probsT", [P, 2, 512])
        col = sb(mem, "na_col", [P, 3 + 1, 4])
        rpb = A["na_rpb"]
        n_r, n_c = 15, 31
        loads = [(gain[:, 0:1], A["na_q_gain"]), (gain[:, 1:2], A["na_k_gain"]), (window[:, :], A["window"])]
        for qr in range(ROWS):
            b = qr % 2
            for h in range(H_A):
                at = h * n_r * n_c + (7 - qr) * n_c + 15 - 63
                src = bass.AP(tensor=rpb.tensor, offset=at, ap=[[1, GRID_W], [n_c, ROWS], [1, GRID_W]])
                dst = bias[64 * b:64 * b + 64, qr // 2, h, :].rearrange("p (r c) -> p r c", c=GRID_W)
                loads.append((dst, src))
        load_small(loads)
        st = Stage()

        @st.gpsimd
        def _(pool):
            pool.memset(flip[:, :], 0.0)
            pool.drain()
            for b in range(2):
                pool.affine_select(out=flip[:, 64 * b:64 * b + 64], in_=flip[:, 64 * b:64 * b + 64],
                                   compare_op=ALU.not_equal, fill=1.0, base=-(64 * b + 63),
                                   pattern=[[1, 64]], channel_multiplier=1)

        @st.vector
        def _(dve):
            for t in range(LT):
                for h in range(H_A):
                    v = bias[:, t, h, :].rearrange("p (r c) -> p r c", c=GRID_W)
                    dve.tensor_tensor(v, v, window[:, :].unsqueeze(1).to_broadcast([P, ROWS, GRID_W]), ALU.add)

        @st.scalar
        def _(act):
            act.mul(gain[:, 0:1], gain[:, 0:1], HD_A ** -0.5)
        st.end()
        turn(lambda i, k: proj[:, i, AQ + k * P:AQ + (k + 1) * P], lambda k: qT[:, k, :], 4, 4,
             lambda k: [(0, 512, gain[:, 0:1], 0.0)])
        turn(lambda i, k: proj[:, i, AK + k * P:AK + (k + 1) * P], lambda k: kT[:, k, :], 4, 4,
             lambda k: [(0, 512, gain[:, 1:2], 0.0)])
        units = []
        for h in range(H_A):
            hp = slice(64 * (h % 2), 64 * (h % 2) + 64)
            for m in range(4):
                q = qT[hp, h // 2, m * P:(m + 1) * P]
                n = 512 if m >= CT else 256
                mms = [(q, kT[hp, h // 2, 0:n], 0, True, m < CT)]
                if m >= CT:
                    mms.append((flip[:, :], bias[:, m - CT, h, :], 256, False, True))
                units.append((mms, n, [proj[:, j, AV + h * HD_A:AV + (h + 1) * HD_A] for j in range(n // P)],
                              omix[:, m, h * HD_A:(h + 1) * HD_A]))
        attend(units, probs, probsT, col)

    def mlstm(mem, proj, omix):
        qT = sb(mem, "ml_qT", [P, 2, 512])
        kT = sb(mem, "ml_kT", [P, 2, 512])
        vaug = sb(mem, "ml_v", [P, 4, H_B, DV_B + 1])
        cap = sb(mem, "ml_cap", [P, 2, 4, 512], BF16)
        rev = sb(mem, "ml_rev", [P, P])
        gb = sb(mem, "ml_gb", [P, 16])
        g = sb(mem, "ml_g", [P, 4, 16])
        t1 = sb(mem, "ml_t1", [P, 4, 16])
        fw = sb(mem, "ml_fw", [P, 4, 2, 8])
        bw = sb(mem, "ml_bw", [P, 4, 2, 8])
        rowI = sb(mem, "ml_rowI", [8, 512])
        rowF = sb(mem, "ml_rowF", [8, 512])
        rowM = sb(mem, "ml_rowM", [8, 512])
        slotc = sb(mem, "ml_slotc", [P, 4, 3, 8])
        colc = sb(mem, "ml_colc", [P, 4, 3, 8])
        e_t = sb(mem, "ml_e", [P, 2, 512])
        w_t = sb(mem, "ml_w", [P, 2, 512])
        pT = sb(mem, "ml_pT", [P, 2, 4, 512])
        den = sb(mem, "ml_den", [P, 2, 4])
        ng = sb(mem, "ml_ng", [P, H_B * DV_B])
        turned_tile = [1, 0, 3, 2]
        turn(lambda i, k: proj[:, i, MQ0 + k * P:MQ0 + (k + 1) * P], lambda k: qT[:, k, :], 4, 2,
             lambda k: [(0, 512, DK_B ** -0.5, 0.0)])
        turn(lambda i, k: proj[:, i, MK0 + k * P:MK0 + (k + 1) * P], lambda k: kT[:, k, :], 4, 2)
        load_small([(gb[:, :], A["mlstm_gate_b"].to_broadcast([P, 16])),
                    (ng[:, :], A["mlstm_norm_g"].to_broadcast([P, H_B * DV_B]))])
        st = Stage()
        a0, d0, f0 = act_out.n, dve_out.n, bank_full.n

        @st.gpsimd
        def _(pool):
            pool.memset(rev[:, :], 0.0)
            pool.memset(cap[:, :, :, :], 0.0)
            pool.drain()
            pool.affine_select(out=rev[:, :], in_=rev[:, :], compare_op=ALU.not_equal, fill=1.0,
                               base=-(P - 1), pattern=[[1, P]], channel_multiplier=1)
            for j in range(4):
                c = cap[:, 0, j, :]
                pool.affine_select(out=c, in_=c, compare_op=ALU.is_ge, fill=BIG, base=-j * P,
                                   pattern=[[1, 512]], channel_multiplier=-1)
                lo = 256 * (j // 2)
                c = cap[:, 1, j, lo:lo + 256]
                pool.affine_select(out=c, in_=c, compare_op=ALU.is_ge, fill=BIG, base=j * P - lo,
                                   pattern=[[-1, 256]], channel_multiplier=1)
                if j >= 2:
                    pool.memset(cap[:, 1, j, 0:256], BIG)

        @st.vector
        def _(dve):
            for m in range(4):
                dve.tensor_copy(vaug[:, m, :, 0:DV_B],
                                proj[:, m, MV0:MV0 + H_B * DV_B].rearrange("p (h d) -> p h d", d=DV_B))
            dve.memset(vaug[:, :, :, DV_B:DV_B + 1], 1.0)
            dve.memset(fw[:, :, :, :], 0.0)
            dve.memset(bw[:, :, :, :], 0.0)
            dve.tensor_tensor(g[:, :, :], proj[:, :, MG0:MG0 + 16], gb[:, :].unsqueeze(1).to_broadcast([P, 4, 16]),
                              ALU.add)
            dve.drain()
            dve.tensor_scalar(t1[:, :, :], g[:, :, :], -1.0, None, ALU.mult)
            dve.drain()
            dve.tensor_tensor(t1[:, :, :], t1[:, :, :], g[:, :, :], ALU.max).then_inc(dve_out.sem, 1)
            dve.wait_ge(act_out.sem, a0 + 1)
            for dst, c in ((fw[:, :, 1, 0:4], 4), (bw[:, :, 1, 4:8], 12)):
                dve.scalar_tensor_tensor(dst, g[:, :, c:c + 4], 0.0, t1[:, :, c:c + 4], ALU.min, ALU.subtract)
            dve.tensor_copy(fw[:, :, 0, 0:4], g[:, :, 0:4])
            dve.tensor_copy(bw[:, :, 0, 4:8], g[:, :, 8:12])

        @st.scalar
        def _(act):
            act.wait_ge(dve_out.sem, d0 + 1)
            act.activation(t1[:, :, :], t1[:, :, :], ACT.Exp, scale=-1.0)
            act.drain()
            act.activation(t1[:, :, :], t1[:, :, :], ACT.Ln, bias=1.0).then_inc(act_out.sem, 1)
        act_out.n += 1
        dve_out.n += 1
        st.end()
        st = Stage()

        @st.tensor
        def _(pe):
            for q in range(2):
                for t in range(4):
                    dst = bank[q][0:8, t * P:(t + 1) * P]
                    pe.matmul(dst, fw[:, t, q, :], ident[:, :], start=True, stop=False)
                    mm = pe.matmul(dst, bw[:, turned_tile[t], q, :], rev[:, :], start=False, stop=True)
                mm.then_inc(bank_full.sem, 1)

        @st.vector
        def _(dve):
            dve.wait_ge(bank_full.sem, f0 + 2)
            dve.tensor_copy(rowF[:, :], bank[1][0:8, :])
            dve.memset(rowM[:, :], 1.0)
            dve.drain()
            dve.tensor_tensor_scan(rowI[:, :], rowM[:, :], rowF[:, :], 0.0, ALU.mult, ALU.add)
            dve.drain()
            dve.tensor_copy(rowF[:, :], rowI[:, :])
            dve.tensor_tensor(rowI[:, :], bank[0][0:8, :], rowI[:, :], ALU.subtract)
            dve.drain()
            dve.tensor_tensor_scan(rowM[:, :], rowI[:, :], rowI[:, :], -BIG, ALU.max, ALU.max)
            dve.drain()
            dve.tensor_tensor(rowF[:, :], rowF[:, :], rowM[:, :], ALU.add)
        bank_full.n += 2
        st.end()
        st = Stage()
        f0, d0 = bank_full.n, dve_out.n

        @st.tensor
        def _(pe):
            for t in range(4):
                for q, r in enumerate((rowI, rowM, rowF)):
                    mm = pe.transpose(bank[0][:, (t * 3 + q) * 8:(t * 3 + q) * 8 + 8], r[:, t * P:(t + 1) * P],
                                      ident[0:8, 0:8])
            mm.then_inc(bank_full.sem, 1)
            pe.wait_ge(dve_out.sem, d0 + 1)
            for t in range(4):
                mm = pe.matmul(bank[1][:, t * 24:(t + 1) * 24], rev[:, :],
                               slotc[:, turned_tile[t], :, :].rearrange("p q r -> p (q r)"),
                               start=True, stop=True)
            mm.then_inc(bank_full.sem, 1)

        @st.vector
        def _(dve):
            dve.wait_ge(bank_full.sem, f0 + 1)
            dve.tensor_copy(slotc[:, :, :, :].rearrange("p t q r -> p (t q r)"), bank[0][:, 0:96])\
                .then_inc(dve_out.sem, 1)
            dve.wait_ge(dve_out.sem, d0 + 1)
            dve.tensor_copy(colc[:, :, :, 0:4], slotc[:, :, :, 0:4])
            dve.wait_ge(bank_full.sem, f0 + 2)
            dve.tensor_copy(colc[:, :, :, 4:8],
                            bank[1][:, 0:96].rearrange("p (t q r) -> p t q r", t=4, q=3)[:, :, :, 4:8])
            dve.drain()
            dve.tensor_scalar(colc[:, :, 2, :], colc[:, :, 2, :], -1.0, None, ALU.mult).then_inc(dve_out.sem, 1)

        @st.scalar
        def _(act):
            act.wait_ge(dve_out.sem, d0 + 2)
            act.activation(colc[:, :, 2, :], colc[:, :, 2, :], ACT.Exp)
        bank_full.n += 2
        dve_out.n += 2
        st.end()
        st = Stage()
        s0, m0, p0, x0, v0, h0 = (scores_ready.n, max_ready.n, probs_ready.n, probsT_ready.n, pv_ready.n,
                                  head_stored.n)
        runs = [(h, r) for h in range(H_B) for r in range(2)]
        seen = {0: lambda j, i: i >= j, 1: lambda j, i: (i // 2 == j // 2 and j >= i) or i // 2 > j // 2}

        @st.tensor
        def _(pe):
            def values(n):
                h, r = runs[n]
                pe.wait_ge(probsT_ready.sem, x0 + 4 * n + 4)
                if n >= 1:
                    pe.wait_ge(head_stored.sem, h0 + n)
                for i in range(4):
                    js = [j for j in range(4) if seen[r](j, i)]
                    for j in js:
                        mm = pe.matmul(bank[6 + i // 2][:, (i % 2) * 129:(i % 2) * 129 + 129],
                                       pT[:, n % 2, j, i * P:(i + 1) * P], vaug[:, j, h, :],
                                       start=(j == js[0]), stop=(j == js[-1]))
                mm.then_inc(pv_ready.sem, 1)

            for n, (h, r) in enumerate(runs):
                hp = slice(64 * (h % 2), 64 * (h % 2) + 64)
                b = bank[n % 2]
                if n >= 2:
                    pe.wait_ge(probsT_ready.sem, x0 + 4 * (n - 1))
                for i in range(4):
                    mm = pe.matmul(b[:, i * P:(i + 1) * P], colc[:, i, 1, r * 4 + h:r * 4 + h + 1].to_broadcast([P, P]),
                                   ident[:, :], start=True, stop=True)
                mm.then_inc(max_ready.sem, 1)
                for j in range(4):
                    q = 4 * n + j
                    if q >= 4:
                        pe.wait_ge(probsT_ready.sem, x0 + q - 3)
                    pe.matmul(bank[2 + q % 4][:, :], kT[hp, h // 2, j * P:(j + 1) * P], qT[hp, h // 2, :],
                              start=True, stop=True).then_inc(scores_ready.sem, 1)
                if n >= 1:
                    values(n - 1)
            values(len(runs) - 1)

        @st.vector
        def _(dve):
            def weigh(n, j):
                h, r = runs[n]
                q = 4 * n + j
                if q >= 2:
                    dve.wait_ge(probs_ready.sem, p0 + q - 1)
                dve.scalar_tensor_tensor(e_t[:, q % 2, :], bank[n % 2][:, :], colc[:, j, 0, r * 4 + h:r * 4 + h + 1],
                                         cap[:, r, j, :], ALU.subtract, ALU.max).then_inc(dve_out.sem, 1)

            def apply(n, j):
                q = 4 * n + j
                dve.wait_ge(probs_ready.sem, p0 + q + 1)
                dve.wait_ge(scores_ready.sem, s0 + q + 1)
                if n >= 2:
                    dve.wait_ge(pv_ready.sem, v0 + n - 1)
                dve.tensor_tensor(pT[:, n % 2, j, :], bank[2 + q % 4][:, :], w_t[:, q % 2, :],
                                  ALU.mult).then_inc(probsT_ready.sem, 1)

            def finish(n):
                h, r = runs[n]
                dve.wait_ge(pv_ready.sem, v0 + n + 1)
                for half in range(2):
                    o = bank[6 + half][:, 0:258].rearrange("p (t d) -> p t d", t=2)
                    dve.tensor_scalar(den[:, 0, 2 * half:2 * half + 2], o[:, :, 128], -1.0, None, ALU.mult)
                    dve.drain()
                    dve.tensor_tensor(den[:, 0, 2 * half:2 * half + 2], den[:, 0, 2 * half:2 * half + 2],
                                      o[:, :, 128], ALU.max)
                dve.drain()
                dve.tensor_tensor(den[:, 0, :], den[:, 0, :], colc[:, :, 2, r * 4 + h], ALU.max)
                dve.drain()
                dve.reciprocal(den[:, 1, :], den[:, 0, :])
                dve.drain()
                for i in range(4):
                    o = bank[6 + i // 2][:, (i % 2) * 129:(i % 2) * 129 + 128]
                    dst = omix[:, i, 512 + h * DV_B:512 + (h + 1) * DV_B]
                    if r == 0:
                        ins = dve.tensor_scalar(dst, o, den[:, 1, i:i + 1], None, ALU.mult)
                    else:
                        ins = dve.scalar_tensor_tensor(dst, o, den[:, 1, i:i + 1], dst, ALU.mult, ALU.add)
                ins.then_inc(head_stored.sem, 1)
                dve.drain()

            for n in range(len(runs)):
                dve.wait_ge(max_ready.sem, m0 + n + 1)
                weigh(n, 0)
                for j in range(4):
                    if j < 3:
                        weigh(n, j + 1)
                    apply(n, j)
                if n >= 1:
                    finish(n - 1)
            finish(len(runs) - 1)
        e0 = dve_out.n

        @st.scalar
        def _(act):
            for n in range(len(runs)):
                for j in range(4):
                    q = 4 * n + j
                    act.wait_ge(dve_out.sem, e0 + q + 1)
                    if q >= 2:
                        act.wait_ge(probsT_ready.sem, x0 + q - 1)
                    act.activation(w_t[:, q % 2, :], e_t[:, q % 2, :], ACT.Exp, scale=-1.0)\
                        .then_inc(probs_ready.sem, 1)
        nr = len(runs)
        for sig, k in ((scores_ready, 4 * nr), (max_ready, nr), (probs_ready, 4 * nr), (probsT_ready, 4 * nr),
                       (pv_ready, nr), (head_stored, nr), (dve_out, 4 * nr)):
            sig.n += k
        st.end()
        hm = omix[:, :, 512:1024]
        head_norm([omix[:, m, 512:1024].rearrange("p (n d) -> p n d", d=DV_B) for m in range(4)], DV_B, e_t)
        st = Stage()
        a0 = act_out.n

        @st.scalar
        def _(act):
            for m in range(4):
                act.activation(proj[:, m, MO0:MO0 + 512], proj[:, m, MO0:MO0 + 512], ACT.Sigmoid)\
                    .then_inc(act_out.sem, 1)

        @st.vector
        def _(dve):
            dve.tensor_tensor(hm, hm, ng[:, :].unsqueeze(1).to_broadcast([P, 4, 512]), ALU.mult)
            dve.drain()
            for m in range(4):
                dve.wait_ge(act_out.sem, a0 + m + 1)
                dve.tensor_tensor(omix[:, m, 512:1024], omix[:, m, 512:1024], proj[:, m, MO0:MO0 + 512], ALU.mult)
        act_out.n += 4
        st.end()

    def odd_mixer(gateb):
        with ExitStack() as mem:
            nq = H_C * HD_C
            q = sb(mem, "gq", [P, LT, nq])
            kv = sb(mem, "gkv", [P, 4, 512])
            o = sb(mem, "go", [P, LT, D])
            w = rows(A["odd_w_in"][0])
            linear(lambda c, m, k: hT[:, k, m * P:(m + 1) * P], [2, 3],
                   [(KT, COLS, [(0, w[:, :, c * COLS:(c + 1) * COLS])]) for c in range(2)],
                   lambda eng, c, i, b: eng.activation(q[:, i, c * COLS:(c + 1) * COLS], b[:, :], ACT.Copy),
                   on="scalar")
            linear(lambda c, m, k: hT[:, k, m * P:(m + 1) * P], range(4), [(KT, COLS, [(0, w[:, :, nq:nq + COLS])])],
                   lambda eng, c, i, b: eng.activation(kv[:, i, :], b[:, :], ACT.Copy), on="scalar")
            gain = sb(mem, "g_gain", [P, 2, HD_C])
            rope = sb(mem, "g_rope", [P, LT, 2, HD_C // 2])
            tmp = sb(mem, "g_tmp", [P, 2, 1024])
            qT = sb(mem, "g_qT", [P, H_C, 256])
            kT = sb(mem, "g_kT", [P, KV_C, 512])
            probs = sb(mem, "g_probs", [P, 2, 512])
            probsT = sb(mem, "g_probsT", [P, 2, 512])
            col = sb(mem, "g_col", [P, 4, 4])
            load_small([(gain[:, 0, :], A["gqa_q_norm_g"].to_broadcast([P, HD_C])),
                        (gain[:, 1, :], A["gqa_k_norm_g"].to_broadcast([P, HD_C])),
                        (rope[:, :, :, :], A["rope_grid"])])
            qv = [q[:, i, :].rearrange("p (n d) -> p n d", d=HD_C) for i in range(LT)]
            kvv = [kv[:, i, 0:256].rearrange("p (n d) -> p n d", d=HD_C) for i in range(4)]
            head_norm(qv + kvv, HD_C, tmp)
            st = Stage()

            @st.vector
            def _(dve):
                for j, v in enumerate(qv + kvv):
                    gv = gain[:, int(j >= LT), :].unsqueeze(1).to_broadcast([P, v.shape[1], HD_C])
                    dve.scalar_tensor_tensor(v, v, HD_C ** -0.5 if j < LT else 1.0, gv, ALU.mult, ALU.mult)
                dve.drain()
                for v, i in [(qv[0], 0), (qv[1], 1), (kvv[2], 0), (kvv[3], 1)]:
                    n = v.shape[1]
                    pairs = v.rearrange("p n (f t) -> p n f t", t=2)
                    x0, x1 = pairs[:, :, :, 0], pairs[:, :, :, 1]
                    c = rope[:, i, 0, :].unsqueeze(1).to_broadcast([P, n, HD_C // 2])
                    s = rope[:, i, 1, :].unsqueeze(1).to_broadcast([P, n, HD_C // 2])
                    half = n * HD_C // 2
                    a, b = [tmp[:, 0, j * half:(j + 1) * half].rearrange("p (n f) -> p n f", n=n) for j in range(2)] \
                        if half <= 512 else [None, None]
                    e, f = [tmp[:, 1, j * half:(j + 1) * half].rearrange("p (n f) -> p n f", n=n) for j in range(2)]
                    dve.tensor_tensor(a, x0, c, ALU.mult)
                    dve.tensor_tensor(b, x1, s, ALU.mult)
                    dve.tensor_tensor(e, x0, s, ALU.mult)
                    dve.tensor_tensor(f, x1, c, ALU.mult)
                    dve.drain()
                    dve.tensor_tensor(x0, a, b, ALU.subtract)
                    dve.tensor_tensor(x1, e, f, ALU.add)
                    dve.drain()
            st.end()
            turn(lambda i, k: q[:, i, k * P:(k + 1) * P], lambda k: qT[:, k, :], LT, H_C)
            turn(lambda i, k: kv[:, i, k * P:(k + 1) * P], lambda k: kT[:, k, :], 4, KV_C)
            units = []
            for h in range(H_C):
                g = h // (H_C // KV_C)
                for i in range(LT):
                    units.append(([(qT[:, h, i * P:(i + 1) * P], kT[:, g, :], 0, True, True)], 512,
                                  [kv[:, j, 256 + g * HD_C:256 + (g + 1) * HD_C] for j in range(4)],
                                  o[:, i, h * HD_C:(h + 1) * HD_C]))
            attend(units, probs, probsT, col)
            project_out(o, A["odd_w_out"][0], [2, 3], gateb, 0)

    tiles2 = [2, 3]

    def hybrid(l):
        def tok(m):
            return slice((m - CT) * P, (m - CT + 1) * P)

        def hcol(c, m, k):
            return hT[:, k, tok(m)]
        w_in = rows(A["w_in_2"][l])
        with ExitStack() as lay:
            gcols = sb(lay, f"h_gcols{l}", [P, 2, KT])
            load_small([(gcols[:, 0, :], A["norm1_cols"][l]), (gcols[:, 1, :], A["norm2_cols"][l])])

            def normed(v):
                with ExitStack() as mem:
                    xn = sb(mem, f"h_xn{l}{v}", [P, LT, D])
                    normalise(tiles2, xn)
                    turn(lambda i, k: xn[:, i, k * P:(k + 1) * P], lambda k: hT[:, k, 0:256], LT, KT,
                         lambda k: [(0, 256, gcols[:, v, k:k + 1], 0.0)])
            normed(0)
            with ExitStack() as mix:
                conf = sb(mix, f"h_conf{l}", [P, KT, S_LAT])
                sc = sb(mix, f"h_sc{l}", [P, KT, S_LAT])
                qkv = sb(mix, f"h_qkv{l}", [P, LT, QKV2])
                gates = sb(mix, f"h_gates{l}", [P, LT, 3 * D], F32)
                merged = sb(mix, f"h_merged{l}", [P, LT, D])
                with ExitStack() as cv:
                    convolutions(l, cv, w_in, conf, sc, qkv, gates, hcol)
                branch_out(l, merged, gates, 0, lambda c, m, k: conf[:, k, tok(m)], A["w_conf_out_2"][l], True)
                branch_out(l, merged, gates, 2, lambda c, m, k: sc[:, k, tok(m)], A["w_sc_out_2"][l], False)
                with ExitStack() as at:
                    o = sb(at, f"h_o{l}", [P, LT, D])
                    with ExitStack() as at2:
                        sparse_attention(l, at2, qkv, o)
                    turn(lambda i, k: o[:, i, k * P:(k + 1) * P], lambda k: hT[:, k, 0:256], LT, KT)
                branch_out(l, merged, gates, 1, hcol, A["w_attn_out_2"][l], False)
                project_out(merged, A["w_o_2"][l], tiles2, None, 0)
            normed(1)
            feed_forward(l)

    def branch_out(l, merged, gates, g, lhs, w, first):
        with ExitStack() as mem:
            tmp = sb(mem, f"bo{l}{g}", [P, 2, COLS])

            def evac(eng, c, i, b):
                cols = slice(c * COLS, (c + 1) * COLS)
                gv = gates[:, i, g * D + c * COLS:g * D + (c + 1) * COLS]
                if first:
                    return eng.tensor_tensor(merged[:, i, cols], b[:, :], gv, ALU.mult)
                eng.drain()
                eng.tensor_tensor(tmp[:, i, :], b[:, :], gv, ALU.mult)
                eng.drain()
                return eng.tensor_tensor(merged[:, i, cols], tmp[:, i, :], merged[:, i, cols], ALU.add)
            linear(lhs, tiles2, [(KT, COLS, [(0, rows(w)[:, :, c * COLS:(c + 1) * COLS])]) for c in range(2)], evac)

    def feature_products(parts, evac_act, evac_dve):
        f0, n0, fa, fd = bank_full.n, chunks[0], bank_free_act.n, bank_free_dve.n
        for c in range(len(parts)):
            used_at[n0 + c] = (bank_full, f0 + c + 1)
        stream(parts)
        st = Stage()

        @st.tensor
        def _(pe):
            for c in range(len(parts)):
                if c >= 4:
                    pe.wait_ge(bank_free_act.sem, fa + c - 3)
                    pe.wait_ge(bank_free_dve.sem, fd + c - 3)
                arrived(pe, n0 + c)
                wt = chunk(n0 + c)[:, :].rearrange("p (k n) -> p k n", k=KT)
                for j in range(4):
                    b = bank[2 * (c % 4) + j // 2]
                    for k in range(KT):
                        mm = pe.matmul(b[:, (j % 2) * 256:(j % 2) * 256 + 256], wt[:, k, j * P:(j + 1) * P],
                                       hT[:, k, 0:256], start=(k == 0), stop=(k == KT - 1))
                mm.then_inc(bank_full.sem, 1)

        @st.scalar
        def _(act):
            for c in range(len(parts)):
                act.wait_ge(bank_full.sem, f0 + c + 1)
                evac_act(act, c, [bank[2 * (c % 4)], bank[2 * (c % 4) + 1]]).then_inc(bank_free_act.sem, 1)

        @st.vector
        def _(dve):
            for c in range(len(parts)):
                dve.wait_ge(bank_full.sem, f0 + c + 1)
                evac_dve(dve, c, [bank[2 * (c % 4)], bank[2 * (c % 4) + 1]], fa).then_inc(bank_free_dve.sem, 1)
        for sig in (bank_full, bank_free_act, bank_free_dve):
            sig.n += len(parts)
        st.end()

    def convolutions(l, mem, w_in, conf, sc, qkv, gates, hcol):
        PAD = 32
        glu = sb(mem, f"c_glu{l}", [P, KT, PAD + S_LAT])
        cx = sb(mem, f"c_cx{l}", [P, KT, 2 + S_LAT])
        tmp = sb(mem, f"c_tmp{l}", [P, 3, 2, COLS])
        cw = sb(mem, f"c_cw{l}", [P, KT, CONF_K])
        sw = sb(mem, f"c_sw{l}", [P, KT, SC_K])
        vec = sb(mem, f"c_vec{l}", [P, 3, KT])
        load_small([(cw[:, :, :], A["conf_w"][l]), (sw[:, :, :], A["sc_w"][l])]
                   + [(vec[:, j, :], A[n][l]) for j, n in enumerate(("conf_b", "ln_g", "ln_b"))])
        st = Stage()

        @st.gpsimd
        def _(pool):
            pool.memset(glu[:, :, 0:PAD], 0.0)
            pool.memset(cx[:, :, 0:2], 0.0)
        st.end()

        def two(a, b, t):
            return [(0, w_in[:, :, a + t * 256:a + (t + 1) * 256]), (256, w_in[:, :, b + t * 256:b + (t + 1) * 256])]
        parts = [two(A2, A2 + D, t) for t in range(4)] + [two(C2 + D, C2 + 2 * D, t) for t in range(4)] \
            + [[(0, w_in[:, :, C2 + t * COLS:C2 + (t + 1) * COLS])] for t in range(2)]

        fd0 = bank_free_dve.n

        def evac_act(act, c, b):
            if 3 <= c < 8:
                act.wait_ge(bank_free_dve.sem, fd0 + c - 2)
            if c < 4:
                return act.activation(tmp[:, c % 3, 0, :], b[1][:, :], ACT.Sigmoid)
            if c < 8:
                return act.activation(tmp[:, c % 3, 0, :], b[1][:, :], ACT.Copy)
            f = 4 * (c - 8)
            act.activation(sc[:, f:f + 2, :].rearrange("p f t -> p (f t)"), b[0][:, :], ACT.Copy)
            return act.activation(sc[:, f + 2:f + 4, :].rearrange("p f t -> p (f t)"), b[1][:, :], ACT.Copy)

        def evac_dve(dve, c, b, fa):
            dve.wait_ge(bank_free_act.sem, fa + c + 1)
            if c >= 8:
                return dve.memset(tmp[:, c % 3, 1, 0:1], 0.0)
            dst, pad = (glu, PAD) if c < 4 else (cx, 2)
            f = 2 * (c % 4)
            return dve.tensor_tensor(dst[:, f:f + 2, pad:pad + S_LAT],
                                     b[0][:, :].rearrange("p (f t) -> p f t", f=2),
                                     tmp[:, c % 3, 0, :].rearrange("p (f t) -> p f t", f=2), ALU.mult)
        feature_products(parts, evac_act, evac_dve)

        widths = [COLS] * 4 + [QKV2 - 4 * COLS] + [COLS] * 6

        def evac(act, c, i, b):
            if c < 5:
                return act.activation(qkv[:, i, c * COLS:c * COLS + widths[c]], b[:, 0:widths[c]], ACT.Copy)
            return act.activation(gates[:, i, (c - 5) * COLS:(c - 4) * COLS], b[:, :], ACT.Sigmoid)

        def conv(dve):
            for f in range(0, KT, 2):
                accs = [tmp[:, j, 0, 0:S_LAT] for j in range(2)]
                for k in range(SC_K):
                    for j in range(2):
                        src = cx[:, f + j, k:k + S_LAT]
                        if k == 0:
                            dve.tensor_scalar(accs[j], src, sw[:, f + j, 0:1], None, ALU.mult)
                        else:
                            dve.scalar_tensor_tensor(accs[j], src, sw[:, f + j, k:k + 1], accs[j],
                                                     ALU.mult, ALU.add)
                    dve.drain()
                for j in range(2):
                    dve.tensor_tensor(sc[:, f + j, :], sc[:, f + j, :], accs[j], ALU.mult)
                dve.drain()
            for k in range(CONF_K):
                for f in range(KT):
                    src = glu[:, f, PAD - (CONF_K - 1) + k:PAD - (CONF_K - 1) + k + S_LAT]
                    if k == 0:
                        dve.tensor_scalar(conf[:, f, :], src, cw[:, f, 0:1], vec[:, 0, f:f + 1], ALU.mult, ALU.add)
                    else:
                        dve.scalar_tensor_tensor(conf[:, f, :], src, cw[:, f, k:k + 1], conf[:, f, :],
                                                 ALU.mult, ALU.add)
                dve.drain()
        linear(hcol, tiles2,
               [(KT, widths[c], [(0, w_in[:, :, (c * COLS if c < 5 else G2 + (c - 5) * COLS):
                                          (c * COLS if c < 5 else G2 + (c - 5) * COLS) + widths[c]])])
                for c in range(11)], evac, on="scalar", side=conv)

        sq = glu[:, :, 0:S_LAT]
        mean, var = tmp[:, 0, 0, 0:S_LAT], tmp[:, 1, 0, 0:S_LAT]
        st = Stage()
        a0, f0, d0 = act_out.n, bank_full.n, dve_out.n

        @st.scalar
        def _(act):
            for f in range(KT):
                act.activation(sq[:, f, :], conf[:, f, :], ACT.Square).then_inc(act_out.sem, 1)
            act.wait_ge(dve_out.sem, d0 + 1)
            act.activation(var, var, ACT.Sqrt, bias=eps_col[:, :]).then_inc(act_out.sem, 1)
            for f in range(KT):
                act.wait_ge(dve_out.sem, d0 + 2 + f)
                act.activation(conf[:, f, :], conf[:, f, :], ACT.Silu, scale=vec[:, 1, f:f + 1],
                               bias=vec[:, 2, f:f + 1])

        @st.tensor
        def _(pe):
            for f in range(KT):
                pe.matmul(bank[0][:, 0:S_LAT], ones[:, :], conf[:, f, :], start=(f == 0), stop=(f == KT - 1))
            for f in range(KT):
                pe.wait_ge(act_out.sem, a0 + f + 1)
                mm = pe.matmul(bank[1][:, 0:S_LAT], ones[:, :], sq[:, f, :], start=(f == 0), stop=(f == KT - 1))
            mm.then_inc(bank_full.sem, 1)

        @st.vector
        def _(dve):
            dve.wait_ge(bank_full.sem, f0 + 1)
            dve.tensor_scalar(mean, bank[0][:, 0:S_LAT], 1.0 / D, None, ALU.mult)
            dve.drain()
            dve.tensor_tensor(var, mean, mean, ALU.mult)
            dve.drain()
            dve.scalar_tensor_tensor(var, bank[1][:, 0:S_LAT], 1.0 / D, var, ALU.mult, ALU.subtract)
            dve.drain()
            dve.tensor_scalar(var, var, 0.0, None, ALU.max).then_inc(dve_out.sem, 1)
            dve.wait_ge(act_out.sem, a0 + KT + 1)
            dve.reciprocal(var, var)
            for f in range(KT):
                dve.tensor_tensor(conf[:, f, :], conf[:, f, :], mean, ALU.subtract)
            dve.drain()
            for f in range(KT):
                dve.tensor_tensor(conf[:, f, :], conf[:, f, :], var, ALU.mult).then_inc(dve_out.sem, 1)
        act_out.n += KT + 1
        bank_full.n += 1
        dve_out.n += KT + 1
        st.end()

    def sparse_attention(l, mem, qkv, o):
        gain = sb(mem, f"s_gain{l}", [P, 2, HD_C])
        rope = sb(mem, f"s_rope{l}", [P, LT, 2, 16])
        ropei = sb(mem, f"s_ropei{l}", [P, LT, 2, 8])
        causal = sb(mem, f"s_causal{l}", [P, LT, S_LAT])
        tmp = sb(mem, f"s_tmp{l}", [P, 2, 1280])
        ik2 = sb(mem, f"s_ik{l}", [P, LT, P])
        qT = sb(mem, f"s_qT{l}", [P, 8, 256])
        kT = sb(mem, f"s_kT{l}", [P, 2, 256])
        iqT = sb(mem, f"s_iqT{l}", [P, 4, 256])
        ikT = sb(mem, f"s_ikT{l}", [P, 1, 256])
        score = sb(mem, f"s_score{l}", [P, LT, S_LAT])
        mask = sb(mem, f"s_mask{l}", [P, LT, S_LAT])
        rel = sb(mem, f"s_rel{l}", [P, 4, S_LAT])
        top = sb(mem, f"s_top{l}", [P, LT, 8])
        probs = sb(mem, f"s_probs{l}", [P, 2, 256])
        probsT = sb(mem, f"s_probsT{l}", [P, 2, 256])
        col = sb(mem, f"s_col{l}", [P, 4, 4])
        load_small([(gain[:, 0, :], A["q_norm_g_2"][l:l + 1, :].to_broadcast([P, HD_C])),
                    (gain[:, 1, :], A["k_norm_g_2"][l:l + 1, :].to_broadcast([P, HD_C])),
                    (rope[:, :, :, :], A["rope_seq"]), (ropei[:, :, :, :], A["rope_idx"]),
                    (causal[:, :, :], A["causal"])])
        qk = [qkv[:, i, 0:1280].rearrange("p (n d) -> p n d", d=HD_C) for i in range(LT)]
        head_norm(qk, HD_C, tmp)
        st = Stage()

        @st.vector
        def _(dve):
            for i in range(LT):
                for lo, hi, g, s in ((0, 8, 0, HD_C ** -0.5), (8, 10, 1, 1.0)):
                    v = qk[i][:, lo:hi, :]
                    dve.scalar_tensor_tensor(v, v, s, gain[:, g, :].unsqueeze(1).to_broadcast([P, hi - lo, HD_C]),
                                             ALU.mult, ALU.mult)
            dve.drain()
            for i in range(LT):
                idx = qkv[:, i, IQ2:IQ2 + 9 * IDX_D].rearrange("p (n d) -> p n d", d=IDX_D)
                for v, table, n, half in ((qk[i], rope, 10, 16), (idx, ropei, 9, 8)):
                    x1, x2 = v[:, :, 0:half], v[:, :, half:2 * half]
                    c = table[:, i, 0, :].unsqueeze(1).to_broadcast([P, n, half])
                    s = table[:, i, 1, :].unsqueeze(1).to_broadcast([P, n, half])
                    a, b, e, f = [tmp[:, i, j * 160:j * 160 + n * half].rearrange("p (n f) -> p n f", n=n)
                                  for j in range(4)]
                    dve.tensor_tensor(a, x1, c, ALU.mult)
                    dve.tensor_tensor(b, x2, s, ALU.mult)
                    dve.tensor_tensor(e, x2, c, ALU.mult)
                    dve.tensor_tensor(f, x1, s, ALU.mult)
                    dve.drain()
                    dve.tensor_tensor(x1, a, b, ALU.subtract)
                    dve.tensor_tensor(x2, e, f, ALU.add)
                    dve.drain()
                for r in range(2):
                    dve.tensor_copy(ik2[:, i, r * IDX_D:(r + 1) * IDX_D], qkv[:, i, IK2:IK2 + IDX_D])
                iw = qkv[:, i, IW2:IW2 + IDX_H]
                dve.tensor_scalar(iw, iw, IDX_H ** -0.5 * IDX_D ** -0.5, None, ALU.mult)
        st.end()
        turn(lambda i, k: qkv[:, i, k * P:(k + 1) * P], lambda k: qT[:, k, :], LT, 8)
        turn(lambda i, k: qkv[:, i, K2 + k * P:K2 + (k + 1) * P], lambda k: kT[:, k, :], LT, 2)
        turn(lambda i, k: qkv[:, i, IQ2 + k * P:IQ2 + (k + 1) * P], lambda k: iqT[:, k, :], LT, 4)
        turn(lambda i, k: ik2[:, i, :], lambda k: ikT[:, k, :], LT, 1)
        st = Stage()
        f0, a0, d0 = bank_full.n, act_out.n, dve_out.n
        jobs = [(i, h) for h in range(IDX_H) for i in range(LT)]

        @st.tensor
        def _(pe):
            for n, (i, h) in enumerate(jobs):
                if n >= 8:
                    pe.wait_ge(act_out.sem, a0 + n - 7)
                hp = slice(64 * (h % 2), 64 * (h % 2) + 64)
                pe.matmul(bank[n % 8][:, 0:S_LAT], iqT[hp, h // 2, i * P:(i + 1) * P], ikT[hp, 0, :],
                          start=True, stop=True).then_inc(bank_full.sem, 1)

        @st.scalar
        def _(act):
            for n, (i, h) in enumerate(jobs):
                act.wait_ge(bank_full.sem, f0 + n + 1)
                if n >= 4:
                    act.wait_ge(dve_out.sem, d0 + n - 3)
                act.activation(rel[:, n % 4, :], bank[n % 8][:, 0:S_LAT], ACT.Relu).then_inc(act_out.sem, 1)

        @st.vector
        def _(dve):
            for n, (i, h) in enumerate(jobs):
                dve.wait_ge(act_out.sem, a0 + n + 1)
                iw = qkv[:, i, IW2 + h:IW2 + h + 1]
                if h == 0:
                    ins = dve.tensor_scalar(score[:, i, :], rel[:, n % 4, :], iw, None, ALU.mult)
                else:
                    ins = dve.scalar_tensor_tensor(score[:, i, :], rel[:, n % 4, :], iw, score[:, i, :],
                                                   ALU.mult, ALU.add)
                ins.then_inc(dve_out.sem, 1)
                if i == LT - 1:
                    dve.drain()
            for i in range(LT):
                dve.scalar_tensor_tensor(score[:, i, :], causal[:, i, :], 3e8, score[:, i, :], ALU.mult, ALU.add)
            dve.drain()
            for _ in range(TOPK // 8):
                for i in range(LT):
                    dve.max(top[:, i, :], score[:, i, :])
                dve.drain()
                for i in range(LT):
                    dve.match_replace(score[:, i, :], top[:, i, :], score[:, i, :], -3.3e38)
                dve.drain()
            for i in range(LT):
                dve.tensor_scalar(mask[:, i, :], score[:, i, :], -3.2e38, -BIG, ALU.is_gt, ALU.mult)
            dve.drain()
            for i in range(LT):
                dve.tensor_tensor(mask[:, i, :], mask[:, i, :], causal[:, i, :], ALU.add)
        bank_full.n += len(jobs)
        act_out.n += len(jobs)
        dve_out.n += len(jobs)
        st.end()
        units = []
        for h in range(8):
            g = h // 4
            for i in range(LT):
                n = (i + 1) * P
                units.append(([(qT[:, h, i * P:(i + 1) * P], kT[:, g, 0:n], 0, True, False),
                               (ident[:, :], mask[:, i, 0:n], 0, False, True)], n,
                              [qkv[:, j, V2 + g * HD_C:V2 + (g + 1) * HD_C] for j in range(n // P)],
                              o[:, i, h * HD_C:(h + 1) * HD_C]))
        attend(units, probs, probsT, col)

    def feed_forward(l):
        w_up = rows(A["w_up_2"][l])
        with ExitStack() as mem:
            hid = sb(mem, f"f_hid{l}", [P, FT, S_LAT])
            acc = sb(mem, f"f_acc{l}", [P, 2, 4, S_LAT])
            cw = sb(mem, f"f_cw{l}", [P, 2 * FT, 3])
            cb = sb(mem, f"f_cb{l}", [P, 2 * FT])
            load_small([(cw[:, :, :], A["ffn_w"][l]), (cb[:, :], A["ffn_b"][l])])
            n_c = FT // 2
            parts = [[(0, w_up[:, :, c * 256:(c + 1) * 256]), (256, w_up[:, :, FFN + c * 256:FFN + (c + 1) * 256])]
                     for c in range(n_c)]
            s0, h0 = moe_silu.n, moe_hidden.n

            def tile_of(c, j):
                return 2 * c + j if j < 2 else FT + 2 * c + j - 2

            def evac_act(act, c, b):
                if c >= 2:
                    act.wait_ge(bank_free_dve.sem, fd0 + c - 1)
                for j in range(4):
                    t = tile_of(c, j)
                    ins = act.activation(acc[:, c % 2, j, :], b[j // 2][:, (j % 2) * 256:(j % 2) * 256 + 256],
                                         ACT.Identity, scale=cw[:, t, 2:3], bias=cb[:, t:t + 1])
                return ins

            def evac_dve(dve, c, b, fa):
                dve.wait_ge(bank_free_act.sem, fa + c + 1)
                for k, sh in ((1, 1), (0, 2)):
                    for j in range(4):
                        a = acc[:, c % 2, j, sh:S_LAT]
                        lo = (j % 2) * 256
                        ins = dve.scalar_tensor_tensor(a, b[j // 2][:, lo:lo + S_LAT - sh],
                                                       cw[:, tile_of(c, j), k:k + 1], a, ALU.mult, ALU.add)
                    if k == 0:
                        ins.then_inc(dve_out.sem, 1)
                    else:
                        dve.drain()
                dve.wait_ge(moe_silu.sem, s0 + c + 1)
                return dve.tensor_tensor(hid[:, 2 * c:2 * c + 2, :], acc[:, c % 2, 0:2, :], acc[:, c % 2, 2:4, :],
                                         ALU.mult)

            fd0, d0 = bank_free_dve.n, dve_out.n
            feature_products_ffn(parts, evac_act, evac_dve, acc, s0, d0)
            w_down = rows(A["w_down_2"][l])
            split = [(0, 8), (8, 8), (16, 6)]

            def evac(eng, c, i, b):
                cols = slice(c * COLS, (c + 1) * COLS)
                return eng.tensor_tensor(x[:, tiles2[i], cols], b[:, :], x[:, tiles2[i], cols], ALU.add)
            linear(lambda c, m, k: hid[:, split[c % 3][0] + k, (m - CT) * P:(m - CT + 1) * P], tiles2,
                   [(kn, COLS, [(0, w_down[:, k0:k0 + kn, c * COLS:(c + 1) * COLS])])
                    for c in range(2) for k0, kn in split], evac, accumulate=3)

    def feature_products_ffn(parts, evac_act, evac_dve, acc, s0, d0):
        f0, n0, fa, fd = bank_full.n, chunks[0], bank_free_act.n, bank_free_dve.n
        for c in range(len(parts)):
            used_at[n0 + c] = (bank_full, f0 + c + 1)
        stream(parts)
        st = Stage()

        @st.tensor
        def _(pe):
            for c in range(len(parts)):
                if c >= 4:
                    pe.wait_ge(bank_free_dve.sem, fd + c - 3)
                arrived(pe, n0 + c)
                wt = chunk(n0 + c)[:, :].rearrange("p (k n) -> p k n", k=KT)
                for j in range(4):
                    b = bank[2 * (c % 4) + j // 2]
                    for k in range(KT):
                        mm = pe.matmul(b[:, (j % 2) * 256:(j % 2) * 256 + 256], wt[:, k, j * P:(j + 1) * P],
                                       hT[:, k, 0:256], start=(k == 0), stop=(k == KT - 1))
                mm.then_inc(bank_full.sem, 1)

        @st.scalar
        def _(act):
            for c in range(len(parts) + 1):
                if c < len(parts):
                    act.wait_ge(bank_full.sem, f0 + c + 1)
                    evac_act(act, c, [bank[2 * (c % 4)], bank[2 * (c % 4) + 1]]).then_inc(bank_free_act.sem, 1)
                if c >= 1:
                    act.wait_ge(dve_out.sem, d0 + c)
                    g = acc[:, (c - 1) % 2, 0:2, :]
                    act.activation(g, g, ACT.Silu).then_inc(moe_silu.sem, 1)

        @st.vector
        def _(dve):
            for c in range(len(parts)):
                dve.wait_ge(bank_full.sem, f0 + c + 1)
                evac_dve(dve, c, [bank[2 * (c % 4)], bank[2 * (c % 4) + 1]], fa).then_inc(bank_free_dve.sem, 1)
        for sig in (bank_full, bank_free_act, bank_free_dve, dve_out, moe_silu):
            sig.n += len(parts)
        st.end()

    def first_layer(l):
        with ExitStack() as mem:
            modc = sb(mem, f"modc{l}", [P, 4 * KT, 2])
            gateb = sb(mem, f"gateb{l}", [P, 2, 2, D])
            gcols = sb(mem, f"gcols{l}", [P, 2, KT])
            ada(l, modc, gateb, gcols)
            modulated(modc, 0, list(range(4)))
            if upto == f"mod{l}":
                return
            (even_mixer, odd_mixer)[l](gateb)
            if upto == f"mix{l}":
                return
            tiles = list(range(4)) if l == 0 else [2, 3]
            modulated(modc, 1, tiles)
            moe(l, tiles, gateb)

    def program():
        for l in range(2):
            first_layer(l)
            if upto in (f"mod{l}", f"mix{l}", f"moe{l}"):
                return
        for l in range(2):
            hybrid(l)
            if upto == f"hyb{l}":
                return
    program()

    @block.sync
    def _(sp):
        sp.wait_ge(stage_done.sem, stage_done.n)
        sp.dma_start(out[0].rearrange("(m p) d -> p m d", p=P), x[:, 2:4, :]).then_inc(out_landed.sem, 16)
        if upto:
            sp.dma_start(upto_out.rearrange("(m p) d -> p m d", p=P), x[:, 0:2, :]).then_inc(out_landed.sem, 16)
            sp.wait_ge(out_landed.sem, 32)
        else:
            sp.wait_ge(out_landed.sem, 16)
    ctx.close()


def constants():
    c = {}
    qc, kc = np.arange(GRID_W)[:, None], np.arange(GRID_W)[None, :]
    start = np.clip(qc - 8, 0, GRID_W - 16)
    win = np.where((kc >= start) & (kc < start + 16), 0.0, -BIG).astype(np.float32)
    c["window"] = np.concatenate([win[::-1], win[::-1]])
    t = np.arange(S_LAT)
    inv = (10000.0 ** (-np.arange(32, dtype=np.float32) / np.float32(32))).astype(np.float32)
    ang = np.concatenate([(t // GRID_W).astype(np.float32)[:, None] * inv,
                          (t % GRID_W).astype(np.float32)[:, None] * inv], axis=-1).astype(np.float32)

    def table(a):
        cs = np.stack([np.cos(a), np.sin(a)], axis=1).astype(np.float32)
        return np.ascontiguousarray(cs.reshape(LT, P, 2, -1).transpose(1, 0, 2, 3))
    c["rope_grid"] = table(ang)
    for name, rot in (("rope_seq", 32), ("rope_idx", 16)):
        inv = np.power(np.float32(500000.0), -np.arange(0, rot, 2, dtype=np.float32) / np.float32(rot))
        c[name] = table(t.astype(np.float32)[:, None] * inv.astype(np.float32)[None, :])
    mask = np.where(t[None, :] <= t[:, None], 0.0, -BIG).astype(np.float32)
    c["causal"] = np.ascontiguousarray(mask.reshape(LT, P, S_LAT).transpose(1, 0, 2))
    return c


def layouts(i):
    a = {n: i[n] for n in ("x", "ctx", "ada_w", "ada_b", "even_w_in", "even_w_out", "na_rpb", "mlstm_gate_b",
                           "mlstm_norm_g", "odd_w_in", "odd_w_out", "gqa_q_norm_g", "gqa_k_norm_g", "router_w",
                           "router_b", "exp_w1", "exp_w3", "exp_w2", "w_in_2", "q_norm_g_2", "k_norm_g_2",
                           "w_attn_out_2", "w_conf_out_2", "w_sc_out_2", "w_o_2", "w_up_2", "w_down_2")}

    def cols(v):
        return v.reshape(v.shape[0], -1, P).transpose(0, 2, 1)

    def taps(v):
        return v.reshape(v.shape[0], v.shape[1], -1, P).transpose(0, 3, 2, 1)
    a["cond"] = np.stack([i["c"][0].reshape(KT, P).T, i["c_ctx"].reshape(KT, P).T], axis=-1)
    a["norm_mix_cols"], a["norm_ffn_cols"] = cols(i["norm_mix_g"]), cols(i["norm_ffn_g"])
    a["norm1_cols"], a["norm2_cols"] = cols(i["norm1_g_2"]), cols(i["norm2_g_2"])
    a["na_q_gain"] = np.tile(i["na_q_norm_g"][0], 2)[:, None]
    a["na_k_gain"] = np.tile(i["na_k_norm_g"][0], 2)[:, None]
    a["conf_w"], a["sc_w"], a["ffn_w"] = taps(i["conf_conv_w_2"]), taps(i["sc_conv_w_2"]), taps(i["ffn_conv_w_2"])
    a["conf_b"], a["ln_g"], a["ln_b"] = cols(i["conf_conv_b_2"]), cols(i["conf_ln_g_2"]), cols(i["conf_ln_b_2"])
    a["ffn_b"] = cols(i["ffn_conv_b_2"])
    a.update(constants())
    return {n: np.ascontiguousarray(v) for n, v in a.items()}


upto_out = None


def kernel(**inputs):
    from concourse import bacc
    from concourse.bass_utils import run_bass_kernel_spmd

    nc = bacc.Bacc("TRN2", target_bir_lowering=False, num_devices=1)
    arrays, A = {}, {}
    for name, a in layouts({n: np.asarray(v) for n, v in inputs.items()}).items():
        arrays[f"in_{name}"] = a
        A[name] = nc.dram_tensor(f"in_{name}", a.shape, mybir.dt.from_np(a.dtype), kind="ExternalInput").ap()
    out = nc.dram_tensor("out_x", (1, S_LAT, D), F32, kind="ExternalOutput").ap()
    build(nc, A, out)
    r = run_bass_kernel_spmd(nc, [arrays], core_ids=[0])
    return r.results[0]["out_x"]
```

```python
from contextlib import ExitStack

import numpy as np
import concourse.bass as bass
from concourse import mybir

F32 = mybir.dt.float32
BF16 = mybir.dt.bfloat16
ALU = mybir.AluOpType
ACT = mybir.ActivationFunctionType
AX = mybir.AxisListType.X

P = 128
D = 1024
KT = D // P
RING = 3
COLS = 512
EPS = 1e-6
BIG = 1e30

S_LAT = 256
S_CTX = 256
LT = S_LAT // P
CT = S_CTX // P
GRID_W = 64
ROWS = S_LAT // GRID_W
H_A, HD_A = 8, 64
H_B, DK_B, DV_B = 4, 64, 128
D_IN_EVEN = 3 * H_A * HD_A + 2 * H_B * DK_B + 2 * H_B * DV_B + 4 * H_B
AQ, AK, AV = 0, 512, 1024
MQ, MK, MV, MO, MG = 1536, 1792, 2048, 2560, 3072
MQ0, MK0, MV0, MO0, MG0 = 0, MK - MQ, MV - MQ, MO - MQ, MG - MQ
H_C, KV_C, HD_C = 8, 2, 128
N_EXP, N_GROUPS, EPG = 16, 4, 4
D_FF = 512
FFN = 2816
FT = FFN // P
CONF_K, SC_K = 31, 3
IDX_H, IDX_D = 8, 64
TOPK = 64
N_IN2 = 10312
Q2, K2, V2, IQ2, IK2, IW2, A2, C2, G2 = 0, 1024, 1280, 1536, 2048, 2112, 2120, 4168, 7240
QKV2 = A2


class Signal:

    def __init__(self, sem):
        self.sem = sem
        self.n = 0


def build(nc, A, out, upto=None):
    ctx = ExitStack()
    serial = [0]

    def sb(stack, name, shape, dt=F32):
        serial[0] += 1
        return stack.enter_context(nc.sbuf_tensor(name, shape, dt))

    def signal(name):
        return Signal(ctx.enter_context(nc.semaphore(name)))

    bank = [ctx.enter_context(nc.psum_tensor(f"bank{i}", [P, COLS], F32)) for i in range(8)]

    ring = [sb(ctx, f"ring{i}", [P, KT * COLS]) for i in range(RING)]
    x = sb(ctx, "x", [P, 4, D])
    hT = sb(ctx, "hT", [P, KT, 512])
    ident = sb(ctx, "ident", [P, P])
    ones = sb(ctx, "ones", [P, P])
    eps_col = sb(ctx, "eps_col", [P, 1])
    stats = sb(ctx, "stats", [P, 3, 64])

    chunk_landed = [signal(f"chunk_landed{i}") for i in range(RING)]
    chunk_used = signal("chunk_used")
    stage_done = signal("stage_done")
    small_landed = signal("small_landed")
    out_landed = signal("out_landed")
    bank_full = signal("bank_full")
    bank_free_act = signal("bank_free_act")
    bank_free_dve = signal("bank_free_dve")
    act_out = signal("act_out")
    dve_out = signal("dve_out")
    scores_ready = signal("scores_ready")
    max_ready = signal("max_ready")
    probs_ready = signal("probs_ready")
    turned_ready = signal("turned_ready")
    probsT_ready = signal("probsT_ready")
    pv_ready = signal("pv_ready")
    head_stored = signal("head_stored")
    chunks = [0]

    block = ctx.enter_context(nc.Block())

    class Stage:

        def __init__(self):
            self.before = stage_done.n
            self.members = 0

        def _run(self, start, fn):
            before = self.before
            self.members += 1

            @start
            def _(eng):
                if before:
                    eng.wait_ge(stage_done.sem, before)
                fn(eng)
                eng.drain()
                eng.sem_inc(stage_done.sem, 1)

        def tensor(self, fn):
            self._run(block.tensor, fn)

        def vector(self, fn):
            self._run(block.vector, fn)

        def scalar(self, fn):
            self._run(block.scalar, fn)

        def gpsimd(self, fn):
            self._run(block.gpsimd, fn)

        def end(self):
            stage_done.n += self.members

    def chunk(n):
        return ring[n % RING]

    def stream(parts):
        n0 = chunks[0]

        @block.sync
        def _(sp):
            for j, pieces in enumerate(parts):
                n = n0 + j
                if n >= RING:
                    used, value = used_at[n - RING]
                    sp.wait_ge(used.sem, value)
                for off, src in pieces:
                    k, w = src.shape[1], src.shape[2]
                    dst = chunk(n)[:, :].rearrange("p (k n) -> p k n", k=KT)[:, 0:k, off:off + w]
                    if len(pieces) == 1:
                        dst = chunk(n)[:, 0:k * w].rearrange("p (k n) -> p k n", k=k)
                    sp.dma_start(dst, src).then_inc(chunk_landed[n % RING].sem, 16)
                    chunk_landed[n % RING].n += 16
                landed_at[n] = chunk_landed[n % RING].n
        chunks[0] += len(parts)
        return n0

    landed_at = {}
    used_at = {}

    def arrived(eng, n):
        eng.wait_ge(chunk_landed[n % RING].sem, landed_at[n])

    def rows(w):
        return w.rearrange("(t p) n -> p t n", p=P)

    _small = [0]

    def load_small(pairs, wait=True):
        st = Stage()

        @st.scalar
        def _(act):
            for dst, src in pairs:
                act.dma_start(dst, src).then_inc(small_landed.sem, 16)
                small_landed.n += 16
            if wait:
                act.wait_ge(small_landed.sem, small_landed.n)
        st.end()

    st = Stage()

    @st.gpsimd
    def _(pool):
        pool.memset(ident[:, :], 0.0)
        pool.memset(ones[:, :], 1.0)
        pool.memset(eps_col[:, :], EPS)
        pool.drain()
        pool.affine_select(out=ident[:, :], in_=ident[:, :], compare_op=ALU.not_equal, fill=1.0,
                           base=0, pattern=[[-1, P]], channel_multiplier=1)
    st.end()

    load_small([(x[:, CT:CT + LT, :], A["x"][0].rearrange("(m p) d -> p m d", p=P)),
                (x[:, 0:CT, :], A["ctx"][0].rearrange("(m p) d -> p m d", p=P))])

    def normalise(tiles, xn):
        st = Stage()
        a0, d0 = act_out.n, dve_out.n

        @st.scalar
        def _(act):
            for i, m in enumerate(tiles):
                act.activation(xn[:, i, :], x[:, m, :], ACT.Square, accum_out=stats[:, 0, i:i + 1])
            act.drain()
            act.activation(stats[:, 1, 0:len(tiles)], stats[:, 0, 0:len(tiles)], ACT.Sqrt,
                           scale=1.0 / D, bias=eps_col[:, :]).then_inc(act_out.sem, 1)

        @st.vector
        def _(dve):
            dve.wait_ge(act_out.sem, a0 + 1)
            dve.reciprocal(stats[:, 2, 0:len(tiles)], stats[:, 1, 0:len(tiles)])
            dve.drain()
            for i, m in enumerate(tiles):
                dve.tensor_scalar(xn[:, i, :], x[:, m, :], stats[:, 2, i:i + 1], None, ALU.mult)
        act_out.n = a0 + 1
        st.end()

    def turn(src, dst, n_tok, n_feat, mods=None):
        st = Stage()
        f0, a0 = bank_full.n, bank_free_act.n

        @st.tensor
        def _(pe):
            for k in range(n_feat):
                if k >= 8:
                    pe.wait_ge(bank_free_act.sem, a0 + k - 7)
                for i in range(n_tok):
                    mm = pe.transpose(bank[k % 8][:, i * P:(i + 1) * P], src(i, k), ident[:, :])
                mm.then_inc(bank_full.sem, 1)

        @st.scalar
        def _(act):
            for k in range(n_feat):
                act.wait_ge(bank_full.sem, f0 + k + 1)
                if mods is None:
                    a = act.activation(dst(k), bank[k % 8][:, 0:n_tok * P], ACT.Copy)
                else:
                    for lo, hi, scale, shift in mods(k):
                        a = act.activation(dst(k)[:, lo:hi], bank[k % 8][:, lo:hi], ACT.Identity,
                                           scale=scale, bias=shift)
                a.then_inc(bank_free_act.sem, 1)
        bank_full.n += n_feat
        bank_free_act.n += n_feat
        st.end()

    def linear(lhs, tiles, parts, evac, on="vector", side=None, accumulate=None, lead=None):
        g = accumulate or 1
        nt = len(tiles)
        f0, n0 = bank_full.n, chunks[0]
        for c in range(len(parts)):
            if c % g == g - 1:
                used_at[n0 + c] = (bank_full, f0 + (c // g + 1) * nt)
            else:
                chunk_used.n += 1
                used_at[n0 + c] = (chunk_used, chunk_used.n)
        stream([pieces for _, _, pieces in parts])
        st = Stage()
        free = bank_free_act if on == "scalar" else bank_free_dve
        e0 = free.n

        @st.tensor
        def _(pe):
            for c, (k_tiles, w, _) in enumerate(parts):
                arrived(pe, n0 + c)
                wt = chunk(n0 + c)[:, 0:k_tiles * w].rearrange("p (k n) -> p k n", k=k_tiles)
                for i, m in enumerate(tiles):
                    use = (c // g) * nt + i
                    if c % g == 0 and use >= 8:
                        pe.wait_ge(free.sem, e0 + use - 7)
                    for k in range(k_tiles):
                        lt = lhs(c, m, k)
                        mm = pe.matmul(bank[use % 8][0:lt.shape[1], 0:w], lt, wt[:, k, :],
                                       start=(k == 0 and c % g == 0),
                                       stop=(k == k_tiles - 1 and c % g == g - 1))
                    if c % g == g - 1:
                        mm.then_inc(bank_full.sem, 1)
                if c % g != g - 1:
                    mm.then_inc(chunk_used.sem, 1)

        def reader(eng):
            if lead:
                lead(eng)
            for c in range(len(parts) // g):
                for i, m in enumerate(tiles):
                    use = c * nt + i
                    eng.wait_ge(bank_full.sem, f0 + use + 1)
                    evac(eng, c, i, bank[use % 8]).then_inc(free.sem, 1)
        if on == "scalar":
            st.scalar(reader)
            if side:
                st.vector(side)
        else:
            st.vector(reader)
            if side:
                st.scalar(side)
        bank_full.n += nt * (len(parts) // g)
        free.n += nt * (len(parts) // g)
        st.end()


    def head_norm(views, d, tmp):
        on_vector, on_scalar = head_norm_programs(views, d, tmp)
        st = Stage()
        st.vector(on_vector)
        st.scalar(on_scalar)
        st.end()

    def head_norm_programs(views, d, tmp):
        n = [v.shape[1] for v in views]
        at = [sum(n[:j]) for j in range(len(n))]
        total = sum(n)
        a0, d0 = act_out.n, dve_out.n

        def on_vector(dve):
            for j, v in enumerate(views):
                sq = tmp[:, j % 2, 0:n[j] * d].rearrange("p (n d) -> p n d", d=d)
                dve.tensor_tensor(sq, v, v, ALU.mult)
                dve.drain()
                red = dve.tensor_reduce(stats[:, 0, at[j]:at[j] + n[j]], sq, AX, ALU.add)
            red.then_inc(dve_out.sem, 1)
            dve.wait_ge(act_out.sem, a0 + 1)
            dve.reciprocal(stats[:, 2, 0:total], stats[:, 1, 0:total])
            dve.drain()
            for j, v in enumerate(views):
                r = stats[:, 2, at[j]:at[j] + n[j]].unsqueeze(2).to_broadcast([P, n[j], d])
                dve.tensor_tensor(v, v, r, ALU.mult)

        def on_scalar(act):
            act.wait_ge(dve_out.sem, d0 + 1)
            act.activation(stats[:, 1, 0:total], stats[:, 0, 0:total], ACT.Sqrt,
                           scale=1.0 / d, bias=eps_col[:, :]).then_inc(act_out.sem, 1)
        act_out.n += 1
        dve_out.n += 1
        return on_vector, on_scalar

    def attend(units, probs, probsT, col):
        st = Stage()
        n = len(units)
        s0, m0, p0, t0 = scores_ready.n, max_ready.n, probs_ready.n, turned_ready.n
        pt0, v0, h0 = probsT_ready.n, pv_ready.n, head_stored.n
        S, T, O = bank[0:2], bank[2:4], bank[4:6]

        @st.tensor
        def _(pe):
            for s in range(n + 2):
                if s < n:
                    if s >= 2:
                        pe.wait_ge(probs_ready.sem, p0 + s - 1)
                    for lt, rhs, lo, start, stop in units[s][0]:
                        mm = pe.matmul(S[s % 2][:, lo:lo + rhs.shape[1]], lt, rhs,
                                       start=start, stop=stop)
                    mm.then_inc(scores_ready.sem, 1)
                if 1 <= s <= n:
                    u = s - 1
                    pe.wait_ge(probs_ready.sem, p0 + u + 1)
                    if u >= 2:
                        pe.wait_ge(probsT_ready.sem, pt0 + u - 1)
                    for j in range(units[u][1] // P):
                        mm = pe.transpose(T[u % 2][:, j * P:(j + 1) * P],
                                          probs[:, u % 2, j * P:(j + 1) * P], ident[:, :])
                    mm.then_inc(turned_ready.sem, 1)
                if s >= 2:
                    u = s - 2
                    pe.wait_ge(probsT_ready.sem, pt0 + u + 1)
                    if u >= 2:
                        pe.wait_ge(head_stored.sem, h0 + u - 1)
                    vs = units[u][2]
                    for j, v in enumerate(vs):
                        mm = pe.matmul(O[u % 2][:, 0:v.shape[1]], probsT[:, u % 2, j * P:(j + 1) * P],
                                       v, start=(j == 0), stop=(j == len(vs) - 1))
                    mm.then_inc(pv_ready.sem, 1)

        @st.vector
        def _(dve):
            for s in range(n + 1):
                if s < n:
                    dve.wait_ge(scores_ready.sem, s0 + s + 1)
                    dve.tensor_reduce(col[:, 1, s % 4:s % 4 + 1], S[s % 2][:, 0:units[s][1]], AX, ALU.max)
                    dve.drain()
                    dve.tensor_scalar(col[:, 0, s % 4:s % 4 + 1], col[:, 1, s % 4:s % 4 + 1], -1.0, None,
                                      ALU.mult).then_inc(max_ready.sem, 1)
                if s >= 1:
                    u = s - 1
                    dve.wait_ge(turned_ready.sem, t0 + u + 1)
                    dve.reciprocal(col[:, 3, u % 4:u % 4 + 1], col[:, 2, u % 4:u % 4 + 1])
                    if u >= 2:
                        dve.wait_ge(pv_ready.sem, v0 + u - 1)
                    dve.tensor_copy(probsT[:, u % 2, 0:units[u][1]],
                                    T[u % 2][:, 0:units[u][1]]).then_inc(probsT_ready.sem, 1)

        @st.scalar
        def _(act):
            for s in range(n + 2):
                if s < n:
                    act.wait_ge(max_ready.sem, m0 + s + 1)
                    if s >= 2:
                        act.wait_ge(turned_ready.sem, t0 + s - 1)
                    act.activation(probs[:, s % 2, 0:units[s][1]], S[s % 2][:, 0:units[s][1]], ACT.Exp,
                                   bias=col[:, 0, s % 4:s % 4 + 1],
                                   accum_out=col[:, 2, s % 4:s % 4 + 1]).then_inc(probs_ready.sem, 1)
                if s >= 2:
                    u = s - 2
                    act.wait_ge(probsT_ready.sem, pt0 + u + 1)
                    act.wait_ge(pv_ready.sem, v0 + u + 1)
                    dst = units[u][3]
                    act.activation(dst, O[u % 2][:, 0:dst.shape[1]], ACT.Copy,
                                   scale=col[:, 3, u % 4:u % 4 + 1]).then_inc(head_stored.sem, 1)
        for sig in (scores_ready, max_ready, probs_ready, turned_ready, probsT_ready, pv_ready, head_stored):
            sig.n += n
        st.end()

    def wait_value(sig):
        return sig.n

    silu_c = sb(ctx, "silu_c", [P, KT, 2])
    router_w = sb(ctx, "router_w_sb", [P, KT, N_EXP])
    router_b = sb(ctx, "router_b_sb", [P, N_EXP])
    load_small([(silu_c[:, :, :], A["cond"]),
                (router_w[:, :, :], rows(A["router_w"])),
                (router_b[:, :], A["router_b"].unsqueeze(0).to_broadcast([P, N_EXP]))])
    st = Stage()

    @st.scalar
    def _(act):
        act.activation(silu_c[:, :, :], silu_c[:, :, :], ACT.Silu)
    st.end()

    def ada(l, modc, gateb, gcols):
        with ExitStack() as mem:
            mod = sb(mem, f"mod{l}", [2, 6 * D])
            load_small([(mod[s:s + 1, :], A["ada_b"][l:l + 1, :]) for s in range(2)]
                       + [(gcols[:, 0, :], A["norm_mix_cols"][l]), (gcols[:, 1, :], A["norm_ffn_cols"][l])])
            w = A["ada_w"][l].rearrange("(t p) n -> p t n", p=P)

            def evac(eng, c, i, b):
                cols = slice(c * COLS, (c + 1) * COLS)
                return eng.tensor_tensor(mod[:, cols], b[0:2, :], mod[:, cols], ALU.add)
            linear(lambda c, m, k: silu_c[:, k, :], [0],
                   [(KT, COLS, [(0, w[:, :, c * COLS:(c + 1) * COLS])]) for c in range(6 * D // COLS)], evac)
            st = Stage()
            f0, a0 = bank_full.n, bank_free_act.n

            @st.tensor
            def _(pe):
                for v, part in enumerate((0, 1, 3, 4)):
                    for k in range(KT):
                        j = v * KT + k
                        mm = pe.transpose(bank[0][:, 2 * j:2 * j + 2],
                                          mod[:, part * D + k * P:part * D + (k + 1) * P], ident[0:2, 0:2])
                mm.then_inc(bank_full.sem, 1)
                for g, part in enumerate((2, 5)):
                    for s in range(2):
                        for half in range(2):
                            j = 1 + (g * 2 + s) * 2 + half
                            if j == 8:
                                pe.wait_ge(bank_free_act.sem, a0 + 1)
                            mm = pe.matmul(bank[j % 8][:, :], ident[0:2, s:s + 1].to_broadcast([2, P]),
                                           mod[:, part * D + half * COLS:part * D + (half + 1) * COLS],
                                           start=True, stop=True)
                            mm.then_inc(bank_full.sem, 1)

            @st.scalar
            def _(act):
                act.wait_ge(bank_full.sem, f0 + 1)
                act.activation(modc[:, :, :], bank[0][:, 0:64], ACT.Copy).then_inc(bank_free_act.sem, 1)
                for j in range(1, 9):
                    act.wait_ge(bank_full.sem, f0 + 1 + j)
                    g, s, half = (j - 1) // 4, (j - 1) // 2 % 2, (j - 1) % 2
                    act.activation(gateb[:, g, s, half * COLS:(half + 1) * COLS], bank[j % 8][:, :], ACT.Copy)

            @st.vector
            def _(dve):
                dve.wait_ge(bank_free_act.sem, a0 + 1)
                for v in range(2):
                    sc = modc[:, (2 * v + 1) * KT:(2 * v + 2) * KT, :]
                    dve.scalar_tensor_tensor(sc, sc, 1.0, gcols[:, v, :].unsqueeze(2).to_broadcast([P, KT, 2]),
                                             ALU.add, ALU.mult)
            bank_full.n += 9
            bank_free_act.n += 1
            st.end()

    def modulated(modc, v, tiles):
        n_ctx = sum(m < CT for m in tiles)

        def mods(k):
            sh, sc = modc[:, 2 * v * KT + k, :], modc[:, (2 * v + 1) * KT + k, :]
            out = []
            if n_ctx:
                out.append((0, n_ctx * P, sc[:, 1:2], sh[:, 1:2]))
            out.append((n_ctx * P, len(tiles) * P, sc[:, 0:1], sh[:, 0:1]))
            return out
        with ExitStack() as mem:
            xn = sb(mem, f"xn{serial[0]}", [P, len(tiles), D])
            normalise(tiles, xn)
            turn(lambda i, k: xn[:, i, k * P:(k + 1) * P], lambda k: hT[:, k, 0:len(tiles) * P],
                 len(tiles), KT, mods)

    def project_out(o, w, tiles, gateb, g):
        turn(lambda i, k: o[:, i, k * P:(k + 1) * P], lambda k: hT[:, k, 0:len(tiles) * P], len(tiles), KT)
        with ExitStack() as mem:
            tmp = sb(mem, f"po{serial[0]}", [P, 2, COLS])

            def evac(eng, c, i, b):
                m, cols = tiles[i], slice(c * COLS, (c + 1) * COLS)
                t = tmp[:, i % 2, :]
                eng.drain()
                if gateb is None:
                    return eng.tensor_tensor(x[:, m, cols], b[:, :], x[:, m, cols], ALU.add)
                eng.tensor_tensor(t, b[:, :], gateb[:, g, int(m < CT), cols], ALU.mult)
                eng.drain()
                return eng.tensor_tensor(x[:, m, cols], t, x[:, m, cols], ALU.add)
            linear(lambda c, m, k: hT[:, k, tiles.index(m) * P:(tiles.index(m) + 1) * P], tiles,
                   [(KT, COLS, [(0, rows(w)[:, :, c * COLS:(c + 1) * COLS])]) for c in range(D // COLS)], evac)

    moe_silu = signal("moe_silu")

    def moe(l, tiles, gateb):
        nt = len(tiles)
        n_y = nt * (D // COLS)
        with ExitStack() as mem:
            comb = sb(mem, f"comb{l}", [P, N_EXP + 1, nt])
            rank = sb(mem, f"rank{l}", [P, N_EXP + 1, nt])
            iota = sb(mem, f"iota{l}", [P, P])
            passes = sb(mem, f"passes{l}", [P, 1], mybir.dt.int32)
            with ExitStack() as mem2:
                route(l, mem2, comb, rank, iota, passes, nt)
            y = sb(mem, f"y{l}", [P, nt, D])
            h_tok = sb(mem, f"h_tok{l}", [P, nt, D])
            turn(lambda i, k: hT[:, (k % 2) * 4 + i, (k // 2) * P:(k // 2 + 1) * P],
                 lambda k: h_tok[:, k // 2, (k % 2) * COLS:(k % 2 + 1) * COLS], 4, 2 * nt)
            pick = sb(mem, f"pick{l}", [P, nt, P])
            pickw = sb(mem, f"pickw{l}", [P, nt, P])
            spread = sb(mem, f"spread{l}", [P, nt * P])
            hg = sb(mem, f"hg{l}", [P, KT, P])
            sg = sb(mem, f"sg{l}", [P, D_FF])
            act_h = sb(mem, f"act_h{l}", [P, D_FF])
            hidT = sb(mem, f"hidT{l}", [P, 4, P])
            ye = sb(mem, f"ye{l}", [P, D])
            cc = sb(mem, f"cc{l}", [P, nt])
            rc = sb(mem, f"rc{l}", [P, nt])
            w1, w3, w2 = A["exp_w1"][l], A["exp_w3"][l], A["exp_w2"][l]
            n0 = chunks[0]
            slot = [(n0 + j) % RING for j in range(3)]

            def sem(name):
                return ctx.enter_context(nc.semaphore(f"{name}{l}"))
            w_landed = [sem(f"moe_w{j}_landed") for j in (1, 3, 2)]
            pick_ready, gathered, hg_ready = sem("pick_ready"), sem("gathered"), sem("hg_ready")
            pickw_turned, spread_ready = sem("pickw_turned"), sem("spread_ready")
            up1_done, up3_done, silu_done, hidden = (sem("up1_done"), sem("up3_done"), sem("silu_done"),
                                                     sem("hidden"))
            hidden_turned, hidT_ready = sem("hidden_turned"), sem("hidT_ready")
            down_done, ye_ready = sem("down_done"), sem("ye_ready")
            scattered, added = sem("scattered"), sem("added")
            routed = stage_done.n

            def load(sp, j, e):
                w = (w1, w3, w2)[j][bass.ds(e, 1)].rearrange("a (t p) n -> p (a t) n", p=P)
                k = w.shape[1]
                sp.dma_start(ring[slot[j]][:, :].rearrange("p (k n) -> p k n", k=k), w)\
                    .then_inc(w_landed[j], 16)

            def passes_of(eng):
                return eng.value_load(passes[0:1, 0:1], min_val=1, max_val=nt)

            @block.sync
            def _(sp):
                for j in range(3):
                    used, value = used_at[n0 + j - RING]
                    sp.wait_ge(used.sem, value)
                sp.wait_ge(stage_done.sem, routed)
                for s in (up1_done, up3_done, down_done):
                    sp.sem_inc(s, 1)
                with sp.Fori(0, passes_of(sp)) as p:
                    with sp.Fori(0, N_EXP) as e:
                        it = p * N_EXP + e
                        sp.wait_ge(up1_done, it + 1)
                        load(sp, 0, e)
                        sp.wait_ge(up3_done, it + 1)
                        load(sp, 1, e)
                        sp.wait_ge(down_done, it * 2 + 1)
                        load(sp, 2, e)

            st = Stage()

            @st.tensor
            def _(pe):
                up1 = ring[slot[0]][:, :].rearrange("p (k n) -> p k n", k=KT)
                up3 = ring[slot[1]][:, :].rearrange("p (k n) -> p k n", k=KT)
                down = ring[slot[2]][:, :].rearrange("p (k n) -> p k n", k=4)
                with pe.Fori(0, passes_of(pe)) as p:
                    with pe.Fori(0, N_EXP) as e:
                        it = p * N_EXP + e
                        pe.wait_ge(pick_ready, it + p + 1)
                        for d in range(KT):
                            for m in range(nt):
                                mm = pe.matmul(bank[6 + d // 4][:, (d % 4) * P:(d % 4 + 1) * P],
                                               h_tok[:, m, d * P:(d + 1) * P], pick[:, m, :],
                                               start=(m == 0), stop=(m == nt - 1))
                            if d % 4 == 3:
                                mm.then_inc(gathered, 1)
                        pe.wait_ge(w_landed[0], it * 16 + 16)
                        pe.wait_ge(added, it * n_y + 1)
                        for half in range(2):
                            pe.wait_ge(hg_ready, it * 2 + 1 + half)
                            for k in range(4 * half, 4 * half + 4):
                                mm = pe.matmul(bank[3][:, :], hg[:, k, :], up1[:, k, :],
                                               start=(k == 0), stop=(k == KT - 1))
                        mm.then_inc(up1_done, 1)
                        pe.wait_ge(w_landed[1], it * 16 + 16)
                        for k in range(KT):
                            mm = pe.matmul(bank[4][:, :], hg[:, k, :], up3[:, k, :],
                                           start=(k == 0), stop=(k == KT - 1))
                        mm.then_inc(up3_done, 1)
                        for m in range(nt):
                            mm = pe.transpose(bank[2][:, m * P:(m + 1) * P], pickw[:, m, :], ident[:, :])
                        mm.then_inc(pickw_turned, 1)
                        pe.wait_ge(hidden, it + 1)
                        for k in range(4):
                            mm = pe.transpose(bank[5][:, k * P:(k + 1) * P], act_h[:, k * P:(k + 1) * P],
                                              ident[:, :])
                        mm.then_inc(hidden_turned, 1)
                        pe.wait_ge(w_landed[2], it * 16 + 16)
                        pe.wait_ge(hidT_ready, it + 1)
                        for half in range(2):
                            for k in range(4):
                                mm = pe.matmul(bank[6 + half][:, :], hidT[:, k, :],
                                               down[:, k, half * COLS:(half + 1) * COLS],
                                               start=(k == 0), stop=(k == 3))
                            mm.then_inc(down_done, 1)
                        pe.wait_ge(spread_ready, it + 1)
                        for i in range(n_y):
                            half, m = i // nt, i % nt
                            if m == 0:
                                pe.wait_ge(ye_ready, it * 2 + 1 + half)
                            if i >= 4:
                                pe.wait_ge(added, it * n_y + i - 2)
                            pe.matmul(bank[i % 4][:, :], spread[:, m * P:(m + 1) * P],
                                      ye[:, half * COLS:(half + 1) * COLS], start=True, stop=True)\
                                .then_inc(scattered, 1)

            @st.scalar
            def _(act):
                with act.Fori(0, passes_of(act)) as p:
                    with act.Fori(0, N_EXP) as e:
                        it = p * N_EXP + e
                        for half in range(2):
                            act.wait_ge(gathered, it * 2 + 1 + half)
                            act.activation(hg[:, 4 * half:4 * half + 4, :].rearrange("p k s -> p (k s)"),
                                           bank[6 + half][:, :], ACT.Copy).then_inc(hg_ready, 1)
                        act.wait_ge(up1_done, it + 2)
                        act.activation(sg[:, :], bank[3][:, :], ACT.Silu).then_inc(silu_done, 1)
                        act.wait_ge(hidden_turned, it + 1)
                        act.activation(hidT[:, :, :].rearrange("p k s -> p (k s)"), bank[5][:, :], ACT.Copy)\
                            .then_inc(hidT_ready, 1)
                        act.wait_ge(pickw_turned, it + 1)
                        act.activation(spread[:, :], bank[2][:, 0:nt * P], ACT.Copy).then_inc(spread_ready, 1)
                        for half in range(2):
                            act.wait_ge(down_done, it * 2 + 2 + half)
                            act.activation(ye[:, half * COLS:(half + 1) * COLS], bank[6 + half][:, :], ACT.Copy)\
                                .then_inc(ye_ready, 1)

            @st.vector
            def _(dve):
                dve.memset(y[:, :, :], 0.0).then_inc(added, 1)

                def picks(e):
                    dve.tensor_copy(cc[:, :], comb[:, bass.ds(e, 1), :].rearrange("p a m -> p (a m)"))
                    dve.tensor_copy(rc[:, :], rank[:, bass.ds(e, 1), :].rearrange("p a m -> p (a m)"))
                    dve.drain()
                    for m in range(nt):
                        dve.tensor_scalar(pick[:, m, :], iota[:, :], rc[:, m:m + 1], None, ALU.is_equal)
                    for m in range(nt):
                        ins = dve.tensor_scalar(pickw[:, m, :], iota[:, :], rc[:, m:m + 1], cc[:, m:m + 1],
                                                ALU.is_equal, ALU.mult)
                    ins.then_inc(pick_ready, 1)
                with dve.Fori(0, passes_of(dve)) as p:
                    dve.drain()
                    picks(0)
                    with dve.Fori(0, N_EXP) as e:
                        it = p * N_EXP + e
                        dve.wait_ge(silu_done, it + 1)
                        dve.wait_ge(up3_done, it + 2)
                        dve.tensor_tensor(act_h[:, :], sg[:, :], bank[4][:, :], ALU.mult).then_inc(hidden, 1)
                        dve.wait_ge(pickw_turned, it + 1)
                        picks(e + 1)
                        for i in range(n_y):
                            half, m = i // nt, i % nt
                            cols = slice(half * COLS, (half + 1) * COLS)
                            dve.wait_ge(scattered, it * n_y + i + 1)
                            dve.tensor_tensor(y[:, m, cols], bank[i % 4][:, :], y[:, m, cols], ALU.add)\
                                .then_inc(added, 1)
                        dve.drain()
                    dve.tensor_scalar(rank[:, :, :], rank[:, :, :], -float(P), None, ALU.add)
                    dve.drain()
                for i, m in enumerate(tiles):
                    dve.tensor_tensor(y[:, i, :], y[:, i, :], gateb[:, 1, int(m < CT), :], ALU.mult)
                dve.drain()
                for i, m in enumerate(tiles):
                    dve.tensor_tensor(x[:, m, :], y[:, i, :], x[:, m, :], ALU.add)
            st.end()
            chunks[0] += 3
            for j in range(3):
                used_at[chunks[0] - 3 + j] = (stage_done, stage_done.n)

    def route(l, mem, comb, rank, iota, passes, nt):
        f0, a0 = bank_full.n, act_out.n
        sc = sb(mem, f"r_sc{l}", [P, nt, N_EXP])
        sel = sb(mem, f"r_sel{l}", [P, nt, N_EXP])
        pair = sb(mem, f"r_pair{l}", [P, nt * N_GROUPS, 6])
        gs = sb(mem, f"r_gs{l}", [P, nt * N_GROUPS])
        best = sb(mem, f"r_best{l}", [P, nt])
        hot = sb(mem, f"r_hot{l}", [P, nt, N_EXP])
        hot2 = sb(mem, f"r_hot2{l}", [P, nt, N_EXP])
        prio = sb(mem, f"r_prio{l}", [P, N_EXP])
        before = sb(mem, f"r_before{l}", [P, P])
        few = sb(mem, f"r_few{l}", [P, 3])
        st = Stage()

        @st.gpsimd
        def _(pool):
            pool.iota(prio[:, :], pattern=[[-1, N_EXP]], base=N_EXP, channel_multiplier=0,
                      allow_small_or_imprecise_dtypes=True)
            pool.iota(iota[:, :], pattern=[[1, P]], base=0, channel_multiplier=0,
                      allow_small_or_imprecise_dtypes=True)
            pool.affine_select(out=before[:, :], in_=ones[:, :], compare_op=ALU.is_gt, fill=0.0,
                               base=0, pattern=[[1, P]], channel_multiplier=-1)

        @st.tensor
        def _(pe):
            for m in range(nt):
                for k in range(KT):
                    mm = pe.matmul(bank[m][:, 0:N_EXP], hT[:, k, m * P:(m + 1) * P], router_w[:, k, :],
                                   start=(k == 0), stop=(k == KT - 1))
            mm.then_inc(bank_full.sem, 1)

        @st.scalar
        def _(act):
            act.wait_ge(bank_full.sem, f0 + 1)
            for m in range(nt):
                act.activation(sc[:, m, :], bank[m][:, 0:N_EXP], ACT.Sigmoid)
        bank_full.n += 1
        st.end()
        st = Stage()

        @st.vector
        def _(dve):
            def bc(a, n):
                return a.unsqueeze(2).to_broadcast([P, a.shape[1], n])

            def first_hot(dst, values, top, n, groups):
                dve.tensor_tensor(dst, values, bc(top, n), ALU.is_equal)
                dve.drain()
                dve.tensor_tensor(dst, dst, prio[:, N_EXP - n:].unsqueeze(1).to_broadcast([P, groups, n]), ALU.mult)
                dve.drain()
                dve.tensor_reduce(top, dst, AX, ALU.max)
                dve.drain()
                dve.tensor_tensor(dst, dst, bc(top, n), ALU.is_equal)
                dve.drain()

            dve.tensor_tensor(sel[:, :, :], sc[:, :, :], router_b[:, :].unsqueeze(1).to_broadcast([P, nt, N_EXP]),
                              ALU.add)
            dve.drain()
            s4 = sel[:, :, :].rearrange("p m (g e) -> p (m g) e", e=EPG)
            for j, (a, b) in enumerate([(0, 1), (0, 2), (0, 3), (1, 2), (1, 3), (2, 3)]):
                dve.tensor_tensor(pair[:, :, j], s4[:, :, a], s4[:, :, b], ALU.add)
            dve.drain()
            dve.tensor_reduce(gs[:, :], pair[:, :, :], AX, ALU.max)
            dve.drain()
            g3 = gs[:, :].rearrange("p (m g) -> p m g", g=N_GROUPS)
            dve.tensor_reduce(best[:, :], g3, AX, ALU.max)
            dve.drain()
            hg = pair[:, :, 0].rearrange("p (m g) -> p m g", g=N_GROUPS)
            first_hot(hg, g3, best[:, :], N_GROUPS, nt)
            dve.tensor_scalar(gs[:, :], pair[:, :, 0], -1.0, BIG, ALU.add, ALU.mult)
            dve.drain()
            dve.tensor_tensor(s4, s4, bc(gs[:, :], EPG), ALU.add)
            dve.drain()
            dve.tensor_reduce(best[:, :], sel[:, :, :], AX, ALU.max)
            dve.drain()
            first_hot(hot[:, :, :], sel[:, :, :], best[:, :], N_EXP, nt)
            dve.scalar_tensor_tensor(sel[:, :, :], hot[:, :, :], -2 * BIG, sel[:, :, :], ALU.mult, ALU.add)
            dve.drain()
            dve.tensor_reduce(best[:, :], sel[:, :, :], AX, ALU.max)
            dve.drain()
            first_hot(hot2[:, :, :], sel[:, :, :], best[:, :], N_EXP, nt)
            dve.tensor_tensor(hot[:, :, :], hot[:, :, :], hot2[:, :, :], ALU.add)
            dve.drain()
            dve.tensor_tensor(sc[:, :, :], sc[:, :, :], hot[:, :, :], ALU.mult)
            dve.drain()
            dve.tensor_reduce(best[:, :], sc[:, :, :], AX, ALU.add)
            dve.drain()
            dve.reciprocal(gs[:, 0:nt], best[:, :])
            dve.drain()
            dve.memset(comb[:, N_EXP, :], 0.0)
            dve.memset(rank[:, N_EXP, :], -1.0)
            dve.tensor_tensor(comb[:, 0:N_EXP, :].rearrange("p e m -> p m e"), sc[:, :, :], bc(gs[:, 0:nt], N_EXP),
                              ALU.mult)
        st.end()
        st = Stage()
        f0 = bank_full.n

        @st.tensor
        def _(pe):
            for m in range(nt):
                for b in range(m + 1):
                    mm = pe.matmul(bank[0][:, m * N_EXP:(m + 1) * N_EXP], before[:, :] if b == m else ones[:, :],
                                   hot[:, b, :], start=(b == 0), stop=(b == m))
            for m in range(nt):
                mm = pe.matmul(bank[1][:, 0:N_EXP], ones[:, :], hot[:, m, :], start=(m == 0), stop=(m == nt - 1))
            mm.then_inc(bank_full.sem, 1)

        @st.vector
        def _(dve):
            dve.wait_ge(bank_full.sem, f0 + 1)
            r = rank[:, 0:N_EXP, :].rearrange("p e m -> p m e")
            dve.scalar_tensor_tensor(r, bank[0][:, 0:nt * N_EXP].rearrange("p (m e) -> p m e", m=nt), 1.0,
                                     hot[:, :, :], ALU.add, ALU.mult)
            dve.tensor_reduce(few[:, 0:1], bank[1][:, 0:N_EXP], AX, ALU.max)
            dve.drain()
            dve.tensor_scalar(rank[:, 0:N_EXP, :], rank[:, 0:N_EXP, :], -1.0, None, ALU.add)
            dve.memset(few[:, 1:2], 1.0)
            for q in range(1, nt):
                dve.drain()
                dve.tensor_scalar(few[:, 2:3], few[:, 0:1], q * P + 0.5, None, ALU.is_gt)
                dve.drain()
                dve.tensor_tensor(few[:, 1:2], few[:, 1:2], few[:, 2:3], ALU.add)
            dve.drain()
            dve.tensor_copy(passes[:, :], few[:, 1:2])
        bank_full.n += 1
        st.end()

    def even_mixer(gateb):
        with ExitStack() as mem:
            omix = sb(mem, "omix", [P, 4, D])
            proj_m = sb(mem, "proj_m", [P, 4, D_IN_EVEN - MQ])
            with ExitStack() as m2:
                proj_a = sb(m2, "proj_a", [P, 4, MQ])
                bias = sb(m2, "na_bias", [P, LT, H_A, S_LAT])
                rpb = A["na_rpb"]
                n_r, n_c = 15, 31
                loads = []
                for qr in range(ROWS):
                    b = qr % 2
                    for h in range(H_A):
                        at = h * n_r * n_c + (7 - qr) * n_c + 15 - 63
                        src = bass.AP(tensor=rpb.tensor, offset=at, ap=[[1, GRID_W], [n_c, ROWS], [1, GRID_W]])
                        dst = bias[64 * b:64 * b + 64, qr // 2, h, :].rearrange("p (r c) -> p r c", c=GRID_W)
                        loads.append((dst, src))
                load_small(loads, wait=False)
                w = rows(A["even_w_in"][0])
                for dst, lo, hi in ((proj_m, MQ, D_IN_EVEN), (proj_a, 0, MQ)):
                    starts = list(range(lo, hi, COLS))
                    widths = [min(COLS, hi - c) for c in starts]

                    def evac(eng, c, i, b, dst=dst, widths=widths):
                        return eng.activation(dst[:, i, c * COLS:c * COLS + widths[c]], b[:, 0:widths[c]], ACT.Copy)
                    linear(lambda c, m, k: hT[:, k, m * P:(m + 1) * P], range(4),
                           [(KT, n, [(0, w[:, :, c:c + n])]) for c, n in zip(starts, widths)], evac, on="scalar")
                neighbourhood(m2, proj_a, omix, bias)
            with ExitStack() as m2:
                mlstm(m2, proj_m, omix)
            project_out(omix, A["even_w_out"][0], list(range(4)), gateb, 0)

    def neighbourhood(mem, proj, omix, bias):
        with ExitStack() as early:
            tmp = sb(early, "na_tmp", [P, 2, 1024])
            head_norm([proj[:, m, 0:1024].rearrange("p (n d) -> p n d", d=HD_A) for m in range(4)], HD_A, tmp)
        qT = sb(mem, "na_qT", [P, 4, 512])
        kT = sb(mem, "na_kT", [P, 4, 512])
        gain = sb(mem, "na_gain", [P, 2])
        flip = sb(mem, "na_flip", [P, P])
        window = sb(mem, "na_window", [P, GRID_W])
        probs = sb(mem, "na_probs", [P, 2, 512])
        probsT = sb(mem, "na_probsT", [P, 2, 512])
        col = sb(mem, "na_col", [P, 3 + 1, 4])
        load_small([(gain[:, 0:1], A["na_q_gain"]), (gain[:, 1:2], A["na_k_gain"]), (window[:, :], A["window"])])
        st = Stage()

        @st.gpsimd
        def _(pool):
            pool.memset(flip[:, :], 0.0)
            pool.drain()
            for b in range(2):
                pool.affine_select(out=flip[:, 64 * b:64 * b + 64], in_=flip[:, 64 * b:64 * b + 64],
                                   compare_op=ALU.not_equal, fill=1.0, base=-(64 * b + 63),
                                   pattern=[[1, 64]], channel_multiplier=1)

        @st.vector
        def _(dve):
            for t in range(LT):
                for h in range(H_A):
                    v = bias[:, t, h, :].rearrange("p (r c) -> p r c", c=GRID_W)
                    dve.tensor_tensor(v, v, window[:, :].unsqueeze(1).to_broadcast([P, ROWS, GRID_W]), ALU.add)

        @st.scalar
        def _(act):
            act.mul(gain[:, 0:1], gain[:, 0:1], HD_A ** -0.5)
        st.end()
        turn(lambda i, k: proj[:, i, AQ + k * P:AQ + (k + 1) * P], lambda k: qT[:, k, :], 4, 4,
             lambda k: [(0, 512, gain[:, 0:1], 0.0)])
        turn(lambda i, k: proj[:, i, AK + k * P:AK + (k + 1) * P], lambda k: kT[:, k, :], 4, 4,
             lambda k: [(0, 512, gain[:, 1:2], 0.0)])
        units = []
        for h in range(H_A):
            hp = slice(64 * (h % 2), 64 * (h % 2) + 64)
            for m in range(4):
                q = qT[hp, h // 2, m * P:(m + 1) * P]
                n = 512 if m >= CT else 256
                mms = [(q, kT[hp, h // 2, 0:n], 0, True, m < CT)]
                if m >= CT:
                    mms.append((flip[:, :], bias[:, m - CT, h, :], 256, False, True))
                units.append((mms, n, [proj[:, j, AV + h * HD_A:AV + (h + 1) * HD_A] for j in range(n // P)],
                              omix[:, m, h * HD_A:(h + 1) * HD_A]))
        attend(units, probs, probsT, col)

    def mlstm(mem, proj, omix):
        qT = sb(mem, "ml_qT", [P, 2, 512])
        kT = sb(mem, "ml_kT", [P, 2, 512])
        vaug = sb(mem, "ml_v", [P, 4, H_B, DV_B + 1])
        cap = sb(mem, "ml_cap", [P, 2, 4, 512], BF16)
        rev = sb(mem, "ml_rev", [P, P])
        gb = sb(mem, "ml_gb", [P, 16])
        g = sb(mem, "ml_g", [P, 4, 16])
        t1 = sb(mem, "ml_t1", [P, 4, 16])
        fw = sb(mem, "ml_fw", [P, 4, 2, 8])
        bw = sb(mem, "ml_bw", [P, 4, 2, 8])
        rowI = sb(mem, "ml_rowI", [8, 512])
        rowF = sb(mem, "ml_rowF", [8, 512])
        rowM = sb(mem, "ml_rowM", [8, 512])
        slotc = sb(mem, "ml_slotc", [P, 4, 3, 8])
        colc = sb(mem, "ml_colc", [P, 4, 3, 8])
        e_t = sb(mem, "ml_e", [P, 2, 512])
        w_t = sb(mem, "ml_w", [P, 2, 512])
        pT = sb(mem, "ml_pT", [P, 2, 4, 512])
        den = sb(mem, "ml_den", [P, 2, 4])
        ng = sb(mem, "ml_ng", [P, H_B * DV_B])
        turned_tile = [1, 0, 3, 2]
        turn(lambda i, k: proj[:, i, MQ0 + k * P:MQ0 + (k + 1) * P], lambda k: qT[:, k, :], 4, 2,
             lambda k: [(0, 512, DK_B ** -0.5, 0.0)])
        turn(lambda i, k: proj[:, i, MK0 + k * P:MK0 + (k + 1) * P], lambda k: kT[:, k, :], 4, 2)
        load_small([(gb[:, :], A["mlstm_gate_b"].to_broadcast([P, 16])),
                    (ng[:, :], A["mlstm_norm_g"].to_broadcast([P, H_B * DV_B]))])
        st = Stage()
        a0, d0, f0 = act_out.n, dve_out.n, bank_full.n

        @st.gpsimd
        def _(pool):
            pool.memset(rev[:, :], 0.0)
            pool.memset(cap[:, :, :, :], 0.0)
            pool.drain()
            pool.affine_select(out=rev[:, :], in_=rev[:, :], compare_op=ALU.not_equal, fill=1.0,
                               base=-(P - 1), pattern=[[1, P]], channel_multiplier=1)
            for j in range(4):
                c = cap[:, 0, j, :]
                pool.affine_select(out=c, in_=c, compare_op=ALU.is_ge, fill=BIG, base=-j * P,
                                   pattern=[[1, 512]], channel_multiplier=-1)
                lo = 256 * (j // 2)
                c = cap[:, 1, j, lo:lo + 256]
                pool.affine_select(out=c, in_=c, compare_op=ALU.is_ge, fill=BIG, base=j * P - lo,
                                   pattern=[[-1, 256]], channel_multiplier=1)
                if j >= 2:
                    pool.memset(cap[:, 1, j, 0:256], BIG)

        @st.vector
        def _(dve):
            for m in range(4):
                dve.tensor_copy(vaug[:, m, :, 0:DV_B],
                                proj[:, m, MV0:MV0 + H_B * DV_B].rearrange("p (h d) -> p h d", d=DV_B))
            dve.memset(vaug[:, :, :, DV_B:DV_B + 1], 1.0)
            dve.memset(fw[:, :, :, :], 0.0)
            dve.memset(bw[:, :, :, :], 0.0)
            dve.tensor_tensor(g[:, :, :], proj[:, :, MG0:MG0 + 16], gb[:, :].unsqueeze(1).to_broadcast([P, 4, 16]),
                              ALU.add)
            dve.drain()
            dve.tensor_scalar(t1[:, :, :], g[:, :, :], -1.0, None, ALU.mult)
            dve.drain()
            dve.tensor_tensor(t1[:, :, :], t1[:, :, :], g[:, :, :], ALU.max).then_inc(dve_out.sem, 1)
            dve.wait_ge(act_out.sem, a0 + 1)
            for dst, c in ((fw[:, :, 1, 0:4], 4), (bw[:, :, 1, 4:8], 12)):
                dve.scalar_tensor_tensor(dst, g[:, :, c:c + 4], 0.0, t1[:, :, c:c + 4], ALU.min, ALU.subtract)
            dve.tensor_copy(fw[:, :, 0, 0:4], g[:, :, 0:4])
            dve.tensor_copy(bw[:, :, 0, 4:8], g[:, :, 8:12])

        @st.scalar
        def _(act):
            act.wait_ge(dve_out.sem, d0 + 1)
            act.activation(t1[:, :, :], t1[:, :, :], ACT.Exp, scale=-1.0)
            act.drain()
            act.activation(t1[:, :, :], t1[:, :, :], ACT.Ln, bias=1.0).then_inc(act_out.sem, 1)
        act_out.n += 1
        dve_out.n += 1
        st.end()
        st = Stage()

        @st.tensor
        def _(pe):
            for q in range(2):
                for t in range(4):
                    dst = bank[q][0:8, t * P:(t + 1) * P]
                    pe.matmul(dst, fw[:, t, q, :], ident[:, :], start=True, stop=False)
                    mm = pe.matmul(dst, bw[:, turned_tile[t], q, :], rev[:, :], start=False, stop=True)
                mm.then_inc(bank_full.sem, 1)

        @st.vector
        def _(dve):
            dve.wait_ge(bank_full.sem, f0 + 2)
            dve.tensor_copy(rowF[:, :], bank[1][0:8, :])
            dve.memset(rowM[:, :], 1.0)
            dve.drain()
            dve.tensor_tensor_scan(rowI[:, :], rowM[:, :], rowF[:, :], 0.0, ALU.mult, ALU.add)
            dve.drain()
            dve.tensor_copy(rowF[:, :], rowI[:, :])
            dve.tensor_tensor(rowI[:, :], bank[0][0:8, :], rowI[:, :], ALU.subtract)
            dve.drain()
            dve.tensor_tensor_scan(rowM[:, :], rowI[:, :], rowI[:, :], -BIG, ALU.max, ALU.max)
            dve.drain()
            dve.tensor_tensor(rowF[:, :], rowF[:, :], rowM[:, :], ALU.add)
        bank_full.n += 2
        st.end()
        st = Stage()
        f0, d0 = bank_full.n, dve_out.n

        @st.tensor
        def _(pe):
            for t in range(4):
                for q, r in enumerate((rowI, rowM, rowF)):
                    mm = pe.transpose(bank[0][:, (t * 3 + q) * 8:(t * 3 + q) * 8 + 8], r[:, t * P:(t + 1) * P],
                                      ident[0:8, 0:8])
            mm.then_inc(bank_full.sem, 1)
            pe.wait_ge(dve_out.sem, d0 + 1)
            for t in range(4):
                mm = pe.matmul(bank[1][:, t * 24:(t + 1) * 24], rev[:, :],
                               slotc[:, turned_tile[t], :, :].rearrange("p q r -> p (q r)"),
                               start=True, stop=True)
            mm.then_inc(bank_full.sem, 1)

        @st.vector
        def _(dve):
            dve.wait_ge(bank_full.sem, f0 + 1)
            dve.tensor_copy(slotc[:, :, :, :].rearrange("p t q r -> p (t q r)"), bank[0][:, 0:96])\
                .then_inc(dve_out.sem, 1)
            dve.wait_ge(dve_out.sem, d0 + 1)
            dve.tensor_copy(colc[:, :, :, 0:4], slotc[:, :, :, 0:4])
            dve.wait_ge(bank_full.sem, f0 + 2)
            dve.tensor_copy(colc[:, :, :, 4:8],
                            bank[1][:, 0:96].rearrange("p (t q r) -> p t q r", t=4, q=3)[:, :, :, 4:8])
            dve.drain()
            dve.tensor_scalar(colc[:, :, 2, :], colc[:, :, 2, :], -1.0, None, ALU.mult).then_inc(dve_out.sem, 1)

        @st.scalar
        def _(act):
            act.wait_ge(dve_out.sem, d0 + 2)
            act.activation(colc[:, :, 2, :], colc[:, :, 2, :], ACT.Exp)
        bank_full.n += 2
        dve_out.n += 2
        st.end()
        st = Stage()
        s0, m0, p0, x0, v0, h0 = (scores_ready.n, max_ready.n, probs_ready.n, probsT_ready.n, pv_ready.n,
                                  head_stored.n)
        runs = [(h, r) for h in range(H_B) for r in range(2)]
        seen = {0: lambda j, i: i >= j, 1: lambda j, i: (i // 2 == j // 2 and j >= i) or i // 2 > j // 2}

        @st.tensor
        def _(pe):
            def values(n):
                h, r = runs[n]
                pe.wait_ge(probsT_ready.sem, x0 + 4 * n + 4)
                if n >= 1:
                    pe.wait_ge(head_stored.sem, h0 + n)
                for i in range(4):
                    js = [j for j in range(4) if seen[r](j, i)]
                    for j in js:
                        mm = pe.matmul(bank[6 + i // 2][:, (i % 2) * 129:(i % 2) * 129 + 129],
                                       pT[:, n % 2, j, i * P:(i + 1) * P], vaug[:, j, h, :],
                                       start=(j == js[0]), stop=(j == js[-1]))
                mm.then_inc(pv_ready.sem, 1)

            for n, (h, r) in enumerate(runs):
                hp = slice(64 * (h % 2), 64 * (h % 2) + 64)
                b = bank[n % 2]
                if n >= 2:
                    pe.wait_ge(probsT_ready.sem, x0 + 4 * (n - 1))
                for i in range(4):
                    mm = pe.matmul(b[:, i * P:(i + 1) * P], colc[:, i, 1, r * 4 + h:r * 4 + h + 1].to_broadcast([P, P]),
                                   ident[:, :], start=True, stop=True)
                mm.then_inc(max_ready.sem, 1)
                for j in range(4):
                    q = 4 * n + j
                    if q >= 4:
                        pe.wait_ge(probsT_ready.sem, x0 + q - 3)
                    pe.matmul(bank[2 + q % 4][:, :], kT[hp, h // 2, j * P:(j + 1) * P], qT[hp, h // 2, :],
                              start=True, stop=True).then_inc(scores_ready.sem, 1)
                if n >= 1:
                    values(n - 1)
            values(len(runs) - 1)

        @st.vector
        def _(dve):
            def weigh(n, j):
                h, r = runs[n]
                q = 4 * n + j
                if q >= 2:
                    dve.wait_ge(probs_ready.sem, p0 + q - 1)
                dve.scalar_tensor_tensor(e_t[:, q % 2, :], bank[n % 2][:, :], colc[:, j, 0, r * 4 + h:r * 4 + h + 1],
                                         cap[:, r, j, :], ALU.subtract, ALU.max).then_inc(dve_out.sem, 1)

            def apply(n, j):
                q = 4 * n + j
                dve.wait_ge(probs_ready.sem, p0 + q + 1)
                dve.wait_ge(scores_ready.sem, s0 + q + 1)
                if n >= 2:
                    dve.wait_ge(pv_ready.sem, v0 + n - 1)
                dve.tensor_tensor(pT[:, n % 2, j, :], bank[2 + q % 4][:, :], w_t[:, q % 2, :],
                                  ALU.mult).then_inc(probsT_ready.sem, 1)

            def finish(n):
                h, r = runs[n]
                dve.wait_ge(pv_ready.sem, v0 + n + 1)
                for half in range(2):
                    o = bank[6 + half][:, 0:258].rearrange("p (t d) -> p t d", t=2)
                    dve.tensor_scalar(den[:, 0, 2 * half:2 * half + 2], o[:, :, 128], -1.0, None, ALU.mult)
                    dve.drain()
                    dve.tensor_tensor(den[:, 0, 2 * half:2 * half + 2], den[:, 0, 2 * half:2 * half + 2],
                                      o[:, :, 128], ALU.max)
                dve.drain()
                dve.tensor_tensor(den[:, 0, :], den[:, 0, :], colc[:, :, 2, r * 4 + h], ALU.max)
                dve.drain()
                dve.reciprocal(den[:, 1, :], den[:, 0, :])
                dve.drain()
                for i in range(4):
                    o = bank[6 + i // 2][:, (i % 2) * 129:(i % 2) * 129 + 128]
                    dst = omix[:, i, 512 + h * DV_B:512 + (h + 1) * DV_B]
                    if r == 0:
                        ins = dve.tensor_scalar(dst, o, den[:, 1, i:i + 1], None, ALU.mult)
                    else:
                        ins = dve.scalar_tensor_tensor(dst, o, den[:, 1, i:i + 1], dst, ALU.mult, ALU.add)
                ins.then_inc(head_stored.sem, 1)
                dve.drain()

            for n in range(len(runs)):
                dve.wait_ge(max_ready.sem, m0 + n + 1)
                weigh(n, 0)
                for j in range(4):
                    if j < 3:
                        weigh(n, j + 1)
                    apply(n, j)
                if n >= 1:
                    finish(n - 1)
            finish(len(runs) - 1)
        e0 = dve_out.n

        @st.scalar
        def _(act):
            for n in range(len(runs)):
                for j in range(4):
                    q = 4 * n + j
                    act.wait_ge(dve_out.sem, e0 + q + 1)
                    if q >= 2:
                        act.wait_ge(probsT_ready.sem, x0 + q - 1)
                    act.activation(w_t[:, q % 2, :], e_t[:, q % 2, :], ACT.Exp, scale=-1.0)\
                        .then_inc(probs_ready.sem, 1)
        nr = len(runs)
        for sig, k in ((scores_ready, 4 * nr), (max_ready, nr), (probs_ready, 4 * nr), (probsT_ready, 4 * nr),
                       (pv_ready, nr), (head_stored, nr), (dve_out, 4 * nr)):
            sig.n += k
        st.end()
        hm = omix[:, :, 512:1024]
        head_norm([omix[:, m, 512:1024].rearrange("p (n d) -> p n d", d=DV_B) for m in range(4)], DV_B, e_t)
        st = Stage()
        a0 = act_out.n

        @st.scalar
        def _(act):
            for m in range(4):
                act.activation(proj[:, m, MO0:MO0 + 512], proj[:, m, MO0:MO0 + 512], ACT.Sigmoid)\
                    .then_inc(act_out.sem, 1)

        @st.vector
        def _(dve):
            dve.tensor_tensor(hm, hm, ng[:, :].unsqueeze(1).to_broadcast([P, 4, 512]), ALU.mult)
            dve.drain()
            for m in range(4):
                dve.wait_ge(act_out.sem, a0 + m + 1)
                dve.tensor_tensor(omix[:, m, 512:1024], omix[:, m, 512:1024], proj[:, m, MO0:MO0 + 512], ALU.mult)
        act_out.n += 4
        st.end()

    def odd_mixer(gateb):
        with ExitStack() as mem:
            nq = H_C * HD_C
            q = sb(mem, "gq", [P, LT, nq])
            kv = sb(mem, "gkv", [P, 4, 512])
            o = sb(mem, "go", [P, LT, D])
            w = rows(A["odd_w_in"][0])
            linear(lambda c, m, k: hT[:, k, m * P:(m + 1) * P], [2, 3],
                   [(KT, COLS, [(0, w[:, :, c * COLS:(c + 1) * COLS])]) for c in range(2)],
                   lambda eng, c, i, b: eng.activation(q[:, i, c * COLS:(c + 1) * COLS], b[:, :], ACT.Copy),
                   on="scalar")
            linear(lambda c, m, k: hT[:, k, m * P:(m + 1) * P], range(4), [(KT, COLS, [(0, w[:, :, nq:nq + COLS])])],
                   lambda eng, c, i, b: eng.activation(kv[:, i, :], b[:, :], ACT.Copy), on="scalar")
            gain = sb(mem, "g_gain", [P, 2, HD_C])
            rope = sb(mem, "g_rope", [P, LT, 2, HD_C // 2])
            tmp = sb(mem, "g_tmp", [P, 2, 1024])
            qT = sb(mem, "g_qT", [P, H_C, 256])
            kT = sb(mem, "g_kT", [P, KV_C, 512])
            probs = sb(mem, "g_probs", [P, 2, 512])
            probsT = sb(mem, "g_probsT", [P, 2, 512])
            col = sb(mem, "g_col", [P, 4, 4])
            load_small([(gain[:, 0, :], A["gqa_q_norm_g"].to_broadcast([P, HD_C])),
                        (gain[:, 1, :], A["gqa_k_norm_g"].to_broadcast([P, HD_C])),
                        (rope[:, :, :, :], A["rope_grid"])])
            qv = [q[:, i, :].rearrange("p (n d) -> p n d", d=HD_C) for i in range(LT)]
            kvv = [kv[:, i, 0:256].rearrange("p (n d) -> p n d", d=HD_C) for i in range(4)]
            head_norm(qv + kvv, HD_C, tmp)
            st = Stage()

            @st.vector
            def _(dve):
                for j, v in enumerate(qv + kvv):
                    gv = gain[:, int(j >= LT), :].unsqueeze(1).to_broadcast([P, v.shape[1], HD_C])
                    dve.scalar_tensor_tensor(v, v, HD_C ** -0.5 if j < LT else 1.0, gv, ALU.mult, ALU.mult)
                dve.drain()
                for v, i in [(qv[0], 0), (qv[1], 1), (kvv[2], 0), (kvv[3], 1)]:
                    n = v.shape[1]
                    pairs = v.rearrange("p n (f t) -> p n f t", t=2)
                    x0, x1 = pairs[:, :, :, 0], pairs[:, :, :, 1]
                    c = rope[:, i, 0, :].unsqueeze(1).to_broadcast([P, n, HD_C // 2])
                    s = rope[:, i, 1, :].unsqueeze(1).to_broadcast([P, n, HD_C // 2])
                    half = n * HD_C // 2
                    a, b = [tmp[:, 0, j * half:(j + 1) * half].rearrange("p (n f) -> p n f", n=n) for j in range(2)] \
                        if half <= 512 else [None, None]
                    e, f = [tmp[:, 1, j * half:(j + 1) * half].rearrange("p (n f) -> p n f", n=n) for j in range(2)]
                    dve.tensor_tensor(a, x0, c, ALU.mult)
                    dve.tensor_tensor(b, x1, s, ALU.mult)
                    dve.tensor_tensor(e, x0, s, ALU.mult)
                    dve.tensor_tensor(f, x1, c, ALU.mult)
                    dve.drain()
                    dve.tensor_tensor(x0, a, b, ALU.subtract)
                    dve.tensor_tensor(x1, e, f, ALU.add)
                    dve.drain()
            st.end()
            turn(lambda i, k: q[:, i, k * P:(k + 1) * P], lambda k: qT[:, k, :], LT, H_C)
            turn(lambda i, k: kv[:, i, k * P:(k + 1) * P], lambda k: kT[:, k, :], 4, KV_C)
            units = []
            for h in range(H_C):
                g = h // (H_C // KV_C)
                for i in range(LT):
                    units.append(([(qT[:, h, i * P:(i + 1) * P], kT[:, g, :], 0, True, True)], 512,
                                  [kv[:, j, 256 + g * HD_C:256 + (g + 1) * HD_C] for j in range(4)],
                                  o[:, i, h * HD_C:(h + 1) * HD_C]))
            attend(units, probs, probsT, col)
            project_out(o, A["odd_w_out"][0], [2, 3], gateb, 0)

    tiles2 = [2, 3]
    small = {}

    def load_second_block(mem):
        small["rope"] = sb(mem, "s_rope", [P, LT, 2, 16])
        small["ropei"] = sb(mem, "s_ropei", [P, LT, 2, 8])
        small["causal"] = sb(mem, "s_causal", [P, LT, S_LAT])
        loads = [(small["rope"][:, :, :, :], A["rope_seq"]), (small["ropei"][:, :, :, :], A["rope_idx"]),
                 (small["causal"][:, :, :], A["causal"])]
        for l in range(2):
            t = small[l] = {name: sb(mem, f"s_{name}{l}", shape) for name, shape in (
                ("gcols", [P, 2, KT]), ("cw", [P, KT, CONF_K]), ("sw", [P, KT, SC_K]), ("vec", [P, 3, KT]),
                ("gain", [P, 2, HD_C]), ("fw", [P, 2 * FT, 3]), ("fb", [P, 2 * FT]))}
            loads += [(t["gcols"][:, 0, :], A["norm1_cols"][l]), (t["gcols"][:, 1, :], A["norm2_cols"][l]),
                      (t["cw"][:, :, :], A["conf_w"][l]), (t["sw"][:, :, :], A["sc_w"][l]),
                      (t["gain"][:, 0, :], A["q_norm_g_2"][l:l + 1, :].to_broadcast([P, HD_C])),
                      (t["gain"][:, 1, :], A["k_norm_g_2"][l:l + 1, :].to_broadcast([P, HD_C])),
                      (t["fw"][:, :, :], A["ffn_w"][l]), (t["fb"][:, :], A["ffn_b"][l])]
            loads += [(t["vec"][:, j, :], A[n][l]) for j, n in enumerate(("conf_b", "ln_g", "ln_b"))]
        load_small(loads, wait=False)

    def hybrid(l):
        def tok(m):
            return slice((m - CT) * P, (m - CT + 1) * P)

        def hcol(c, m, k):
            return hT[:, k, tok(m)]
        w_in = rows(A["w_in_2"][l])
        with ExitStack() as lay:
            gcols = small[l]["gcols"]

            def normed(v):
                with ExitStack() as mem:
                    xn = sb(mem, f"h_xn{l}{v}", [P, LT, D])
                    normalise(tiles2, xn)
                    turn(lambda i, k: xn[:, i, k * P:(k + 1) * P], lambda k: hT[:, k, 0:256], LT, KT,
                         lambda k: [(0, 256, gcols[:, v, k:k + 1], 0.0)])
            normed(0)
            with ExitStack() as mix:
                conf = sb(mix, f"h_conf{l}", [P, KT, S_LAT])
                sc = sb(mix, f"h_sc{l}", [P, KT, S_LAT])
                qkv = sb(mix, f"h_qkv{l}", [P, LT, QKV2])
                gates = sb(mix, f"h_gates{l}", [P, LT, 3 * D], F32)
                merged = sb(mix, f"h_merged{l}", [P, LT, D])
                with ExitStack() as cv:
                    convolutions(l, cv, w_in, conf, sc, qkv, gates, hcol)

                def conf_out(lead, side):
                    branch_out(l, merged, gates, 0, lambda c, m, k: conf[:, k, tok(m)], A["w_conf_out_2"][l], True,
                               lead, side)

                def sc_out(lead):
                    branch_out(l, merged, gates, 2, lambda c, m, k: sc[:, k, tok(m)], A["w_sc_out_2"][l], False,
                               lead)
                with ExitStack() as at:
                    o = sb(at, f"h_o{l}", [P, LT, D])
                    with ExitStack() as at2:
                        sparse_attention(l, at2, qkv, o, conf_out, sc_out)
                    turn(lambda i, k: o[:, i, k * P:(k + 1) * P], lambda k: hT[:, k, 0:256], LT, KT)
                branch_out(l, merged, gates, 1, hcol, A["w_attn_out_2"][l], False)
                project_out(merged, A["w_o_2"][l], tiles2, None, 0)
            normed(1)
            feed_forward(l)

    def branch_out(l, merged, gates, g, lhs, w, first, lead=None, side=None):
        with ExitStack() as mem:
            tmp = sb(mem, f"bo{l}{g}", [P, 2, COLS])

            def evac(eng, c, i, b):
                cols = slice(c * COLS, (c + 1) * COLS)
                gv = gates[:, i, g * D + c * COLS:g * D + (c + 1) * COLS]
                if first:
                    return eng.tensor_tensor(merged[:, i, cols], b[:, :], gv, ALU.mult)
                eng.drain()
                eng.tensor_tensor(tmp[:, i, :], b[:, :], gv, ALU.mult)
                eng.drain()
                return eng.tensor_tensor(merged[:, i, cols], tmp[:, i, :], merged[:, i, cols], ALU.add)
            linear(lhs, tiles2, [(KT, COLS, [(0, rows(w)[:, :, c * COLS:(c + 1) * COLS])]) for c in range(2)], evac,
                   lead=lead, side=side)

    def feature_products(parts, evac_act, evac_dve):
        f0, n0, fa, fd = bank_full.n, chunks[0], bank_free_act.n, bank_free_dve.n
        for c in range(len(parts)):
            used_at[n0 + c] = (bank_full, f0 + c + 1)
        stream(parts)
        st = Stage()

        @st.tensor
        def _(pe):
            for c in range(len(parts)):
                if c >= 4:
                    pe.wait_ge(bank_free_act.sem, fa + c - 3)
                    pe.wait_ge(bank_free_dve.sem, fd + c - 3)
                arrived(pe, n0 + c)
                wt = chunk(n0 + c)[:, :].rearrange("p (k n) -> p k n", k=KT)
                for j in range(4):
                    b = bank[2 * (c % 4) + j // 2]
                    for k in range(KT):
                        mm = pe.matmul(b[:, (j % 2) * 256:(j % 2) * 256 + 256], wt[:, k, j * P:(j + 1) * P],
                                       hT[:, k, 0:256], start=(k == 0), stop=(k == KT - 1))
                mm.then_inc(bank_full.sem, 1)

        @st.scalar
        def _(act):
            for c in range(len(parts)):
                act.wait_ge(bank_full.sem, f0 + c + 1)
                evac_act(act, c, [bank[2 * (c % 4)], bank[2 * (c % 4) + 1]]).then_inc(bank_free_act.sem, 1)

        @st.vector
        def _(dve):
            for c in range(len(parts)):
                dve.wait_ge(bank_full.sem, f0 + c + 1)
                evac_dve(dve, c, [bank[2 * (c % 4)], bank[2 * (c % 4) + 1]], fa).then_inc(bank_free_dve.sem, 1)
        for sig in (bank_full, bank_free_act, bank_free_dve):
            sig.n += len(parts)
        st.end()

    def convolutions(l, mem, w_in, conf, sc, qkv, gates, hcol):
        PAD = 32
        glu = sb(mem, f"c_glu{l}", [P, KT, PAD + S_LAT])
        cx = sb(mem, f"c_cx{l}", [P, KT, 2 + S_LAT])
        tmp = sb(mem, f"c_tmp{l}", [P, 3, 2, COLS])
        cw, sw, vec = small[l]["cw"], small[l]["sw"], small[l]["vec"]
        st = Stage()

        @st.gpsimd
        def _(pool):
            pool.memset(glu[:, :, 0:PAD], 0.0)
            pool.memset(cx[:, :, 0:2], 0.0)
        st.end()

        def two(a, b, t):
            return [(0, w_in[:, :, a + t * 256:a + (t + 1) * 256]), (256, w_in[:, :, b + t * 256:b + (t + 1) * 256])]
        parts = [two(A2, A2 + D, t) for t in range(4)] + [two(C2 + D, C2 + 2 * D, t) for t in range(4)] \
            + [[(0, w_in[:, :, C2 + t * COLS:C2 + (t + 1) * COLS])] for t in range(2)]

        fd0 = bank_free_dve.n

        def evac_act(act, c, b):
            if 3 <= c < 8:
                act.wait_ge(bank_free_dve.sem, fd0 + c - 2)
            if c < 4:
                return act.activation(tmp[:, c % 3, 0, :], b[1][:, :], ACT.Sigmoid)
            if c < 8:
                return act.activation(tmp[:, c % 3, 0, :], b[1][:, :], ACT.Copy)
            f = 4 * (c - 8)
            act.activation(sc[:, f:f + 2, :].rearrange("p f t -> p (f t)"), b[0][:, :], ACT.Copy)
            return act.activation(sc[:, f + 2:f + 4, :].rearrange("p f t -> p (f t)"), b[1][:, :], ACT.Copy)

        def evac_dve(dve, c, b, fa):
            dve.wait_ge(bank_free_act.sem, fa + c + 1)
            if c >= 8:
                return dve.memset(tmp[:, c % 3, 1, 0:1], 0.0)
            dst, pad = (glu, PAD) if c < 4 else (cx, 2)
            f = 2 * (c % 4)
            return dve.tensor_tensor(dst[:, f:f + 2, pad:pad + S_LAT],
                                     b[0][:, :].rearrange("p (f t) -> p f t", f=2),
                                     tmp[:, c % 3, 0, :].rearrange("p (f t) -> p f t", f=2), ALU.mult)
        feature_products(parts, evac_act, evac_dve)

        widths = [COLS] * 4 + [QKV2 - 4 * COLS] + [COLS] * 6

        def evac(act, c, i, b):
            if c < 5:
                return act.activation(qkv[:, i, c * COLS:c * COLS + widths[c]], b[:, 0:widths[c]], ACT.Copy)
            return act.activation(gates[:, i, (c - 5) * COLS:(c - 4) * COLS], b[:, :], ACT.Sigmoid)

        def conv(dve):
            for f in range(0, KT, 2):
                accs = [tmp[:, j, 0, 0:S_LAT] for j in range(2)]
                for k in range(SC_K):
                    for j in range(2):
                        src = cx[:, f + j, k:k + S_LAT]
                        if k == 0:
                            dve.tensor_scalar(accs[j], src, sw[:, f + j, 0:1], None, ALU.mult)
                        else:
                            dve.scalar_tensor_tensor(accs[j], src, sw[:, f + j, k:k + 1], accs[j],
                                                     ALU.mult, ALU.add)
                    dve.drain()
                for j in range(2):
                    dve.tensor_tensor(sc[:, f + j, :], sc[:, f + j, :], accs[j], ALU.mult)
                dve.drain()
            for k in range(CONF_K):
                for f in range(KT):
                    src = glu[:, f, PAD - (CONF_K - 1) + k:PAD - (CONF_K - 1) + k + S_LAT]
                    if k == 0:
                        dve.tensor_scalar(conf[:, f, :], src, cw[:, f, 0:1], vec[:, 0, f:f + 1], ALU.mult, ALU.add)
                    else:
                        dve.scalar_tensor_tensor(conf[:, f, :], src, cw[:, f, k:k + 1], conf[:, f, :],
                                                 ALU.mult, ALU.add)
                dve.drain()
        linear(hcol, tiles2,
               [(KT, widths[c], [(0, w_in[:, :, (c * COLS if c < 5 else G2 + (c - 5) * COLS):
                                          (c * COLS if c < 5 else G2 + (c - 5) * COLS) + widths[c]])])
                for c in range(11)], evac, on="scalar", side=conv)

        sq = glu[:, :, 0:S_LAT]
        mean, var = tmp[:, 0, 0, 0:S_LAT], tmp[:, 1, 0, 0:S_LAT]
        st = Stage()
        a0, f0, d0 = act_out.n, bank_full.n, dve_out.n

        @st.scalar
        def _(act):
            for f in range(KT):
                act.activation(sq[:, f, :], conf[:, f, :], ACT.Square).then_inc(act_out.sem, 1)
            act.wait_ge(dve_out.sem, d0 + 1)
            act.activation(var, var, ACT.Sqrt, bias=eps_col[:, :]).then_inc(act_out.sem, 1)
            for f in range(KT):
                act.wait_ge(dve_out.sem, d0 + 2 + f)
                act.activation(conf[:, f, :], conf[:, f, :], ACT.Silu, scale=vec[:, 1, f:f + 1],
                               bias=vec[:, 2, f:f + 1])

        @st.tensor
        def _(pe):
            for f in range(KT):
                pe.matmul(bank[0][:, 0:S_LAT], ones[:, :], conf[:, f, :], start=(f == 0), stop=(f == KT - 1))
            for f in range(KT):
                pe.wait_ge(act_out.sem, a0 + f + 1)
                mm = pe.matmul(bank[1][:, 0:S_LAT], ones[:, :], sq[:, f, :], start=(f == 0), stop=(f == KT - 1))
            mm.then_inc(bank_full.sem, 1)

        @st.vector
        def _(dve):
            dve.wait_ge(bank_full.sem, f0 + 1)
            dve.tensor_scalar(mean, bank[0][:, 0:S_LAT], 1.0 / D, None, ALU.mult)
            dve.drain()
            dve.tensor_tensor(var, mean, mean, ALU.mult)
            dve.drain()
            dve.scalar_tensor_tensor(var, bank[1][:, 0:S_LAT], 1.0 / D, var, ALU.mult, ALU.subtract)
            dve.drain()
            dve.tensor_scalar(var, var, 0.0, None, ALU.max).then_inc(dve_out.sem, 1)
            dve.wait_ge(act_out.sem, a0 + KT + 1)
            dve.reciprocal(var, var)
            for f in range(KT):
                dve.tensor_tensor(conf[:, f, :], conf[:, f, :], mean, ALU.subtract)
            dve.drain()
            for f in range(KT):
                dve.tensor_tensor(conf[:, f, :], conf[:, f, :], var, ALU.mult).then_inc(dve_out.sem, 1)
        act_out.n += KT + 1
        bank_full.n += 1
        dve_out.n += KT + 1
        st.end()

    def sparse_attention(l, mem, qkv, o, conf_out, sc_out):
        gain, rope, ropei, causal = small[l]["gain"], small["rope"], small["ropei"], small["causal"]
        tmp = sb(mem, f"s_tmp{l}", [P, 2, 1280])
        ik2 = sb(mem, f"s_ik{l}", [P, LT, P])
        qT = sb(mem, f"s_qT{l}", [P, 8, 256])
        kT = sb(mem, f"s_kT{l}", [P, 2, 256])
        iqT = sb(mem, f"s_iqT{l}", [P, 4, 256])
        ikT = sb(mem, f"s_ikT{l}", [P, 1, 256])
        score = sb(mem, f"s_score{l}", [P, LT, S_LAT])
        mask = sb(mem, f"s_mask{l}", [P, LT, S_LAT])
        rel = sb(mem, f"s_rel{l}", [P, 4, S_LAT])
        top = sb(mem, f"s_top{l}", [P, LT, 8])
        probs = sb(mem, f"s_probs{l}", [P, 2, 256])
        probsT = sb(mem, f"s_probsT{l}", [P, 2, 256])
        col = sb(mem, f"s_col{l}", [P, 4, 4])
        qk = [qkv[:, i, 0:1280].rearrange("p (n d) -> p n d", d=HD_C) for i in range(LT)]
        norm_vector, norm_scalar = head_norm_programs(qk, HD_C, tmp)

        def prepare(dve):
            norm_vector(dve)
            dve.drain()
            for i in range(LT):
                for lo, hi, g, s in ((0, 8, 0, HD_C ** -0.5), (8, 10, 1, 1.0)):
                    v = qk[i][:, lo:hi, :]
                    dve.scalar_tensor_tensor(v, v, s, gain[:, g, :].unsqueeze(1).to_broadcast([P, hi - lo, HD_C]),
                                             ALU.mult, ALU.mult)
            dve.drain()
            for i in range(LT):
                idx = qkv[:, i, IQ2:IQ2 + 9 * IDX_D].rearrange("p (n d) -> p n d", d=IDX_D)
                for v, table, n, half in ((qk[i], rope, 10, 16), (idx, ropei, 9, 8)):
                    x1, x2 = v[:, :, 0:half], v[:, :, half:2 * half]
                    c = table[:, i, 0, :].unsqueeze(1).to_broadcast([P, n, half])
                    s = table[:, i, 1, :].unsqueeze(1).to_broadcast([P, n, half])
                    a, b, e, f = [tmp[:, i, j * 160:j * 160 + n * half].rearrange("p (n f) -> p n f", n=n)
                                  for j in range(4)]
                    dve.tensor_tensor(a, x1, c, ALU.mult)
                    dve.tensor_tensor(b, x2, s, ALU.mult)
                    dve.tensor_tensor(e, x2, c, ALU.mult)
                    dve.tensor_tensor(f, x1, s, ALU.mult)
                    dve.drain()
                    dve.tensor_tensor(x1, a, b, ALU.subtract)
                    dve.tensor_tensor(x2, e, f, ALU.add)
                    dve.drain()
                for r in range(2):
                    dve.tensor_copy(ik2[:, i, r * IDX_D:(r + 1) * IDX_D], qkv[:, i, IK2:IK2 + IDX_D])
                iw = qkv[:, i, IW2:IW2 + IDX_H]
                dve.tensor_scalar(iw, iw, IDX_H ** -0.5 * IDX_D ** -0.5, None, ALU.mult)
        conf_out(prepare, norm_scalar)
        turn(lambda i, k: qkv[:, i, k * P:(k + 1) * P], lambda k: qT[:, k, :], LT, 8)
        turn(lambda i, k: qkv[:, i, K2 + k * P:K2 + (k + 1) * P], lambda k: kT[:, k, :], LT, 2)
        turn(lambda i, k: qkv[:, i, IQ2 + k * P:IQ2 + (k + 1) * P], lambda k: iqT[:, k, :], LT, 4)
        turn(lambda i, k: ik2[:, i, :], lambda k: ikT[:, k, :], LT, 1)
        st = Stage()
        f0, a0, d0 = bank_full.n, act_out.n, dve_out.n
        jobs = [(i, h) for h in range(IDX_H) for i in range(LT)]

        @st.tensor
        def _(pe):
            for n, (i, h) in enumerate(jobs):
                if n >= 8:
                    pe.wait_ge(act_out.sem, a0 + n - 7)
                hp = slice(64 * (h % 2), 64 * (h % 2) + 64)
                pe.matmul(bank[n % 8][:, 0:S_LAT], iqT[hp, h // 2, i * P:(i + 1) * P], ikT[hp, 0, :],
                          start=True, stop=True).then_inc(bank_full.sem, 1)

        @st.scalar
        def _(act):
            for n, (i, h) in enumerate(jobs):
                act.wait_ge(bank_full.sem, f0 + n + 1)
                if n >= 4:
                    act.wait_ge(dve_out.sem, d0 + n - 3)
                act.activation(rel[:, n % 4, :], bank[n % 8][:, 0:S_LAT], ACT.Relu).then_inc(act_out.sem, 1)

        @st.vector
        def _(dve):
            for n, (i, h) in enumerate(jobs):
                dve.wait_ge(act_out.sem, a0 + n + 1)
                iw = qkv[:, i, IW2 + h:IW2 + h + 1]
                if h == 0:
                    ins = dve.tensor_scalar(score[:, i, :], rel[:, n % 4, :], iw, None, ALU.mult)
                else:
                    ins = dve.scalar_tensor_tensor(score[:, i, :], rel[:, n % 4, :], iw, score[:, i, :],
                                                   ALU.mult, ALU.add)
                ins.then_inc(dve_out.sem, 1)
                if i == LT - 1:
                    dve.drain()
        bank_full.n += len(jobs)
        act_out.n += len(jobs)
        dve_out.n += len(jobs)
        st.end()

        def select(dve):
            for i in range(LT):
                dve.scalar_tensor_tensor(score[:, i, :], causal[:, i, :], 3e8, score[:, i, :], ALU.mult, ALU.add)
            dve.drain()
            for _ in range(TOPK // 8):
                for i in range(LT):
                    dve.max(top[:, i, :], score[:, i, :])
                dve.drain()
                for i in range(LT):
                    dve.match_replace(score[:, i, :], top[:, i, :], score[:, i, :], -3.3e38)
                dve.drain()
            for i in range(LT):
                dve.tensor_scalar(mask[:, i, :], score[:, i, :], -3.2e38, -BIG, ALU.is_gt, ALU.mult)
            dve.drain()
            for i in range(LT):
                dve.tensor_tensor(mask[:, i, :], mask[:, i, :], causal[:, i, :], ALU.add)
        sc_out(select)
        units = []
        for h in range(8):
            g = h // 4
            for i in range(LT):
                n = (i + 1) * P
                units.append(([(qT[:, h, i * P:(i + 1) * P], kT[:, g, 0:n], 0, True, False),
                               (ident[:, :], mask[:, i, 0:n], 0, False, True)], n,
                              [qkv[:, j, V2 + g * HD_C:V2 + (g + 1) * HD_C] for j in range(n // P)],
                              o[:, i, h * HD_C:(h + 1) * HD_C]))
        attend(units, probs, probsT, col)

    def feed_forward(l):
        w_up = rows(A["w_up_2"][l])
        with ExitStack() as mem:
            hid = sb(mem, f"f_hid{l}", [P, FT, S_LAT])
            acc = sb(mem, f"f_acc{l}", [P, 2, 4, S_LAT])
            cw, cb = small[l]["fw"], small[l]["fb"]
            n_c = FT // 2
            parts = [[(0, w_up[:, :, c * 256:(c + 1) * 256]), (256, w_up[:, :, FFN + c * 256:FFN + (c + 1) * 256])]
                     for c in range(n_c)]
            s0 = moe_silu.n

            def tile_of(c, j):
                return 2 * c + j if j < 2 else FT + 2 * c + j - 2

            def evac_act(act, c, b):
                if c >= 2:
                    act.wait_ge(bank_free_dve.sem, fd0 + c - 1)
                for j in range(4):
                    t = tile_of(c, j)
                    ins = act.activation(acc[:, c % 2, j, :], b[j // 2][:, (j % 2) * 256:(j % 2) * 256 + 256],
                                         ACT.Identity, scale=cw[:, t, 2:3], bias=cb[:, t:t + 1])
                return ins

            def evac_dve(dve, c, b, fa):
                dve.wait_ge(bank_free_act.sem, fa + c + 1)
                for k, sh in ((1, 1), (0, 2)):
                    for j in range(4):
                        a = acc[:, c % 2, j, sh:S_LAT]
                        lo = (j % 2) * 256
                        ins = dve.scalar_tensor_tensor(a, b[j // 2][:, lo:lo + S_LAT - sh],
                                                       cw[:, tile_of(c, j), k:k + 1], a, ALU.mult, ALU.add)
                    if k == 0:
                        ins.then_inc(dve_out.sem, 1)
                    else:
                        dve.drain()
                dve.wait_ge(moe_silu.sem, s0 + c + 1)
                return dve.tensor_tensor(hid[:, 2 * c:2 * c + 2, :], acc[:, c % 2, 0:2, :], acc[:, c % 2, 2:4, :],
                                         ALU.mult)

            fd0, d0 = bank_free_dve.n, dve_out.n
            feature_products_ffn(parts, evac_act, evac_dve, acc, s0, d0)
            w_down = rows(A["w_down_2"][l])
            split = [(0, 8), (8, 8), (16, 6)]

            def evac(eng, c, i, b):
                cols = slice(c * COLS, (c + 1) * COLS)
                return eng.tensor_tensor(x[:, tiles2[i], cols], b[:, :], x[:, tiles2[i], cols], ALU.add)
            linear(lambda c, m, k: hid[:, split[c % 3][0] + k, (m - CT) * P:(m - CT + 1) * P], tiles2,
                   [(kn, COLS, [(0, w_down[:, k0:k0 + kn, c * COLS:(c + 1) * COLS])])
                    for c in range(2) for k0, kn in split], evac, accumulate=3)

    def feature_products_ffn(parts, evac_act, evac_dve, acc, s0, d0):
        f0, n0, fa, fd = bank_full.n, chunks[0], bank_free_act.n, bank_free_dve.n
        for c in range(len(parts)):
            used_at[n0 + c] = (bank_full, f0 + c + 1)
        stream(parts)
        st = Stage()

        @st.tensor
        def _(pe):
            for c in range(len(parts)):
                if c >= 4:
                    pe.wait_ge(bank_free_dve.sem, fd + c - 3)
                arrived(pe, n0 + c)
                wt = chunk(n0 + c)[:, :].rearrange("p (k n) -> p k n", k=KT)
                for j in range(4):
                    b = bank[2 * (c % 4) + j // 2]
                    for k in range(KT):
                        mm = pe.matmul(b[:, (j % 2) * 256:(j % 2) * 256 + 256], wt[:, k, j * P:(j + 1) * P],
                                       hT[:, k, 0:256], start=(k == 0), stop=(k == KT - 1))
                mm.then_inc(bank_full.sem, 1)

        @st.scalar
        def _(act):
            for c in range(len(parts) + 1):
                if c < len(parts):
                    act.wait_ge(bank_full.sem, f0 + c + 1)
                    evac_act(act, c, [bank[2 * (c % 4)], bank[2 * (c % 4) + 1]]).then_inc(bank_free_act.sem, 1)
                if c >= 1:
                    act.wait_ge(dve_out.sem, d0 + c)
                    g = acc[:, (c - 1) % 2, 0:2, :]
                    act.activation(g, g, ACT.Silu).then_inc(moe_silu.sem, 1)

        @st.vector
        def _(dve):
            for c in range(len(parts)):
                dve.wait_ge(bank_full.sem, f0 + c + 1)
                evac_dve(dve, c, [bank[2 * (c % 4)], bank[2 * (c % 4) + 1]], fa).then_inc(bank_free_dve.sem, 1)
        for sig in (bank_full, bank_free_act, bank_free_dve, dve_out, moe_silu):
            sig.n += len(parts)
        st.end()

    def first_layer(l):
        with ExitStack() as mem:
            modc = sb(mem, f"modc{l}", [P, 4 * KT, 2])
            gateb = sb(mem, f"gateb{l}", [P, 2, 2, D])
            gcols = sb(mem, f"gcols{l}", [P, 2, KT])
            ada(l, modc, gateb, gcols)
            modulated(modc, 0, list(range(4)))
            if upto == f"mod{l}":
                return
            (even_mixer, odd_mixer)[l](gateb)
            if upto == f"mix{l}":
                return
            tiles = list(range(4)) if l == 0 else [2, 3]
            modulated(modc, 1, tiles)
            moe(l, tiles, gateb)

    def program():
        for l in range(2):
            if l == 1:
                load_second_block(ctx)
            first_layer(l)
            if upto in (f"mod{l}", f"mix{l}", f"moe{l}"):
                return
        for l in range(2):
            hybrid(l)
            if upto == f"hyb{l}":
                return
    program()

    @block.sync
    def _(sp):
        sp.wait_ge(stage_done.sem, stage_done.n)
        sp.dma_start(out[0].rearrange("(m p) d -> p m d", p=P), x[:, 2:4, :]).then_inc(out_landed.sem, 16)
        if upto:
            sp.dma_start(upto_out.rearrange("(m p) d -> p m d", p=P), x[:, 0:2, :]).then_inc(out_landed.sem, 16)
            sp.wait_ge(out_landed.sem, 32)
        else:
            sp.wait_ge(out_landed.sem, 16)
    ctx.close()


def constants():
    c = {}
    qc, kc = np.arange(GRID_W)[:, None], np.arange(GRID_W)[None, :]
    start = np.clip(qc - 8, 0, GRID_W - 16)
    win = np.where((kc >= start) & (kc < start + 16), 0.0, -BIG).astype(np.float32)
    c["window"] = np.concatenate([win[::-1], win[::-1]])
    t = np.arange(S_LAT)
    inv = (10000.0 ** (-np.arange(32, dtype=np.float32) / np.float32(32))).astype(np.float32)
    ang = np.concatenate([(t // GRID_W).astype(np.float32)[:, None] * inv,
                          (t % GRID_W).astype(np.float32)[:, None] * inv], axis=-1).astype(np.float32)

    def table(a):
        cs = np.stack([np.cos(a), np.sin(a)], axis=1).astype(np.float32)
        return np.ascontiguousarray(cs.reshape(LT, P, 2, -1).transpose(1, 0, 2, 3))
    c["rope_grid"] = table(ang)
    for name, rot in (("rope_seq", 32), ("rope_idx", 16)):
        inv = np.power(np.float32(500000.0), -np.arange(0, rot, 2, dtype=np.float32) / np.float32(rot))
        c[name] = table(t.astype(np.float32)[:, None] * inv.astype(np.float32)[None, :])
    mask = np.where(t[None, :] <= t[:, None], 0.0, -BIG).astype(np.float32)
    c["causal"] = np.ascontiguousarray(mask.reshape(LT, P, S_LAT).transpose(1, 0, 2))
    return c


def layouts(i):
    a = {n: i[n] for n in ("x", "ctx", "ada_w", "ada_b", "even_w_in", "even_w_out", "na_rpb", "mlstm_gate_b",
                           "mlstm_norm_g", "odd_w_in", "odd_w_out", "gqa_q_norm_g", "gqa_k_norm_g", "router_w",
                           "router_b", "exp_w1", "exp_w3", "exp_w2", "w_in_2", "q_norm_g_2", "k_norm_g_2",
                           "w_attn_out_2", "w_conf_out_2", "w_sc_out_2", "w_o_2", "w_up_2", "w_down_2")}

    def cols(v):
        return v.reshape(v.shape[0], -1, P).transpose(0, 2, 1)

    def taps(v):
        return v.reshape(v.shape[0], v.shape[1], -1, P).transpose(0, 3, 2, 1)
    a["cond"] = np.stack([i["c"][0].reshape(KT, P).T, i["c_ctx"].reshape(KT, P).T], axis=-1)
    a["norm_mix_cols"], a["norm_ffn_cols"] = cols(i["norm_mix_g"]), cols(i["norm_ffn_g"])
    a["norm1_cols"], a["norm2_cols"] = cols(i["norm1_g_2"]), cols(i["norm2_g_2"])
    a["na_q_gain"] = np.tile(i["na_q_norm_g"][0], 2)[:, None]
    a["na_k_gain"] = np.tile(i["na_k_norm_g"][0], 2)[:, None]
    a["conf_w"], a["sc_w"], a["ffn_w"] = taps(i["conf_conv_w_2"]), taps(i["sc_conv_w_2"]), taps(i["ffn_conv_w_2"])
    a["conf_b"], a["ln_g"], a["ln_b"] = cols(i["conf_conv_b_2"]), cols(i["conf_ln_g_2"]), cols(i["conf_ln_b_2"])
    a["ffn_b"] = cols(i["ffn_conv_b_2"])
    a.update(constants())
    return {n: np.ascontiguousarray(v) for n, v in a.items()}


upto_out = None


def kernel(**inputs):
    from concourse import bacc
    from concourse.bass_utils import run_bass_kernel_spmd

    nc = bacc.Bacc("TRN2", target_bir_lowering=False, num_devices=1)
    arrays, A = {}, {}
    for name, a in layouts({n: np.asarray(v) for n, v in inputs.items()}).items():
        arrays[f"in_{name}"] = a
        A[name] = nc.dram_tensor(f"in_{name}", a.shape, mybir.dt.from_np(a.dtype), kind="ExternalInput").ap()
    out = nc.dram_tensor("out_x", (1, S_LAT, D), F32, kind="ExternalOutput").ap()
    build(nc, A, out)
    r = run_bass_kernel_spmd(nc, [arrays], core_ids=[0])
    return r.results[0]["out_x"]
```
